# Optimizing a Trainium2 kernel written in Bass

```python
import numpy as np
import jax
import jax.numpy as jnp
from jax import lax
import math

D_MODEL = 1024
BATCH = 1
SEQ = 1024
DEPTH = 1

GRID_W = 64
CTX_LEN = 256
N_MOD = 6
EPS = 1e-6

RW_HEAD_DIM = 64
RW_HEADS = (D_MODEL // 2) // RW_HEAD_DIM
RW_WIDTH = RW_HEADS * RW_HEAD_DIM
RW_DECAY_LORA = 64
RW_AAA_LORA = 64
RW_GATE_LORA = 128
RW_GN_EPS = 1e-5 * RW_HEAD_DIM
CONV_K = 3

HG_KEY_DIM = 64
HG_VAL_DIM = 64
HG_HEADS = (D_MODEL // 2) // HG_VAL_DIM
HG_KWIDTH = HG_HEADS * HG_KEY_DIM
HG_VWIDTH = HG_HEADS * HG_VAL_DIM
HG_CHUNK = 32

D_MIX = RW_WIDTH + HG_VWIDTH
IN_SPLITS = (RW_WIDTH, RW_WIDTH, RW_WIDTH, 2 * RW_DECAY_LORA, 2 * RW_AAA_LORA, RW_GATE_LORA,
             HG_KWIDTH, HG_KWIDTH, HG_KWIDTH, HG_VWIDTH, HG_VWIDTH)
P_IN = sum(IN_SPLITS)

N_EXPERTS = 64
N_GROUPS = 8
TOPK_GROUPS = 4
TOP_K = 8
D_EXPERT = D_MODEL // 4
D_SHARED = D_MODEL // 4
ROUTE_SCALE = 2.5
MOE_BLOCK = 256


def _rmsnorm(x, g):
    xf = x.astype(jnp.float32)
    y = xf * lax.rsqrt(jnp.mean(xf * xf, axis=-1, keepdims=True) + EPS)
    return (y * g.astype(jnp.float32)).astype(x.dtype)

def _split_cols(u):
    idx = [int(i) for i in np.cumsum(IN_SPLITS)[:-1]]
    return jnp.split(u, idx, axis=-1)

def _heads(t, h, d):
    return t.reshape(t.shape[0], t.shape[1], h, d).astype(jnp.float32)

def _conv_latent(u, kern, rows):
    b, l, ch = u.shape
    u2 = u.reshape(b, rows, GRID_W, ch)
    out = lax.conv_general_dilated(u2, kern[:, :, None, :].astype(u.dtype), window_strides=(1, 1),
                                   padding='SAME', dimension_numbers=('NHWC', 'HWIO', 'NHWC'),
                                   feature_group_count=ch)
    return out.reshape(b, l, ch)

def _conv_context(u, kern):
    ch = u.shape[-1]
    return lax.conv_general_dilated(u, kern[CONV_K // 2][:, None, :].astype(u.dtype), window_strides=(1,),
                                    padding='SAME', dimension_numbers=('NWC', 'WIO', 'NWC'),
                                    feature_group_count=ch)

def _rwkv7_scan(r, w, k, v, a, b, s0, reverse, emit):
    def step(s, inp):
        r_t, w_t, k_t, v_t, a_t, b_t = inp
        sa = jnp.einsum('bhvk,bhk->bhv', s, a_t)
        s = s * w_t[:, :, None, :] + sa[..., None] * b_t[:, :, None, :] + v_t[..., None] * k_t[:, :, None, :]
        y = jnp.einsum('bhvk,bhk->bhv', s, r_t) if emit else None
        return s, y
    xs = tuple(jnp.moveaxis(t, 1, 0) for t in (r, w, k, v, a, b))
    s_fin, ys = lax.scan(step, s0, xs, reverse=reverse)
    return (jnp.moveaxis(ys, 0, 1) if emit else None), s_fin

def _rwkv7_mix(cols, conv_fn, s0, w0, w2, a0, a2, g2, k_k, k_a, r_k, lnx_g, lnx_b, emit):
    r, k, v, wd, ad, gd = cols
    r, k, v = jnp.split(conv_fn(jnp.concatenate([r, k, v], axis=-1)), 3, axis=-1)
    bsz, l, _ = r.shape
    rh = _heads(r, RW_HEADS, RW_HEAD_DIM)
    vh = _heads(v, RW_HEADS, RW_HEAD_DIM)
    kk = _heads(k * k_k, RW_HEADS, RW_HEAD_DIM)
    kk = kk / jnp.maximum(jnp.sqrt(jnp.sum(kk * kk, axis=-1, keepdims=True)), 1e-12)
    ys, bonus, states = [], [], []
    for d in range(2):
        wl = wd[..., d * RW_DECAY_LORA:(d + 1) * RW_DECAY_LORA]
        al = ad[..., d * RW_AAA_LORA:(d + 1) * RW_AAA_LORA]
        w = -jax.nn.softplus(-(w0[d] + jnp.tanh(wl) @ w2[d])) - 0.5
        decay = jnp.exp(-jnp.exp(_heads(w, RW_HEADS, RW_HEAD_DIM)))
        a_flat = jax.nn.sigmoid(a0[d] + al @ a2[d])
        a = _heads(a_flat, RW_HEADS, RW_HEAD_DIM)
        kd = _heads(k * (1.0 + (a_flat - 1.0) * k_a), RW_HEADS, RW_HEAD_DIM)
        y, s = _rwkv7_scan(rh, decay, kd, vh, -kk, kk * a, s0[d], d == 1, emit)
        states.append(s)
        if emit:
            ys.append(y)
            bonus.append(jnp.sum(rh * kd * r_k.astype(jnp.float32), axis=-1, keepdims=True) * vh)
    if not emit:
        return None, (states[0], states[1])
    y = ys[0] + ys[1]
    mu = jnp.mean(y, axis=-1, keepdims=True)
    var = jnp.mean(jnp.square(y - mu), axis=-1, keepdims=True)
    yn = ((y - mu) * lax.rsqrt(var + RW_GN_EPS)).reshape(bsz, l, RW_WIDTH) * lnx_g + lnx_b
    yn = yn + (bonus[0] + bonus[1]).reshape(bsz, l, RW_WIDTH)
    g = jax.nn.sigmoid(gd) @ g2
    return (yn * g).astype(r.dtype), (states[0], states[1])

def _gla_chunked(q, k, v, logf, s0, emit):
    bsz, l, h, _ = q.shape
    dv = v.shape[-1]
    n = l // HG_CHUNK
    blk = lambda t: jnp.moveaxis(t.reshape(bsz, n, HG_CHUNK, h, t.shape[-1]), 3, 1)
    q, k, v, logf = blk(q), blk(k), blk(v), blk(logf)
    cum = jnp.cumsum(logf, axis=3)
    last = cum[:, :, :, -1:, :]
    kv = jnp.einsum('bhnjk,bhnjv->bhnkv', k * jnp.exp(last - cum), v)
    chunk_decay = jnp.exp(last[:, :, :, 0, :])
    def step(s, inp):
        dc, kvc = inp
        return dc[..., None] * s + kvc, s
    s_fin, s_prev = lax.scan(step, s0, (jnp.moveaxis(chunk_decay, 2, 0), jnp.moveaxis(kv, 2, 0)))
    if not emit:
        return None, s_fin
    s_prev = jnp.moveaxis(s_prev, 0, 2)
    ref = cum[:, :, :, HG_CHUNK // 2:HG_CHUNK // 2 + 1, :]
    scores = jnp.einsum('bhnik,bhnjk->bhnij', q * jnp.exp(cum - ref), k * jnp.exp(ref - cum))
    causal = jnp.tril(jnp.ones((HG_CHUNK, HG_CHUNK), dtype=bool))
    scores = jnp.where(causal, scores, 0.0)
    o = (jnp.einsum('bhnij,bhnjv->bhniv', scores, v)
         + jnp.einsum('bhnik,bhnkv->bhniv', q * jnp.exp(cum), s_prev))
    return jnp.moveaxis(o, 1, 3).reshape(bsz, l, h, dv), s_fin

def _hgrn2_mix(cols, s0, lb, norm_g, emit):
    q, f_fw, f_bw, i, g = cols
    bsz, l, _ = q.shape
    qh = _heads(jax.nn.silu(q), HG_HEADS, HG_KEY_DIM) * (HG_KEY_DIM ** -0.5)
    ih = _heads(i, HG_HEADS, HG_VAL_DIM)
    outs, states = [], []
    for d, f_raw in enumerate((f_fw, f_bw)):
        fr = _heads(f_raw, HG_HEADS, HG_KEY_DIM)
        lbd = lb[d].reshape(HG_HEADS, HG_KEY_DIM)
        logf = jnp.log(lbd + (1.0 - lbd) * jax.nn.sigmoid(fr))
        kf = (1.0 - lbd) * jax.nn.sigmoid(-fr)
        args = (qh, kf, ih, logf)
        if d == 1:
            args = tuple(jnp.flip(t, axis=1) for t in args)
        o, s = _gla_chunked(args[0], args[1], args[2], args[3], s0[d], emit)
        states.append(s)
        if emit:
            outs.append(jnp.flip(o, axis=1) if d == 1 else o)
    if not emit:
        return None, (states[0], states[1])
    o = outs[0] + outs[1]
    o = o * lax.rsqrt(jnp.mean(o * o, axis=-1, keepdims=True) + EPS) * norm_g.astype(jnp.float32)
    o = o.reshape(bsz, l, HG_VWIDTH) * jax.nn.silu(g)
    return o.astype(g.dtype), (states[0], states[1])

def _swiglu(x, wg, wu, wd):
    return (jax.nn.silu(x @ wg) * (x @ wu)) @ wd

def _moe(h, router_w, router_b, wg, wu, wd, sg, su, sd):
    t = h.shape[0]
    scores = jax.nn.sigmoid(h.astype(jnp.float32) @ router_w.astype(jnp.float32))
    sel = scores + router_b.astype(jnp.float32)
    grp = sel.reshape(t, N_GROUPS, N_EXPERTS // N_GROUPS)
    grp_score = jnp.sum(lax.top_k(grp, 2)[0], axis=-1)
    _, top_g = lax.top_k(grp_score, TOPK_GROUPS)
    gmask = jnp.any(top_g[:, :, None] == jnp.arange(N_GROUPS)[None, None, :], axis=1)
    sel = jnp.where(jnp.repeat(gmask, N_EXPERTS // N_GROUPS, axis=1), sel, -jnp.inf)
    _, top_e = lax.top_k(sel, TOP_K)
    gate = jnp.take_along_axis(scores, top_e, axis=1)
    gate = gate / jnp.sum(gate, axis=-1, keepdims=True) * ROUTE_SCALE
    n_assign = t * TOP_K
    flat_e = top_e.reshape(-1)
    flat_tok = jnp.arange(n_assign, dtype=jnp.int32) // TOP_K
    flat_gate = gate.reshape(-1)
    order = jnp.argsort(flat_e)
    e_sorted, tok_sorted, gate_sorted = flat_e[order], flat_tok[order], flat_gate[order]
    counts = jnp.bincount(flat_e, length=N_EXPERTS)
    starts = jnp.cumsum(counts) - counts
    padded = (counts + MOE_BLOCK - 1) // MOE_BLOCK * MOE_BLOCK
    pad_end = jnp.cumsum(padded)
    pad_start = pad_end - padded
    dest = pad_start[e_sorted] + (jnp.arange(n_assign, dtype=jnp.int32) - starts[e_sorted])
    n_blocks = -(-n_assign // MOE_BLOCK) + N_EXPERTS
    tok_buf = jnp.zeros((n_blocks * MOE_BLOCK,), jnp.int32).at[dest].set(tok_sorted).reshape(n_blocks, MOE_BLOCK)
    gate_buf = jnp.zeros((n_blocks * MOE_BLOCK,), jnp.float32).at[dest].set(gate_sorted).reshape(n_blocks, MOE_BLOCK)
    blk_e = jnp.minimum(jnp.searchsorted(pad_end, jnp.arange(n_blocks, dtype=jnp.int32) * MOE_BLOCK, side='right'),
                        N_EXPERTS - 1)
    def step(out, inp):
        tok, gw, e = inp
        y = _swiglu(h[tok], wg[e], wu[e], wd[e]) * gw[:, None].astype(h.dtype)
        return out.at[tok].add(y), None
    routed, _ = lax.scan(step, jnp.zeros_like(h), (tok_buf, gate_buf, blk_e))
    return _swiglu(h, sg, su, sd) + routed

def first_inputs(seed: int = 0) -> dict:
    key = jax.random.key(seed)
    ks = jax.random.split(key, 32)
    nrm = lambda k, shape, scale: jax.random.normal(k, shape, jnp.float32) * scale
    d = D_MODEL
    return {
        'x': nrm(ks[0], (BATCH, SEQ, d), 1.0),
        'c': nrm(ks[1], (BATCH, d), 1.0),
        'ctx': nrm(ks[2], (BATCH, CTX_LEN, d), 1.0),
        'c_ctx': nrm(ks[3], (d,), 1.0),
        'w_mod': nrm(ks[4], (DEPTH, d, N_MOD * d), 0.5 * d ** -0.5),
        'b_mod': nrm(ks[5], (DEPTH, N_MOD * d), 0.02),
        'norm1_g': 1.0 + nrm(ks[6], (DEPTH, d), 0.05),
        'norm2_g': 1.0 + nrm(ks[7], (DEPTH, d), 0.05),
        'w_in': nrm(ks[8], (DEPTH, d, P_IN), d ** -0.5),
        'rw_conv': jnp.zeros((DEPTH, CONV_K, CONV_K, 3 * RW_WIDTH), jnp.float32).at[:, CONV_K // 2, CONV_K // 2, :].set(1.0)
                   + nrm(ks[9], (DEPTH, CONV_K, CONV_K, 3 * RW_WIDTH), 0.15),
        'rw_w0': jax.random.uniform(ks[10], (DEPTH, 2, RW_WIDTH), jnp.float32, -6.0, -1.0),
        'rw_w2': nrm(ks[11], (DEPTH, 2, RW_DECAY_LORA, RW_WIDTH), 0.1),
        'rw_a0': nrm(ks[12], (DEPTH, 2, RW_WIDTH), 0.3),
        'rw_a2': nrm(ks[13], (DEPTH, 2, RW_AAA_LORA, RW_WIDTH), 0.1),
        'rw_g2': nrm(ks[14], (DEPTH, RW_GATE_LORA, RW_WIDTH), RW_GATE_LORA ** -0.5),
        'rw_k_k': 0.85 + nrm(ks[15], (DEPTH, RW_WIDTH), 0.05),
        'rw_k_a': 1.0 + nrm(ks[16], (DEPTH, RW_WIDTH), 0.05),
        'rw_r_k': nrm(ks[17], (DEPTH, RW_HEADS, RW_HEAD_DIM), 0.1),
        'rw_lnx_g': 1.0 + nrm(ks[18], (DEPTH, RW_WIDTH), 0.05),
        'rw_lnx_b': nrm(ks[19], (DEPTH, RW_WIDTH), 0.02),
        'hg_lb_logits': nrm(ks[20], (2, DEPTH + 1, HG_KWIDTH), 0.5),
        'hg_norm_g': 1.0 + nrm(ks[21], (DEPTH, HG_VAL_DIM), 0.05),
        'w_out': nrm(ks[22], (DEPTH, D_MIX, d), D_MIX ** -0.5),
        'router_w': nrm(ks[23], (DEPTH, d, N_EXPERTS), d ** -0.5),
        'router_b': nrm(ks[24], (DEPTH, N_EXPERTS), 0.01),
        'exp_w_gate': nrm(ks[25], (DEPTH, N_EXPERTS, d, D_EXPERT), d ** -0.5),
        'exp_w_up': nrm(ks[26], (DEPTH, N_EXPERTS, d, D_EXPERT), d ** -0.5),
        'exp_w_down': nrm(ks[27], (DEPTH, N_EXPERTS, D_EXPERT, d), D_EXPERT ** -0.5),
        'sh_w_gate': nrm(ks[28], (DEPTH, d, D_SHARED), d ** -0.5),
        'sh_w_up': nrm(ks[29], (DEPTH, d, D_SHARED), d ** -0.5),
        'sh_w_down': nrm(ks[30], (DEPTH, D_SHARED, d), D_SHARED ** -0.5),
        'final_norm_g': 1.0 + nrm(ks[31], (d,), 0.05),
    }

def first_block(x, c, ctx, c_ctx, w_mod, b_mod, norm1_g, norm2_g, w_in, rw_conv, rw_w0, rw_w2, rw_a0, rw_a2,
              rw_g2, rw_k_k, rw_k_a, rw_r_k, rw_lnx_g, rw_lnx_b, hg_lb_logits, hg_norm_g, w_out, router_w,
              router_b, exp_w_gate, exp_w_up, exp_w_down, sh_w_gate, sh_w_up, sh_w_down, final_norm_g):
    bsz, seq, d = x.shape
    rows = seq // GRID_W
    ctx_len = ctx.shape[1]
    lb_all = jnp.cumsum(jax.nn.softmax(hg_lb_logits.astype(jnp.float32), axis=1), axis=1)
    zero_rw = jnp.zeros((bsz, RW_HEADS, RW_HEAD_DIM, RW_HEAD_DIM), jnp.float32)
    zero_hg = jnp.zeros((bsz, HG_HEADS, HG_KEY_DIM, HG_VAL_DIM), jnp.float32)
    for l in range(DEPTH):
        last = l == DEPTH - 1
        mod_lat = (jax.nn.silu(c) @ w_mod[l] + b_mod[l])[:, None, :]
        mod_ctx = (jax.nn.silu(c_ctx) @ w_mod[l] + b_mod[l])[None, None, :]
        sh1, sc1, g1, sh2, sc2, g2 = jnp.split(mod_lat, N_MOD, axis=-1)
        csh1, csc1, cg1, csh2, csc2, cg2 = jnp.split(mod_ctx, N_MOD, axis=-1)
        h_lat = _rmsnorm(x, norm1_g[l]) * (1.0 + sc1) + sh1
        h_ctx = _rmsnorm(ctx, norm1_g[l]) * (1.0 + csc1) + csh1
        cols_lat = _split_cols(h_lat @ w_in[l])
        cols_ctx = _split_cols(h_ctx @ w_in[l])
        kern = rw_conv[l]
        rw_p = (rw_w0[l], rw_w2[l], rw_a0[l], rw_a2[l], rw_g2[l], rw_k_k[l], rw_k_a[l], rw_r_k[l],
                rw_lnx_g[l], rw_lnx_b[l])
        lb_l = lb_all[:, l]
        y_rw_ctx, s_rw = _rwkv7_mix(cols_ctx[:6], lambda u: _conv_context(u, kern), (zero_rw, zero_rw), *rw_p,
                                    emit=not last)
        y_rw_lat, _ = _rwkv7_mix(cols_lat[:6], lambda u: _conv_latent(u, kern, rows), s_rw, *rw_p, emit=True)
        y_hg_ctx, s_hg = _hgrn2_mix(cols_ctx[6:], (zero_hg, zero_hg), lb_l, hg_norm_g[l], emit=not last)
        y_hg_lat, _ = _hgrn2_mix(cols_lat[6:], s_hg, lb_l, hg_norm_g[l], emit=True)
        x = x + g1 * (jnp.concatenate([y_rw_lat, y_hg_lat], axis=-1) @ w_out[l])
        moe_p = (router_w[l], router_b[l], exp_w_gate[l], exp_w_up[l], exp_w_down[l],
                 sh_w_gate[l], sh_w_up[l], sh_w_down[l])
        h2_lat = _rmsnorm(x, norm2_g[l]) * (1.0 + sc2) + sh2
        if last:
            x = x + g2 * _moe(h2_lat.reshape(-1, d), *moe_p).reshape(bsz, seq, d)
        else:
            ctx = ctx + cg1 * (jnp.concatenate([y_rw_ctx, y_hg_ctx], axis=-1) @ w_out[l])
            h2_ctx = _rmsnorm(ctx, norm2_g[l]) * (1.0 + csc2) + csh2
            tokens = jnp.concatenate([h2_ctx, h2_lat], axis=1).reshape(-1, d)
            f = _moe(tokens, *moe_p).reshape(bsz, ctx_len + seq, d)
            ctx = ctx + cg2 * f[:, :ctx_len]
            x = x + g2 * f[:, ctx_len:]
    return _rmsnorm(x, final_norm_g)


CONV_WIDTH = 4
MIX_WIDTH = 2 * D_MODEL
ATT_HEAD_DIM = 64
ATT_WIDTH = MIX_WIDTH // 4
ATT_HEADS = ATT_WIDTH // ATT_HEAD_DIM
Q_BLOCK = 128
SSD_HEAD_DIM = 64
SSD_WIDTH = MIX_WIDTH // 2
SSD_HEADS = SSD_WIDTH // SSD_HEAD_DIM
SSD_GROUPS = 2
SSD_STATE = 128
SSD_CHUNK = 128
SSD_CONV_DIM = SSD_WIDTH + 2 * SSD_GROUPS * SSD_STATE
DT_MIN = 0.001
DT_MAX = 0.1
LRU_WIDTH = MIX_WIDTH // 4
LRU_BLOCKS = 8
LRU_BLOCK_DIM = LRU_WIDTH // LRU_BLOCKS
LRU_C = 8.0
IN_SIZES = (ATT_WIDTH, ATT_WIDTH, ATT_WIDTH, ATT_WIDTH, ATT_HEADS,
            SSD_WIDTH, SSD_CONV_DIM, SSD_HEADS,
            LRU_WIDTH, LRU_WIDTH)
D_IN = sum(IN_SIZES)


def rms_norm(x, g):
    xf = x.astype(jnp.float32)
    return xf * lax.rsqrt(jnp.mean(xf * xf, axis=-1, keepdims=True) + EPS) * g

def causal_dwconv(x, w, b):
    k = w.shape[0]
    y = lax.conv_general_dilated(
        x, w.astype(x.dtype)[:, None, :], window_strides=(1,),
        padding=((k - 1, 0),), dimension_numbers=('NWC', 'WIO', 'NWC'),
        feature_group_count=x.shape[-1])
    return y + b

def fox_attention(q, k, v, log_f, q_g, k_g):
    bsz, seq = q.shape[0], q.shape[1]
    nb = seq // Q_BLOCK
    q = rms_norm(q, q_g)
    k = rms_norm(k, k_g)
    c = jnp.cumsum(log_f.astype(jnp.float32), axis=1)
    qb = q.reshape(bsz, nb, Q_BLOCK, ATT_HEADS, ATT_HEAD_DIM).transpose(1, 0, 3, 2, 4)
    cq = c.reshape(bsz, nb, Q_BLOCK, ATT_HEADS).transpose(1, 0, 3, 2)
    kt = k.transpose(0, 2, 1, 3)
    vt = v.transpose(0, 2, 1, 3)
    ck = c.transpose(0, 2, 1)
    kpos = jnp.arange(seq)
    scale = ATT_HEAD_DIM ** -0.5

    def one_block(args):
        q_i, c_i, blk = args
        logits = jnp.einsum('bhqd,bhkd->bhqk', q_i, kt) * scale + (c_i[..., :, None] - ck[:, :, None, :])
        qpos = blk * Q_BLOCK + jnp.arange(Q_BLOCK)
        logits = jnp.where(kpos[None, :] <= qpos[:, None], logits, -jnp.inf)
        p = jax.nn.softmax(logits.astype(jnp.float32), axis=-1)
        return jnp.einsum('bhqk,bhkd->bhqd', p, vt)

    o = lax.map(one_block, (qb, cq, jnp.arange(nb)))
    return o.transpose(1, 0, 3, 2, 4).reshape(bsz, seq, ATT_WIDTH)

def ssd_mixer(xbc_raw, dt_raw, z, conv_w, conv_b, dt_bias, a_log, d_skip, norm_g):
    bsz, seq = xbc_raw.shape[0], xbc_raw.shape[1]
    nc = seq // SSD_CHUNK
    e = SSD_HEADS // SSD_GROUPS
    gn = SSD_GROUPS * SSD_STATE
    xbc = jax.nn.silu(causal_dwconv(xbc_raw, conv_w, conv_b))
    xs, bm, cm = jnp.split(xbc, [SSD_WIDTH, SSD_WIDTH + gn], axis=-1)
    dt = jax.nn.softplus(dt_raw + dt_bias)
    a = -jnp.exp(a_log.astype(jnp.float32))
    xh = xs.reshape(bsz, seq, SSD_HEADS, SSD_HEAD_DIM)
    xdt = (xh * dt[..., None]).reshape(bsz, nc, SSD_CHUNK, SSD_GROUPS, e, SSD_HEAD_DIM)
    adt = (dt * a).reshape(bsz, nc, SSD_CHUNK, SSD_GROUPS, e).transpose(0, 1, 3, 4, 2)
    bc = bm.reshape(bsz, nc, SSD_CHUNK, SSD_GROUPS, SSD_STATE)
    cc = cm.reshape(bsz, nc, SSD_CHUNK, SSD_GROUPS, SSD_STATE)
    a_cs = jnp.cumsum(adt, axis=-1)
    causal = jnp.tril(jnp.ones((SSD_CHUNK, SSD_CHUNK), dtype=bool))
    seg = a_cs[..., :, None] - a_cs[..., None, :]
    lmat = jnp.exp(jnp.where(causal, seg, -jnp.inf))
    cb = jnp.einsum('bclgn,bcsgn->bcgls', cc, bc)
    y_diag = jnp.einsum('bcgels,bcsgep->bclgep', cb[:, :, :, None] * lmat, xdt)
    decay_states = jnp.exp(a_cs[..., -1:] - a_cs)
    states = jnp.einsum('bclgn,bcgel,bclgep->bcgepn', bc, decay_states, xdt)
    tot = jnp.concatenate([jnp.zeros_like(a_cs[:, :1, ..., -1]), a_cs[..., -1]], axis=1)
    tot_cs = jnp.cumsum(tot, axis=1)
    seg_c = tot_cs[:, :, None] - tot_cs[:, None, :]
    causal_c = jnp.tril(jnp.ones((nc + 1, nc + 1), dtype=bool))[None, :, :, None, None]
    decay_chunk = jnp.exp(jnp.where(causal_c, seg_c, -jnp.inf))
    states_pad = jnp.concatenate([jnp.zeros_like(states[:, :1]), states], axis=1)
    new_states = jnp.einsum('bzcge,bcgepn->bzgepn', decay_chunk, states_pad)
    prev_states = new_states[:, :nc]
    y_off = jnp.einsum('bclgn,bcgepn,bcgel->bclgep', cc, prev_states, jnp.exp(a_cs))
    y = (y_diag + y_off).reshape(bsz, seq, SSD_HEADS, SSD_HEAD_DIM) + xh * d_skip[:, None]
    y = y.reshape(bsz, seq, SSD_WIDTH)
    gated = (y * jax.nn.silu(z)).reshape(bsz, seq, SSD_GROUPS, SSD_WIDTH // SSD_GROUPS)
    gated = rms_norm(gated, 1.0).reshape(bsz, seq, SSD_WIDTH)
    return gated * norm_g

def _lin_combine(c1, c2):
    a1, b1 = c1
    a2, b2 = c2
    return a1 * a2, a2 * b1 + b2

def rglru_mixer(x_raw, conv_w, conv_b, w_a, b_a, w_x, b_x, lam):
    bsz, seq = x_raw.shape[0], x_raw.shape[1]
    xc = causal_dwconv(x_raw, conv_w, conv_b)
    xb = xc.reshape(bsz, seq, LRU_BLOCKS, LRU_BLOCK_DIM)
    r = jax.nn.sigmoid(jnp.einsum('bsnd,nde->bsne', xb, w_a).reshape(bsz, seq, LRU_WIDTH) + b_a)
    i = jax.nn.sigmoid(jnp.einsum('bsnd,nde->bsne', xb, w_x).reshape(bsz, seq, LRU_WIDTH) + b_x)
    log_a = (-LRU_C * r * jax.nn.softplus(-lam)).astype(jnp.float32)
    a = jnp.exp(log_a)
    mult = jnp.sqrt(-jnp.expm1(2.0 * log_a))
    mult = jnp.where((jnp.arange(seq) == 0)[None, :, None], 1.0, mult)
    b = mult * (i * xc)
    _, h = lax.associative_scan(_lin_combine, (a, b), axis=1)
    return h

def second_inputs(seed: int = 0) -> dict:
    key = jax.random.key(seed)
    ks = jax.random.split(key, 24)
    f32 = jnp.float32
    L = DEPTH
    nrm = lambda k, s: jax.random.normal(k, s, f32)
    x = nrm(ks[0], (BATCH, SEQ, D_MODEL))
    norm_g = 1.0 + 0.05 * nrm(ks[1], (L, D_MODEL))
    w_in = nrm(ks[2], (L, D_MODEL, D_IN)) * D_MODEL ** -0.5
    q_norm_g = 1.0 + 0.05 * nrm(ks[3], (L, ATT_HEAD_DIM))
    k_norm_g = 1.0 + 0.05 * nrm(ks[4], (L, ATT_HEAD_DIM))
    forget_b = jax.random.uniform(ks[5], (L, ATT_HEADS), f32, minval=1.0, maxval=4.0)
    ssd_conv_w = nrm(ks[6], (L, CONV_WIDTH, SSD_CONV_DIM)) * CONV_WIDTH ** -0.5
    ssd_conv_b = 0.02 * nrm(ks[7], (L, SSD_CONV_DIM))
    dt0 = jnp.exp(jax.random.uniform(ks[8], (L, SSD_HEADS), f32) * (math.log(DT_MAX) - math.log(DT_MIN)) + math.log(DT_MIN))
    ssd_dt_bias = dt0 + jnp.log(-jnp.expm1(-dt0))
    ssd_a_log = jnp.log(jax.random.uniform(ks[9], (L, SSD_HEADS), f32, minval=1.0, maxval=16.0))
    ssd_d = 1.0 + 0.1 * nrm(ks[10], (L, SSD_HEADS))
    ssd_norm_g = 1.0 + 0.05 * nrm(ks[11], (L, SSD_WIDTH))
    lru_conv_w = nrm(ks[12], (L, CONV_WIDTH, LRU_WIDTH)) * CONV_WIDTH ** -0.5
    lru_conv_b = 0.02 * nrm(ks[13], (L, LRU_WIDTH))
    lru_w_a = nrm(ks[14], (L, LRU_BLOCKS, LRU_BLOCK_DIM, LRU_BLOCK_DIM)) * LRU_BLOCK_DIM ** -0.5
    lru_b_a = 0.02 * nrm(ks[15], (L, LRU_WIDTH))
    lru_w_x = nrm(ks[16], (L, LRU_BLOCKS, LRU_BLOCK_DIM, LRU_BLOCK_DIM)) * LRU_BLOCK_DIM ** -0.5
    lru_b_x = 0.02 * nrm(ks[17], (L, LRU_WIDTH))
    a_pow_c = jax.random.uniform(ks[18], (L, LRU_WIDTH), f32, minval=0.9, maxval=0.999)
    s = a_pow_c ** (1.0 / LRU_C)
    lru_lambda = jnp.log(s) - jnp.log1p(-s)
    w_out = nrm(ks[19], (L, MIX_WIDTH, D_MODEL)) * MIX_WIDTH ** -0.5
    return {'x': x, 'norm_g': norm_g, 'w_in': w_in, 'q_norm_g': q_norm_g, 'k_norm_g': k_norm_g,
            'forget_b': forget_b, 'ssd_conv_w': ssd_conv_w, 'ssd_conv_b': ssd_conv_b,
            'ssd_dt_bias': ssd_dt_bias, 'ssd_a_log': ssd_a_log, 'ssd_d': ssd_d,
            'ssd_norm_g': ssd_norm_g, 'lru_conv_w': lru_conv_w, 'lru_conv_b': lru_conv_b,
            'lru_w_a': lru_w_a, 'lru_b_a': lru_b_a, 'lru_w_x': lru_w_x, 'lru_b_x': lru_b_x,
            'lru_lambda': lru_lambda, 'w_out': w_out}

def second_block(x, norm_g, w_in, q_norm_g, k_norm_g, forget_b, ssd_conv_w, ssd_conv_b,
              ssd_dt_bias, ssd_a_log, ssd_d, ssd_norm_g, lru_conv_w, lru_conv_b,
              lru_w_a, lru_b_a, lru_w_x, lru_b_x, lru_lambda, w_out):
    out_dtype = x.dtype
    h = x.astype(jnp.float32)
    bsz, seq = h.shape[0], h.shape[1]
    split_points = np.cumsum(IN_SIZES)[:-1].tolist()
    for l in range(DEPTH):
        u = rms_norm(h, norm_g[l])
        proj = jnp.einsum('bsd,de->bse', u, w_in[l])
        (q, k, v, z_att, f_raw, z_ssd, xbc, dt_raw, x_lru, z_lru) = jnp.split(proj, split_points, axis=-1)
        hs = (bsz, seq, ATT_HEADS, ATT_HEAD_DIM)
        log_f = jax.nn.log_sigmoid(f_raw + forget_b[l])
        y_att = fox_attention(q.reshape(hs), k.reshape(hs), v.reshape(hs), log_f,
                              q_norm_g[l], k_norm_g[l]) * jax.nn.silu(z_att)
        y_ssd = ssd_mixer(xbc, dt_raw, z_ssd, ssd_conv_w[l], ssd_conv_b[l], ssd_dt_bias[l],
                          ssd_a_log[l], ssd_d[l], ssd_norm_g[l])
        y_lru = rglru_mixer(x_lru, lru_conv_w[l], lru_conv_b[l], lru_w_a[l], lru_b_a[l],
                            lru_w_x[l], lru_b_x[l], lru_lambda[l]) * jax.nn.silu(z_lru)
        mix = jnp.concatenate([y_att, y_ssd, y_lru], axis=-1)
        h = h + jnp.einsum('bse,ed->bsd', mix, w_out[l])
    return h.astype(out_dtype)


def setup_inputs(seed=0):
    out = dict(first_inputs(seed))
    for name, value in second_inputs(seed + 1).items():
        if name != "x":
            out[name + "_2"] = value
    return out


def reference(
    x, c, ctx, c_ctx, w_mod, b_mod, norm1_g, norm2_g, w_in, rw_conv, rw_w0, rw_w2, rw_a0, rw_a2,
    rw_g2, rw_k_k, rw_k_a, rw_r_k, rw_lnx_g, rw_lnx_b, hg_lb_logits, hg_norm_g, w_out, router_w,
    router_b, exp_w_gate, exp_w_up, exp_w_down, sh_w_gate, sh_w_up, sh_w_down, final_norm_g,
    norm_g_2, w_in_2, q_norm_g_2, k_norm_g_2, forget_b_2, ssd_conv_w_2, ssd_conv_b_2,
    ssd_dt_bias_2, ssd_a_log_2, ssd_d_2, ssd_norm_g_2, lru_conv_w_2, lru_conv_b_2, lru_w_a_2,
    lru_b_a_2, lru_w_x_2, lru_b_x_2, lru_lambda_2, w_out_2,
):
    x = first_block(
        x, c, ctx, c_ctx, w_mod, b_mod, norm1_g, norm2_g, w_in, rw_conv, rw_w0, rw_w2, rw_a0,
        rw_a2, rw_g2, rw_k_k, rw_k_a, rw_r_k, rw_lnx_g, rw_lnx_b, hg_lb_logits, hg_norm_g,
        w_out, router_w, router_b, exp_w_gate, exp_w_up, exp_w_down, sh_w_gate, sh_w_up,
        sh_w_down, final_norm_g,
    )
    return second_block(
        x, norm_g_2, w_in_2, q_norm_g_2, k_norm_g_2, forget_b_2, ssd_conv_w_2, ssd_conv_b_2,
        ssd_dt_bias_2, ssd_a_log_2, ssd_d_2, ssd_norm_g_2, lru_conv_w_2, lru_conv_b_2,
        lru_w_a_2, lru_b_a_2, lru_w_x_2, lru_b_x_2, lru_lambda_2, w_out_2,
    )


_drawn_inputs = setup_inputs


def setup_inputs(seed=0):
    import zlib

    import numpy as np

    out = dict(_drawn_inputs(seed))
    spreads = {}
    factors = {'rw_lnx_g': 2.978,
     'rw_lnx_b': 5.606,
     'hg_norm_g': 2.914,
     'q_norm_g_2': 8.0,
     'k_norm_g_2': 8.0,
     'ssd_conv_b_2': 3.518,
     'lru_b_a_2': 63.082,
     'lru_b_x_2': 29.348}
    for name, (base, spread) in spreads.items():
        noise = np.random.default_rng([zlib.crc32(name.encode()), seed]).standard_normal(out[name].shape)
        drawn = base * np.exp(spread * noise) if base else spread * noise
        out[name] = jnp.asarray(drawn.astype(out[name].dtype))
    for name, factor in factors.items():
        out[name] = (out[name] * factor).astype(out[name].dtype)
    return out
```

```python
from contextlib import ExitStack

import concourse.bass as bass
from concourse import mybir
import numpy as np

F32 = mybir.dt.float32
ALU = mybir.AluOpType
ACT = mybir.ActivationFunctionType
AX = mybir.AxisListType
P = 128
BANK = 512

D = 1024
KD = D // P
SEQ = 1024
CTX = 256
TOK = CTX + SEQ
GRID_W = 64
GRID_H = SEQ // GRID_W
HEAD = 64
HEADS = 8
WID = HEADS * HEAD
QT = WID // P
EPS = 1e-6
RW_GN_EPS = 1e-5 * HEAD
RW_CHUNK = 64
RW_CHUNKS = TOK // RW_CHUNK
HG_CHUNK = 32
HG_CHUNKS = TOK // HG_CHUNK
TILES = TOK // P
LAT_TILES = SEQ // P
CTX_TILES = CTX // P
N_MOD = 6
P_IN = 3 * WID + 3 * P + 5 * WID
ROW_R, ROW_K, ROW_V = 0, WID, 2 * WID
ROW_WD, ROW_AD, ROW_GD = 3 * WID, 3 * WID + P, 3 * WID + 2 * P
ROW_Q = 3 * WID + 3 * P
ROW_FF, ROW_FB, ROW_I, ROW_G = ROW_Q + WID, ROW_Q + 2 * WID, ROW_Q + 3 * WID, ROW_Q + 4 * WID

N_EXPERTS = 64
N_GROUPS = 8
TOPK_GROUPS = 4
TOP_K = 8
D_EXPERT = 256
ROUTE_SCALE = 2.5

SSD_HEADS = 16
SSD_WIDTH = SSD_HEADS * HEAD
SSD_GROUPS = 2
SSD_STATE = 128
SSD_CONV = SSD_WIDTH + 2 * SSD_GROUPS * SSD_STATE
SSD_CHUNKS = SEQ // P
CONV_WIDTH = 4
MIX2 = 2 * D
ROW2_Q, ROW2_K, ROW2_V, ROW2_ZA, ROW2_F = 0, WID, 2 * WID, 3 * WID, 4 * WID
ROW2_ZS = ROW2_F + HEADS
ROW2_XBC = ROW2_ZS + SSD_WIDTH
ROW2_DT = ROW2_XBC + SSD_CONV
ROW2_XL = ROW2_DT + SSD_HEADS
ROW2_ZL = ROW2_XL + WID
D_IN = ROW2_ZL + WID


def chunks(n, size=BANK):
    return [(a, min(size, n - a)) for a in range(0, n, size)]


def steps(eng, n, unroll, body):
    if n >= 2 * unroll:
        with eng.Fori(0, n // unroll) as i:
            for u in range(unroll):
                body(i * unroll + u, u, i)
        done = n // unroll * unroll
    else:
        done = 0
    for s in range(done, n):
        body(s, s % unroll, s // unroll)


class Stage:

    def __init__(self, nc, name):
        self.nc, self.name, self.ctx, self.sems = nc, name, ExitStack(), []

    def __enter__(self):
        self.ctx.__enter__()
        self.ctx.enter_context(self.nc.allow_non_contiguous_dma(reason="columns of small parameters"))
        return self

    def __exit__(self, *a):
        return self.ctx.__exit__(*a)

    def sb(self, name, shape, dt=F32):
        return self.ctx.enter_context(self.nc.sbuf_tensor(f"{self.name}_{name}", shape, dt))

    def psum(self, name, shape):
        return self.ctx.enter_context(self.nc.psum_tensor(f"{self.name}_{name}", shape, F32))

    def sem(self, name):
        self.sems.append(self.ctx.enter_context(self.nc.semaphore(f"{self.name}_{name}")))
        return self.sems[-1]

    def block(self):
        self.ctx.callback(self.clear)
        return self.ctx.enter_context(self.nc.Block())

    def clear(self):
        for sem in self.sems:
            self.nc.gpsimd.sem_clear(sem)
        self.nc.all_engine_barrier()


def column(ap, n=P):
    return ap.rearrange("(k p) -> p k", p=n)


def build_constants(nc, ctx):
    def sb(name, shape):
        return ctx.enter_context(nc.sbuf_tensor(name, shape, F32))

    c = {
        "ident": sb("ident", [P, P]),
        "headsum": sb("headsum", [P, P]),
        "rw_after": sb("rw_after", [P, 2, P]),
        "rw_from": sb("rw_from", [P, 2, P]),
        "rw_level": sb("rw_level", [P, 2, 6, P]),
        "hg_from": sb("hg_from", [P, 2, P]),
        "upto": sb("upto", [P, P]),
        "ones": sb("ones", [P, P]),
    }
    with Stage(nc, "consts") as st:
        block = st.block()

        @block.gpsimd
        def _(pool):
            def keep(ap, pattern, base, mult, op=ALU.is_ge):
                pool.drain()
                nc.gpsimd.affine_select(out=ap, in_=ap, pattern=pattern, compare_op=op, fill=0.0,
                                        base=base, channel_multiplier=mult)

            def same(ap, size):
                view = ap.rearrange("p (b s) -> p b s", s=size)
                keep(view, [[-size, P // size], [0, size]], 0, 1)
                keep(view, [[size, P // size], [0, size]], size - 1, -1)

            for name in ("ident", "rw_level"):
                nc.gpsimd.memset(c[name][:], 0.0)
            for name in ("headsum", "rw_after", "rw_from", "hg_from", "upto", "ones"):
                nc.gpsimd.memset(c[name][:], 1.0)
            pool.drain()
            nc.gpsimd.affine_select(out=c["ident"][:, :], in_=c["ident"][:, :], pattern=[[-1, P]],
                                    compare_op=ALU.not_equal, fill=1.0, base=0, channel_multiplier=1)
            same(c["headsum"][:, :], HEAD)
            keep(c["upto"][:, :], [[1, P]], 0, -1)
            for d in range(2):
                sign = 1 if d == 0 else -1
                same(c["rw_after"][:, d, :], RW_CHUNK)
                keep(c["rw_after"][:, d, :], [[sign, P]], -1, -sign)
                same(c["rw_from"][:, d, :], RW_CHUNK)
                keep(c["rw_from"][:, d, :], [[sign, P]], 0, -sign)
                same(c["hg_from"][:, d, :], HG_CHUNK)
                keep(c["hg_from"][:, d, :], [[sign, P]], 0, -sign)
                for level in range(6):
                    s = 1 << level
                    view = c["rw_level"][:, d, level, :].rearrange("p (b h s) -> p b h s", h=2, s=s)[:, :, 1 - d, :]
                    nb = P // (2 * s)
                    pool.drain()
                    nc.gpsimd.memset(view, 1.0)
                    keep(view, [[-2 * s, nb], [0, s]], -s * d, 1)
                    keep(view, [[2 * s, nb], [0, s]], s * d + s - 1, -1)
            pool.drain()
    return c


def modulation(nc, c, c_ctx, w_mod, b_mod, mods):
    with Stage(nc, "mod") as st:
        cond = st.sb("cond", [P, 2, KD])
        act_c = st.sb("act_c", [P, KD, 2])
        w = st.sb("w", [P, 2, KD, BANK])
        bias = st.sb("bias", [2, N_MOD * D])
        res = st.sb("res", [2, N_MOD * D])
        ps = st.psum("ps", [P, 2, BANK])
        in_ready, w_used = st.sem("in_ready"), st.sem("w_used")
        w_ready = [st.sem(f"w_ready{u}") for u in range(2)]
        silu_ready, out_ready, stored = st.sem("silu_ready"), st.sem("out_ready"), st.sem("stored")
        n = N_MOD * D // BANK
        block = st.block()

        @block.sync
        def _(sp):
            sp.dma_start(cond[:, 0, :], column(c[0])).then_inc(in_ready, 16)
            sp.dma_start(cond[:, 1, :], column(c_ctx)).then_inc(in_ready, 16)
            sp.dma_start(bias[0:1, :], b_mod).then_inc(in_ready, 16)
            sp.dma_start(bias[1:2, :], b_mod).then_inc(in_ready, 16)
            for s in range(n):
                if s >= 2:
                    sp.wait_ge(w_used, s - 1)
                sp.dma_start(w[:, s % 2], w_mod[0, :, s * BANK:(s + 1) * BANK]
                             .rearrange("(k p) m -> p k m", p=P)).then_inc(w_ready[s % 2], 16)
            sp.wait_ge(out_ready, n)
            sp.dma_start(mods, res[:, :]).then_inc(stored, 16)
            sp.wait_ge(stored, 16)

        @block.scalar
        def _(act):
            act.wait_ge(in_ready, 64)
            nc.scalar.activation(act_c[:].rearrange("p k t -> p t k"), cond[:], ACT.Silu).then_inc(silu_ready, 1)

        @block.tensor
        def _(pe):
            pe.wait_ge(silu_ready, 1)
            for s in range(n):
                pe.wait_ge(w_ready[s % 2], 16 * (s // 2 + 1))
                if s >= 2:
                    pe.wait_ge(out_ready, s - 1)
                for k in range(KD):
                    mm = nc.tensor.matmul(ps[0:2, s % 2, :], act_c[:, k, :], w[:, s % 2, k, :],
                                          start=(k == 0), stop=(k == KD - 1))
                mm.then_inc(w_used, 1)

        @block.vector
        def _(dve):
            for s in range(n):
                dve.wait_ge(w_used, s + 1)
                at = slice(s * BANK, (s + 1) * BANK)
                nc.vector.tensor_tensor(res[:, at], ps[0:2, s % 2, :], bias[:, at], ALU.add).then_inc(out_ready, 1)


def norm_columns(nc, consts, name, sources, params, dst, keep=None):
    with Stage(nc, name) as st:
        scale = st.sb("scale", [P, 2, KD])
        bias = st.sb("bias", [P, 2, KD])
        x = st.sb("x", [P, 2, D])
        y = st.sb("y", [P, 2, D])
        sq = st.sb("sq", [P, D])
        ms = st.sb("ms", [P, 2, 4])
        ps = st.psum("ps", [P, 2, KD, P])
        par_ready, par_made = st.sem("par_ready"), st.sem("par_made")
        x_ready, x_used = [st.sem(f"x_ready{u}") for u in range(2)], st.sem("x_used")
        var_ready, root_ready = st.sem("var_ready"), st.sem("root_ready")
        y_ready, turned, out_ready = st.sem("y_ready"), st.sem("turned"), st.sem("out_ready")
        loads, make = params(st, scale, bias)
        block = st.block()
        total = sum(a.shape[0] // P for a, _, _ in sources)

        def each(eng, body):
            done = 0
            for src, col, idx in sources:
                steps(eng, src.shape[0] // P, 2, lambda s, u, r: body(s, u, r, done, src, col, idx))
                done += src.shape[0] // P

        @block.sync
        def _(sp):
            for a, b in loads:
                sp.dma_start(a, b).then_inc(par_ready, 16)

            def load(s, u, r, done, src, col, idx):
                sp.wait_ge(x_used, s + done + 1)
                sp.dma_start(x[:, u, :], src[bass.ds(s * P, P), :]).then_inc(x_ready[u], 16)

            each(sp, load)

        @block.scalar
        def _(act):
            act.wait_ge(par_made, 1)

            def body(s, u, r, done, src, col, idx):
                act.drain()
                act.wait_ge(x_ready[u], (r + done // 2 + 1) * 16)
                nc.scalar.activation(sq[:, :], x[:, u, :], ACT.Square, accum_out=ms[:, u, 0:1]).then_inc(var_ready, 1)
                act.wait_ge(root_ready, s + done + 1)
                nc.scalar.activation(ms[:, u, 2:3], ms[:, u, 1:2], ACT.Sqrt).then_inc(var_ready, 1)
                act.wait_ge(turned, s + done + 1)
                for k in range(KD):
                    op = nc.scalar.activation(dst[:, k, bass.ds(s * P + col, P)], ps[:, u, k, :], ACT.Identity,
                                              bias=bias[:, idx, k:k + 1], scale=scale[:, idx, k:k + 1])
                op.then_inc(out_ready, 1)

            each(act, body)

        @block.vector
        def _(dve):
            dve.wait_ge(par_ready, 16 * len(loads))
            make(dve)
            dve.drain()
            dve.sem_inc(par_made, 1)
            dve.sem_inc(x_used, 2)

            def body(s, u, r, done, src, col, idx):
                dve.wait_ge(var_ready, (s + done) * 2 + 1)
                nc.vector.tensor_scalar(ms[:, u, 1:2], ms[:, u, 0:1], 1.0 / D, EPS, ALU.mult, ALU.add)\
                    .then_inc(root_ready, 1)
                dve.wait_ge(var_ready, (s + done) * 2 + 2)
                nc.vector.reciprocal(ms[:, u, 3:4], ms[:, u, 2:3])
                dve.drain()
                nc.vector.tensor_scalar(y[:, u, :], x[:, u, :], ms[:, u, 3:4], None, ALU.mult).then_inc(y_ready, 1)
                dve.wait_ge(y_ready, s + done + 1)
                dve.sem_inc(x_used, 1)

            each(dve, body)

        @block.tensor
        def _(pe):
            def body(s, u, r, done, src, col, idx):
                pe.wait_ge(y_ready, s + done + 1)
                for k in range(KD):
                    tr = nc.tensor.transpose(ps[:, u, k, :], y[:, u, k * P:(k + 1) * P], consts["ident"][:, :])
                tr.then_inc(turned, 1)

            each(pe, body)


def linear_columns(nc, name, w, act, tokens, out):
    K, M = w.shape
    KT = K // P
    parts = chunks(tokens)
    full, rest = M // P, M % P
    with Stage(nc, name) as st:
        wt = st.sb("w", [P, 2, KT, P])
        res = st.sb("res", [P, 2, tokens])
        ps = st.psum("ps", [P, 2, len(parts), BANK])
        w_ready, mm_done = [st.sem(f"w_ready{u}") for u in range(2)], st.sem("mm_done")
        act_read, dve_read = st.sem("act_read"), st.sem("dve_read")
        stored = [st.sem(f"stored{u}") for u in range(2)]
        block = st.block()
        waits = full + (1 if rest else 0)

        def each(eng, body):
            steps(eng, full, 2, lambda s, u, r: body(s, u, r, P))
            if rest:
                body(full, full % 2, full // 2, rest)

        @block.sync
        def _(sp):
            sp.sem_inc(mm_done, 2)

            def load(s, u, r, m):
                sp.wait_ge(mm_done, s + 1)
                sp.dma_start(wt[:, u, :, 0:m], w[:, bass.ds(s * P, m)].rearrange("(k p) m -> p k m", p=P))\
                    .then_inc(w_ready[u], 16)

            each(sp, load)

        @block.tensor
        def _(pe):
            def body(s, u, r, m):
                pe.wait_ge(w_ready[u], (r + 1) * 16)
                pe.wait_ge(act_read, s + 1)
                pe.wait_ge(dve_read, s + 1)
                for n, (at, size) in enumerate(parts):
                    for k in range(KT):
                        mm = nc.tensor.matmul(ps[0:m, u, n, 0:size], wt[:, u, k, 0:m], act[:, k, at:at + size],
                                              start=(k == 0), stop=(k == KT - 1))
                mm.then_inc(mm_done, 1)

            each(pe, body)

        @block.scalar
        def _(eng):
            eng.sem_inc(act_read, 2)
            for u in range(2):
                eng.sem_inc(stored[u], 16)

            def body(s, u, r, m):
                eng.wait_ge(mm_done, s + 3)
                eng.wait_ge(stored[u], (r + 1) * 16)
                at, size = parts[0]
                nc.scalar.copy(res[0:m, u, at:at + size], ps[0:m, u, 0, 0:size]).then_inc(act_read, 1)
                eng.wait_ge(act_read, s + 3)
                eng.wait_ge(dve_read, s + 3)
                eng.dma_start(out[bass.ds(s * P, m), :], res[0:m, u, :]).then_inc(stored[u], 16)

            each(eng, body)
            for u in range(2):
                eng.wait_ge(stored[u], 16 * ((waits - u + 1) // 2 + 1))

        @block.vector
        def _(eng):
            eng.sem_inc(dve_read, 2)

            def body(s, u, r, m):
                eng.wait_ge(mm_done, s + 3)
                eng.wait_ge(stored[u], (r + 1) * 16)
                for n, (at, size) in enumerate(parts[1:], 1):
                    cp = nc.vector.tensor_copy(res[0:m, u, at:at + size], ps[0:m, u, n, 0:size])
                cp.then_inc(dve_read, 1)

            each(eng, body)


def rwkv_prepare(nc, consts, proj, par, rw):
    with Stage(nc, "rwprep") as st:
        raw = st.sb("raw", [P, 3, TOK])
        rkv = st.sb("rkv", [P, 3, TOK])
        wd = st.sb("wd", [P, TOK])
        ad = st.sb("ad", [P, TOK])
        gd = st.sb("gd", [P, SEQ])
        cols = st.sb("cols", [P, 10])
        taps = st.sb("taps", [P, 3, 9])
        w2 = st.sb("w2", [P, 3, P])
        reset = st.sb("reset", [P, TOK])
        kk = st.sb("kk", [P, TOK])
        sq = st.sb("sq", [P, TOK])
        kd = st.sb("kd", [P, 2, TOK])
        sig_w = st.sb("sig_w", [P, TOK])
        sig_a = st.sb("sig_a", [P, TOK])
        inc = st.sb("inc", [P, TOK])
        exc = st.sb("exc", [P, TOK])
        cum = st.sb("cum", [P, TOK])
        fac = st.sb("fac", [P, 2, 6, TOK])
        tot = st.sb("tot", [P, 2, RW_CHUNKS])
        gate = st.sb("gate", [P, SEQ])
        bonus = st.sb("bonus", [P, SEQ])
        ps = st.psum("ps", [P, 2, 3 * BANK])
        once, in_ready, par_ready = st.sem("once"), st.sem("in_ready"), st.sem("par_ready")
        raw_used, sig_gd = st.sem("raw_used"), st.sem("sig_gd")
        sq_ready, sum_ready, sum_used, root_ready = (st.sem("sq_ready"), st.sem("sum_ready"), st.sem("sum_used"),
                                                    st.sem("root_ready"))
        z_ready, z_used, al_ready, al_used = st.sem("z_ready"), st.sem("z_used"), st.sem("al_ready"), st.sem("al_used")
        logs_ready, exps_ready, fac_ready = st.sem("logs_ready"), st.sem("exps_ready"), st.sem("fac_ready")
        fac_sent = [st.sem(f"fac_sent{d}") for d in range(2)]
        prod_ready, bsum_ready, bsum_used = st.sem("prod_ready"), st.sem("bsum_ready"), st.sem("bsum_used")
        g_ready, g_used, extra_sent = st.sem("g_ready"), st.sem("g_used"), st.sem("extra_sent")
        W0, A0, KK, KA, RK, OMKA = 0, 2, 4, 5, 6, 7
        tok = chunks(TOK)
        lat = chunks(SEQ)
        block = st.block()

        def by_chunk(ap):
            return ap.rearrange("p (c t) -> p c t", t=RW_CHUNK)

        def grid(ap):
            return ap[:, CTX:TOK].rearrange("p (y x) -> p y x", x=GRID_W)

        @block.sync
        def _(sp):
            for d in range(2):
                sp.sem_inc(fac_sent[d], 112)
            sp.sem_inc(extra_sent, 48)
            sp.dma_start(wd[:, :], proj[ROW_WD:ROW_WD + P, :]).then_inc(once, 16)
            sp.dma_start(ad[:, :], proj[ROW_AD:ROW_AD + P, :]).then_inc(once, 16)
            sp.dma_start(gd[:, :], proj[ROW_GD:ROW_GD + P, CTX:TOK]).then_inc(once, 16)

            def body(i, u, r):
                at = bass.ds(i * P, P)
                sp.wait_ge(raw_used, i * 2 + 2)
                for j, row in enumerate((ROW_R, ROW_K, ROW_V)):
                    sp.dma_start(raw[:, j, :], proj[bass.ds(i * P + row, P), :]).then_inc(in_ready, 16)
                    sp.dma_start(taps[:, j, :], par["conv"][:, bass.ds(i * P + row, P)].rearrange("t p -> p t"))\
                        .then_inc(in_ready, 16)
                sp.dma_start(cols[:, W0:W0 + 2], par["w0"][:, at].rearrange("d p -> p d")).then_inc(par_ready, 16)
                sp.dma_start(cols[:, A0:A0 + 2], par["a0"][:, at].rearrange("d p -> p d")).then_inc(par_ready, 16)
                for j, name in ((KK, "k_k"), (KA, "k_a"), (RK, "r_k")):
                    sp.dma_start(cols[:, j:j + 1], par[name][at].rearrange("(p o) -> p o", o=1))\
                        .then_inc(par_ready, 16)
                sp.dma_start(w2[:, 0, :], par["w2"][:, at]).then_inc(par_ready, 16)
                sp.dma_start(w2[:, 1, :], par["a2"][:, at]).then_inc(par_ready, 16)
                sp.dma_start(w2[:, 2, :], par["g2"][:, at]).then_inc(par_ready, 16)

                for d in range(2):
                    sp.wait_ge(fac_ready, i * 2 + d + 2)
                    for j, name in enumerate(("a", "r", "b", "k", "bh", "kh")):
                        sp.dma_start(rw[name][d, at, :], fac[:, d, j, :]).then_inc(fac_sent[d], 16)
                    sp.dma_start(rw["tot"][d, at, :], tot[:, d, :]).then_inc(fac_sent[d], 16)
                sp.wait_ge(bsum_used, i + 2)
                sp.wait_ge(g_used, i + 2)
                sp.dma_start(rw["v"][at, :], rkv[:, 2, :]).then_inc(extra_sent, 16)
                sp.dma_start(rw["bonus"][at, :], bonus[:, :]).then_inc(extra_sent, 16)
                sp.dma_start(rw["gate"][at, :], gate[:, :]).then_inc(extra_sent, 16)

            steps(sp, QT, 1, body)
            for d in range(2):
                sp.wait_ge(fac_sent[d], 112 * (QT + 1))
            sp.wait_ge(extra_sent, 48 * (QT + 1))

        @block.tensor
        def _(pe):
            pe.wait_ge(sig_gd, 1)

            def body(i, u, r):
                pe.wait_ge(sq_ready, i + 1)
                pe.wait_ge(g_used, i + 1)
                for at, n in tok:
                    mm = nc.tensor.matmul(ps[:, 0, at:at + n], consts["headsum"][:, :], sq[:, at:at + n],
                                          start=True, stop=True)
                mm.then_inc(sum_ready, 1)
                pe.wait_ge(par_ready, (i + 1) * (16 * 8))
                for d in range(2):
                    rows = slice(d * HEAD, (d + 1) * HEAD)
                    pe.wait_ge(bsum_used, i + 1) if d == 0 else pe.wait_ge(z_used, i * 2 + 1)
                    for at, n in tok:
                        mm = nc.tensor.matmul(ps[:, 1, at:at + n], w2[rows, 0, :], wd[rows, at:at + n],
                                              start=True, stop=True)
                    mm.then_inc(z_ready, 1)
                    pe.wait_ge(sum_used, i + 1) if d == 0 else pe.wait_ge(al_used, i * 2 + 1)
                    for at, n in tok:
                        mm = nc.tensor.matmul(ps[:, 0, at:at + n], w2[rows, 1, :], ad[rows, at:at + n],
                                              start=True, stop=True)
                    mm.then_inc(al_ready, 1)
                pe.wait_ge(prod_ready, i + 1)
                pe.wait_ge(z_used, i * 2 + 2)
                for at, n in lat:
                    mm = nc.tensor.matmul(ps[:, 1, at:at + n], consts["headsum"][:, :],
                                          sq[:, CTX + at:CTX + at + n], start=True, stop=True)
                mm.then_inc(bsum_ready, 1)
                pe.wait_ge(al_used, i * 2 + 2)
                for at, n in lat:
                    mm = nc.tensor.matmul(ps[:, 0, at:at + n], w2[:, 2, :], gd[:, at:at + n],
                                          start=True, stop=True)
                mm.then_inc(g_ready, 1)

            steps(pe, QT, 1, body)

        @block.scalar
        def _(act):
            act.wait_ge(once, 48)
            nc.scalar.activation(wd[:, :], wd[:, :], ACT.Tanh)
            nc.scalar.activation(gd[:, :], gd[:, :], ACT.Sigmoid).then_inc(sig_gd, 1)
            act.sem_inc(g_used, 1)

            def body(i, u, r):
                act.wait_ge(root_ready, i * 2 + 1)
                nc.scalar.activation(sq[:, :], kk[:, :], ACT.Square).then_inc(sq_ready, 1)
                act.wait_ge(root_ready, i * 2 + 2)
                nc.scalar.activation(sq[:, :], sq[:, :], ACT.Sqrt).then_inc(sum_used, 1)
                for d in range(2):
                    act.drain()
                    act.wait_ge(z_ready, i * 2 + d + 1)
                    act.wait_ge(logs_ready, i * 2 + d + 1)
                    nc.scalar.activation(sig_w[:, :], ps[:, 1, 0:TOK], ACT.Sigmoid, bias=cols[:, W0 + d:W0 + d + 1])\
                        .then_inc(z_used, 1)
                    act.wait_ge(al_ready, i * 2 + d + 1)
                    act.wait_ge(fac_ready, i * 2 + d + 1)
                    nc.scalar.activation(sig_a[:, :], ps[:, 0, 0:TOK], ACT.Sigmoid, bias=cols[:, A0 + d:A0 + d + 1])\
                        .then_inc(al_used, 1)
                    act.wait_ge(logs_ready, i * 2 + d + 2)
                    act.wait_ge(fac_sent[d], (i + 1) * 112)
                    nc.scalar.activation(fac[:, d, 0, :], exc[:, :], ACT.Exp)
                    nc.scalar.activation(fac[:, d, 1, :], inc[:, :], ACT.Exp)
                    nc.scalar.activation(fac[:, d, 2, :], inc[:, :], ACT.Exp, scale=-1.0)
                    nc.scalar.activation(fac[:, d, 4, :], sig_w[:, :], ACT.Exp)
                    nc.scalar.activation(tot[:, d, :], by_chunk(cum[:, :])[:, :, RW_CHUNK - 1], ACT.Exp)\
                        .then_inc(exps_ready, 1)
                act.wait_ge(g_ready, i + 1)
                act.wait_ge(extra_sent, (i + 1) * 48)
                nc.scalar.copy(gate[:, :], ps[:, 0, 0:SEQ]).then_inc(g_used, 1)

            steps(act, QT, 1, body)

        @block.vector
        def _(dve):
            nc.vector.memset(reset[:, :], 1.0)
            dve.drain()
            nc.vector.memset(by_chunk(reset[:, :])[:, :, 0:1], 0.0)
            dve.drain()
            dve.sem_inc(raw_used, 2)
            dve.sem_inc(logs_ready, 1)
            dve.sem_inc(fac_ready, 1)
            dve.sem_inc(bsum_used, 1)

            def body(i, u, r):
                dve.wait_ge(in_ready, (i + 1) * 96)
                dve.wait_ge(extra_sent, (i + 1) * 48)
                for j in range(3):
                    nc.vector.tensor_scalar(rkv[:, j, :], raw[:, j, :], taps[:, j, 4:5], None, ALU.mult)
                for dx in (-1, 1):
                    dve.drain()
                    a, b = max(0, -dx), max(0, dx)
                    for j in range(3):
                        nc.vector.scalar_tensor_tensor(rkv[:, j, a:CTX - b], raw[:, j, b:CTX - a],
                                                       taps[:, j, 4 + dx:5 + dx], rkv[:, j, a:CTX - b],
                                                       ALU.mult, ALU.add)
                for dy in (-1, 0, 1):
                    for dx in (-1, 0, 1):
                        if dy == 0 and dx == 0:
                            continue
                        dve.drain()
                        t = (dy + 1) * 3 + dx + 1
                        ya, yb, xa, xb = max(0, -dy), max(0, dy), max(0, -dx), max(0, dx)
                        for j in range(3):
                            o = grid(rkv[:, j, :])[:, ya:GRID_H - yb, xa:GRID_W - xb]
                            s = grid(raw[:, j, :])[:, yb:GRID_H - ya, xb:GRID_W - xa]
                            nc.vector.scalar_tensor_tensor(o, s, taps[:, j, t:t + 1], o, ALU.mult, ALU.add)
                dve.drain()
                dve.sem_inc(raw_used, 1)
                rr, k, v = (rkv[:, j, :] for j in range(3))
                dve.wait_ge(par_ready, (i + 1) * (16 * 8))
                nc.vector.tensor_scalar(kk[:, :], k, cols[:, KK:KK + 1], None, ALU.mult).then_inc(root_ready, 1)
                nc.vector.tensor_scalar(cols[:, OMKA:OMKA + 1], cols[:, KA:KA + 1], -1.0, 1.0, ALU.mult, ALU.add)
                dve.wait_ge(sum_ready, i + 1)
                nc.vector.tensor_scalar(sq[:, :], ps[:, 0, 0:TOK], 1e-24, None, ALU.max).then_inc(root_ready, 1)
                dve.wait_ge(sum_used, i + 1)
                nc.vector.reciprocal(sq[:, :], sq[:, :])
                dve.drain()
                nc.vector.tensor_tensor(kk[:, :], kk[:, :], sq[:, :], ALU.mult)
                for d in range(2):
                    dve.wait_ge(z_used, i * 2 + d + 1)
                    nc.vector.tensor_scalar(sig_w[:, :], sig_w[:, :], -float(np.exp(-0.5)), None, ALU.mult)
                    dve.drain()
                    nc.vector.tensor_tensor_scan(cum[:, :], reset[:, :], sig_w[:, :], 0.0, ALU.mult, ALU.add)
                    dve.drain()
                    last = by_chunk(cum[:, :])[:, :, RW_CHUNK - 1:RW_CHUNK].broadcast_to([P, RW_CHUNKS, RW_CHUNK])
                    if d == 0:
                        nc.vector.tensor_tensor(exc[:, :], cum[:, :], sig_w[:, :], ALU.subtract)
                        nc.vector.tensor_copy(inc[:, :], cum[:, :])
                    else:
                        nc.vector.tensor_tensor(by_chunk(exc[:, :]), last, by_chunk(cum[:, :]), ALU.subtract)
                        dve.drain()
                        nc.vector.tensor_tensor(inc[:, :], exc[:, :], sig_w[:, :], ALU.add)
                    dve.drain()
                    nc.vector.tensor_tensor(by_chunk(sig_w[:, :]), last, by_chunk(inc[:, :]), ALU.subtract)
                    dve.wait_ge(al_used, i * 2 + d + 1)
                    nc.vector.tensor_scalar(kd[:, d, :], sig_a[:, :], cols[:, KA:KA + 1], cols[:, OMKA:OMKA + 1],
                                            ALU.mult, ALU.add)
                    nc.vector.tensor_tensor(sig_a[:, :], sig_a[:, :], kk[:, :], ALU.mult)
                    dve.drain()
                    nc.vector.tensor_tensor(kd[:, d, :], kd[:, d, :], k, ALU.mult).then_inc(logs_ready, 1)
                    dve.drain()
                    dve.wait_ge(exps_ready, i * 2 + d + 1)
                    f = [fac[:, d, j, :] for j in range(6)]
                    nc.vector.scalar_tensor_tensor(f[0], kk[:, :], -1.0, f[0], ALU.mult, ALU.mult)
                    nc.vector.tensor_tensor(f[1], rr, f[1], ALU.mult)
                    nc.vector.tensor_tensor(f[3], kd[:, d, :], f[2], ALU.mult)
                    nc.vector.tensor_tensor(f[5], kd[:, d, :], f[4], ALU.mult)
                    dve.drain()
                    nc.vector.tensor_tensor(f[2], sig_a[:, :], f[2], ALU.mult)
                    nc.vector.tensor_tensor(f[4], sig_a[:, :], f[4], ALU.mult).then_inc(fac_ready, 1)
                nc.vector.tensor_tensor(sq[:, :], kd[:, 0, :], kd[:, 1, :], ALU.add)
                dve.drain()
                nc.vector.scalar_tensor_tensor(sq[:, :], sq[:, :], cols[:, RK:RK + 1], rr, ALU.mult, ALU.mult)\
                    .then_inc(prod_ready, 1)
                dve.wait_ge(bsum_ready, i + 1)
                dve.sem_inc(raw_used, 1)
                nc.vector.tensor_tensor(bonus[:, :], ps[:, 1, 0:SEQ], rkv[:, 2, CTX:TOK], ALU.mult)\
                    .then_inc(bsum_used, 1)

            steps(dve, QT, 1, body)


def over(ap, n):
    return ap.rearrange("p (o t) -> p o t", o=1).broadcast_to([ap.shape[0], n, ap.shape[1]])


def last_of(ap, n):
    return ap.rearrange("p (h o) -> p h o", o=1).broadcast_to([ap.shape[0], ap.shape[1], n])


class Turns:

    def __init__(self, sem, phases, ahead=0):
        self.sem, self.phases, self.ahead = sem, phases, ahead

    def after(self, rnd, phase):
        return rnd * len(self.phases) + sum(p <= phase for p in self.phases) + self.ahead


def rwkv_chunks(nc, consts, rw, d):
    HQ = 4
    with Stage(nc, f"rwchunk{d}") as st:
        def pair(name, shape):
            return [st.sb(f"{name}{u}", shape) for u in range(2)]

        ar = pair("ar", [HEAD, HQ, 2, P])
        bk = pair("bk", [HEAD, 2, HQ, P])
        flat = pair("flat", [P, 4, 2, P])
        tot = pair("tot", [HEAD, 2, HQ])
        rT = pair("rT", [HEAD, HQ, P])
        az = pair("az", [P, HQ, P])
        bkv = pair("bkv", [P, 3, HQ, HEAD])
        at = pair("at", [P, HQ, P])
        cb = pair("cb", [P, HQ, P])
        bkT = pair("bkT", [P, HQ, P])
        ck = pair("ck", [P, HQ, P])
        T = pair("T", [P, HQ, P])
        TT = pair("TT", [P, HQ, P])
        X = pair("X", [P, 2, HQ, P])
        W = pair("W", [P, HQ, P])
        wu = pair("wu", [P, HQ, P])
        diag = pair("diag", [HEAD, HQ * 2, HEAD])
        q_out = pair("q_out", [HEAD, HQ, P])
        y_out = pair("y_out", [P, HQ, HEAD])
        m_out = pair("m_out", [HEAD, HQ * 2, HEAD])
        n_out = pair("n_out", [HEAD, HQ * 2, HEAD])
        ps = [st.psum(f"ps{u}", [P, 4, BANK]) for u in range(2)]

        TURN, BKCK, FIRST, LAST, ZED, WUP, OUT = 0, 1, 2, 11, 12, 13, 14
        level_w = {2 * l: l for l in range(1, 6)}
        level_t = {2 * l + 1: l for l in range(1, 6)}
        loaded = [st.sem(f"loaded{u}") for u in range(2)]
        stored = [st.sem(f"stored{u}") for u in range(2)]
        mm = [Turns(st.sem(f"products{u}"), list(range(15))) for u in range(2)]
        vec = [Turns(st.sem(f"read_by_vector{u}"), [TURN, BKCK, *level_t, OUT], 1) for u in range(2)]
        sca = [Turns(st.sem(f"read_by_scalar{u}"), [TURN, *level_w, ZED, WUP, OUT], 1) for u in range(2)]
        lev = [Turns(st.sem(f"levels{u}"), [TURN, *level_w], 1) for u in range(2)]
        LOADS, STORES = 10, 4
        block = st.block()

        def rounds(eng, body):
            with eng.Fori(0, TILES) as t:
                body(t)

        @block.sync
        def _(sp):
            def body(t):
                tk = bass.ds(t * P, P)
                for u in range(2):
                    rows = slice(u * HQ * HEAD, (u + 1) * HQ * HEAD)
                    sp.wait_ge(mm[u].sem, t * 15 + 2)
                    sp.wait_ge(sca[u].sem, t * 9 + 1)
                    sp.wait_ge(lev[u].sem, t * 6 + 1)
                    for j, name in enumerate(("a", "r")):
                        sp.dma_start(ar[u][:, :, j, :], rw[name][d, rows, tk].rearrange("(h k) t -> k h t", k=HEAD))\
                            .then_inc(loaded[u], 16)
                    for j, name in enumerate(("b", "k")):
                        sp.dma_start(bk[u][:, j], rw[name][d, rows, tk].rearrange("(h k) t -> k h t", k=HEAD))\
                            .then_inc(loaded[u], 16)
                    for j, name in enumerate(("a", "bh", "kh")):
                        sp.dma_start(flat[u][:, j], rw[name][d, rows, tk].rearrange("(g p) t -> p g t", p=P))\
                            .then_inc(loaded[u], 16)
                    sp.dma_start(flat[u][:, 3], rw["v"][rows, tk].rearrange("(g p) t -> p g t", p=P))\
                        .then_inc(loaded[u], 16)
                    for c in range(2):
                        sp.dma_start(tot[u][:, c, :], rw["tot"][d, rows, bass.ds(t * 2 + c, 1)]
                                     .rearrange("(h k) c -> k (h c)", k=HEAD)).then_inc(loaded[u], 16)

            for u in range(2):
                sp.sem_inc(mm[u].sem, 2)
            rounds(sp, body)

        for u in range(2):
            mm[u].ahead = 2

        @block.tensor
        def _(pe):
            def phase(p, t, u):
                b = ps[u]
                if p == TURN:
                    pe.wait_ge(loaded[u], (t + 1) * (16 * LOADS))
                pe.wait_ge(vec[u].sem, vec[u].after(t, p - 1))
                pe.wait_ge(sca[u].sem, sca[u].after(t, p - 1))
                if p == TURN:
                    for j in range(4):
                        for g in range(2):
                            nc.tensor.transpose(b[:, j // 2, ((j % 2) * 2 + g) * P:((j % 2) * 2 + g + 1) * P],
                                                flat[u][:, j, g, :], consts["ident"][:, :])
                    for h in range(HQ):
                        op = nc.tensor.matmul(b[:, 2 + h // 2, (h % 2) * 2 * P:(h % 2 + 1) * 2 * P],
                                              bk[u][:, 0, h, :], ar[u][:, h], start=True, stop=True)
                elif p == BKCK:
                    for h in range(HQ):
                        nc.tensor.matmul(b[:, h // 2, (h % 2) * 2 * P:(h % 2 + 1) * 2 * P],
                                         bk[u][:, 1, h, :], ar[u][:, h], start=True, stop=True)
                    for h in range(HQ):
                        op = nc.tensor.matmul(b[:, 2, h * P:(h + 1) * P], ar[u][:, h, 0, :], bk[u][:, 0, h, :],
                                              start=True, stop=True)
                elif p in level_w:
                    l = level_w[p]
                    pe.wait_ge(lev[u].sem, lev[u].after(t, p))
                    for h in range(HQ):
                        op = nc.tensor.matmul(b[:, 3, h * P:(h + 1) * P], X[u][:, l % 2, h, :], T[u][:, h, :],
                                              start=True, stop=True)
                elif p in level_t:
                    if level_t[p] < 5:
                        for h in range(HQ):
                            nc.tensor.matmul(b[:, 0, h * P:(h + 1) * P], TT[u][:, h, :], W[u][:, h, :],
                                             start=True, stop=True)
                    for h in range(HQ):
                        op = nc.tensor.matmul(b[:, 1, h * P:(h + 1) * P], W[u][:, h, :], TT[u][:, h, :],
                                              start=True, stop=True)
                elif p == ZED:
                    for h in range(HQ):
                        op = nc.tensor.matmul(b[:, 2, h * HEAD:(h + 1) * HEAD], bkT[u][:, h, :], bkv[u][:, 2, h, :],
                                              start=True, stop=True)
                elif p == WUP:
                    for h in range(HQ):
                        op = nc.tensor.matmul(b[:, 3, h * P:(h + 1) * P], TT[u][:, h, :], az[u][:, h, :],
                                              start=True, stop=True)
                else:
                    for h in range(HQ):
                        nc.tensor.matmul(b[0:HEAD, 0, h * P:(h + 1) * P], wu[u][:, h, 0:HEAD], cb[u][:, h, :],
                                         start=True, stop=True)
                    for h in range(HQ):
                        y = b[:, 1, h * HEAD:(h + 1) * HEAD]
                        nc.tensor.matmul(y, cb[u][:, h, :], wu[u][:, h, HEAD:P], start=True, stop=False)
                        nc.tensor.matmul(y, ck[u][:, h, :], bkv[u][:, 2, h, :], start=False, stop=True)
                    for h in range(HQ):
                        for c in range(2):
                            rows = slice(c * HEAD, (c + 1) * HEAD)
                            m, n = (b[0:HEAD, 2 + c, (j * HQ + h) * HEAD:(j * HQ + h + 1) * HEAD] for j in range(2))
                            nc.tensor.matmul(m, wu[u][rows, h, 0:HEAD], bkv[u][rows, 0, h, :],
                                             start=True, stop=True)
                            nc.tensor.matmul(n, bkv[u][rows, 0, h, :], wu[u][rows, h, HEAD:P],
                                             start=True, stop=False)
                            op = nc.tensor.matmul(n, bkv[u][rows, 1, h, :], bkv[u][rows, 2, h, :],
                                                  start=False, stop=True)
                op.then_inc(mm[u].sem, 1)

            rounds(pe, lambda t: [phase(p, t, u) for p in range(15) for u in range(2)])

        @block.gpsimd
        def _(pool):
            for u in range(2):
                pool.sem_inc(lev[u].sem, 1)

            def body(t):
                for u in range(2):
                    pool.wait_ge(loaded[u], (t + 1) * (16 * LOADS))
                    pool.wait_ge(vec[u].sem, vec[u].after(t, -1))
                    nc.gpsimd.tensor_tensor(diag[u][:], over(consts["ident"][0:HEAD, 0:HEAD], 2 * HQ),
                                            last_of(tot[u][:].rearrange("k c h -> k (c h)"), HEAD), ALU.mult)\
                        .then_inc(lev[u].sem, 1)
                for p, l in level_w.items():
                    for u in range(2):
                        pool.wait_ge(vec[u].sem, vec[u].after(t, TURN))
                        if l > 2:
                            pool.wait_ge(mm[u].sem, mm[u].after(t, 2 * (l - 2)))
                        nc.gpsimd.tensor_tensor(X[u][:, l % 2], at[u][:], over(consts["rw_level"][:, d, l, :], HQ),
                                                ALU.mult).then_inc(lev[u].sem, 1)

            rounds(pool, body)

        @block.scalar
        def _(act):
            for u in range(2):
                act.sem_inc(sca[u].sem, 1)
                act.sem_inc(stored[u], 16 * STORES)

            def phase(p, t, u):
                b = ps[u]
                act.wait_ge(mm[u].sem, mm[u].after(t, p))
                if p == TURN:
                    nc.scalar.copy(az[u][:, :, 0:HEAD], b[:, 0, 0:2 * P].rearrange("t (h k) -> t h k", k=HEAD))
                    nc.scalar.copy(bkv[u][:, 0], b[:, 0, 2 * P:4 * P].rearrange("t (h k) -> t h k", k=HEAD))
                    nc.scalar.copy(bkv[u][:, 1:3], b[:, 1, :].rearrange("t (j h k) -> t j h k", j=2, k=HEAD))
                    act.wait_ge(vec[u].sem, vec[u].after(t, -1))
                    op = nc.scalar.copy(rT[u][:], ar[u][:, :, 1, :])
                elif p in level_w:
                    op = nc.scalar.copy(W[u][:], b[:, 3, :].rearrange("p (h t) -> p h t", h=HQ))
                elif p == ZED:
                    op = nc.scalar.copy(az[u][:, :, HEAD:P], b[:, 2, 0:HQ * HEAD].rearrange("p (h t) -> p h t", h=HQ))
                elif p == WUP:
                    op = nc.scalar.copy(wu[u][:], b[:, 3, :].rearrange("p (h t) -> p h t", h=HQ))
                else:
                    act.wait_ge(stored[u], (t + 1) * (16 * STORES))
                    nc.scalar.copy(y_out[u][:], b[:, 1, 0:HQ * HEAD].rearrange("p (h t) -> p h t", h=HQ))
                    op = nc.scalar.copy(n_out[u][:].rearrange("p (c h) t -> p c (h t)", c=2), b[0:HEAD, 2:4, HQ * HEAD:])
                op.then_inc(sca[u].sem, 1)
                if p == OUT:
                    act.wait_ge(sca[u].sem, sca[u].after(t, p))
                    act.wait_ge(vec[u].sem, vec[u].after(t, p))
                    for name, src in (("q", q_out), ("y", y_out), ("m", m_out), ("n", n_out)):
                        act.dma_start(rw[name + "_out"][d, bass.ds(t, 1), u].rearrange("o p h n -> (o p) h n"),
                                      src[u][:]).then_inc(stored[u], 16)

            rounds(act, lambda t: [phase(p, t, u) for p in sca[0].phases for u in range(2)])
            for u in range(2):
                act.wait_ge(stored[u], 16 * STORES * (TILES + 1))

        @block.vector
        def _(dve):
            for u in range(2):
                dve.sem_inc(vec[u].sem, 1)
            eye = over(consts["ident"][:, :], HQ)

            def quad(ap):
                return ap.rearrange("p (h t) -> p h t", h=HQ)

            def phase(p, t, u):
                b = ps[u]
                dve.wait_ge(mm[u].sem, mm[u].after(t, p))
                if p in (TURN, BKCK):
                    banks = b[:, 2:4, :] if p == TURN else b[:, 0:2, :]
                    v = banks.rearrange("p b (g j t) -> p (b g) j t", g=2, j=2)
                    strict, upto = (at, cb) if p == TURN else (bkT, ck)
                    nc.vector.tensor_tensor(strict[u][:], v[:, :, 0, :], over(consts["rw_after"][:, d, :], HQ), ALU.mult)
                    if p == BKCK:
                        nc.vector.tensor_tensor(TT[u][:], at[u][:], over(consts["rw_level"][:, d, 0, :], HQ), ALU.mult)
                        nc.vector.tensor_tensor(T[u][:], quad(b[:, 2, :]), over(consts["rw_level"][:, 1 - d, 0, :], HQ),
                                                ALU.mult)
                        dve.drain()
                        nc.vector.tensor_tensor(TT[u][:], TT[u][:], eye, ALU.add)
                        nc.vector.tensor_tensor(T[u][:], T[u][:], eye, ALU.add)
                    op = nc.vector.tensor_tensor(upto[u][:], v[:, :, 1, :], over(consts["rw_from"][:, d, :], HQ), ALU.mult)
                elif p in level_t:
                    if level_t[p] < 5:
                        nc.vector.tensor_tensor(T[u][:], T[u][:], quad(b[:, 0, :]), ALU.add)
                    op = nc.vector.tensor_tensor(TT[u][:], TT[u][:], quad(b[:, 1, :]), ALU.add)
                else:
                    dve.wait_ge(stored[u], (t + 1) * (16 * STORES))
                    nc.vector.tensor_tensor(q_out[u][:], rT[u][:], quad(b[0:HEAD, 0, :]), ALU.add)
                    dve.wait_ge(sca[u].sem, sca[u].after(t, OUT))
                    op = nc.vector.tensor_tensor(m_out[u][:].rearrange("p (c h) t -> p c (h t)", c=2),
                                                 diag[u][:].rearrange("p (c h) t -> p c (h t)", c=2),
                                                 b[0:HEAD, 2:4, 0:HQ * HEAD], ALU.add)
                op.then_inc(vec[u].sem, 1)

            rounds(dve, lambda t: [phase(p, t, u) for p in vec[0].phases for u in range(2)])


def rwkv_states(nc, rw):
    with Stage(nc, "rwstate") as st:
        m = st.sb("m", [HEAD, 2, 2, 2, 4 * 2 * HEAD])
        n = st.sb("n", [HEAD, 2, 2, 2, 4 * 2 * HEAD])
        s = st.sb("s", [HEAD, 2, 2, 3, HEADS, HEAD])
        ps = st.psum("ps", [P, 2, 2, HEADS * HEAD])
        loaded = [st.sem(f"loaded{u}") for u in range(2)]
        stored = [st.sem(f"stored{u}") for u in range(2)]
        products, added = st.sem("products"), st.sem("added")
        block = st.block()

        def tile_of(d, r):
            return r if d == 0 else ((CTX_TILES - 1 - r) if r < CTX_TILES else TILES - 1 + CTX_TILES - r)

        @block.sync
        def _(sp):
            for r in range(TILES):
                u = r % 2
                if r >= 2:
                    sp.wait_ge(added, 2 * r - 1)
                for d in range(2):
                    for dst, name in ((m, "m_out"), (n, "n_out")):
                        sp.dma_start(dst[:, u, d], rw[name][d, tile_of(d, r)].rearrange("q k h v -> k q (h v)"))\
                            .then_inc(loaded[u], 16)

        @block.tensor
        def _(pe):
            for r in range(TILES):
                pe.wait_ge(loaded[r % 2], 64 * (r // 2 + 1))
                for c in range(2):
                    pe.wait_ge(added, 2 * r + c + 1)
                    for d in range(2):
                        part = c if d == 0 else 1 - c
                        for h in range(HEADS):
                            at = (part * 4 + h % 4) * HEAD
                            op = nc.tensor.matmul(ps[0:HEAD, c, d, h * HEAD:(h + 1) * HEAD],
                                                  m[:, r % 2, d, h // 4, at:at + HEAD],
                                                  s[:, r % 2, d, c, h, :], start=True, stop=True)
                    op.then_inc(products, 1)

        @block.vector
        def _(dve):
            nc.vector.memset(s[:, 0, :, 0], 0.0).then_inc(added, 1)
            for r in range(TILES):
                u = r % 2
                if r >= 2:
                    dve.wait_ge(stored[u], 32 * (r // 2))
                for c in range(2):
                    dve.wait_ge(products, 2 * r + c + 1)
                    if c == 1 and r >= 1:
                        dve.wait_ge(stored[1 - u], 32 * ((r - 1) // 2 + 1))
                    for d in range(2):
                        part = c if d == 0 else 1 - c
                        dst = s[:, u, d, 1] if c == 0 else s[:, 1 - u, d, 0]
                        for q in range(2):
                            op = nc.vector.tensor_tensor(
                                dst[:, 4 * q:4 * q + 4, :],
                                ps[0:HEAD, c, d, q * 4 * HEAD:(q + 1) * 4 * HEAD].rearrange("k (h v) -> k h v", h=4),
                                n[:, u, d, q].rearrange("k (c h v) -> k c h v", h=4, c=2)[:, part], ALU.add)
                    op.then_inc(added, 1)

        @block.scalar
        def _(act):
            for r in range(TILES):
                act.wait_ge(added, 2 * r + 2)
                for d in range(2):
                    act.dma_start(rw["s"][d, tile_of(d, r)], s[:, r % 2, d, 0:2]).then_inc(stored[r % 2], 16)
            for u in range(2):
                act.wait_ge(stored[u], 32 * (TILES // 2))


def rwkv_output(nc, consts, rw, par, mix):
    with Stage(nc, "rwout") as st:
        q = st.sb("q", [HEAD, 2, 2, HEADS, P])
        s = st.sb("s", [HEAD, 2, 2, 2, HEADS, HEAD])
        yo = st.sb("yo", [P, 2, 2, WID])
        y = st.sb("y", [P, 2, WID])
        sq = st.sb("sq", [P, WID])
        stat = st.sb("stat", [P, 2, 4, HEADS])
        ex = st.sb("ex", [P, 2, 2, QT, P])
        res = st.sb("res", [P, 2, QT, P])
        lnx = st.sb("lnx", [P, 2, QT])
        ps = st.psum("ps", [P, 2, 2, BANK])
        pt = st.psum("pt", [P, 2, BANK])
        once = st.sem("once")
        loaded = [st.sem(f"loaded{u}") for u in range(2)]
        stored = [st.sem(f"stored{u}") for u in range(2)]
        products, y_made, var_made, root_made = st.sem("products"), st.sem("y_made"), st.sem("var_made"), st.sem("root_made")
        turned, res_made = st.sem("turned"), st.sem("res_made")
        block = st.block()
        LOADS = 2 * (2 + 2 + 2) + 2

        @block.sync
        def _(sp):
            sp.dma_start(lnx[:, 0, :], column(par["lnx_g"])).then_inc(once, 16)
            sp.dma_start(lnx[:, 1, :], column(par["lnx_b"])).then_inc(once, 16)

            def body(i, u, r):
                sp.wait_ge(res_made, i + 1)
                t = bass.ds(i + CTX_TILES, 1)
                for d in range(2):
                    for g in range(2):
                        sp.dma_start(q[:, u, d, g * 4:g * 4 + 4, :],
                                     rw["q_out"][d, t, g].rearrange("o k h t -> (o k) h t")).then_inc(loaded[u], 16)
                        sp.dma_start(yo[:, u, d, g * 4 * HEAD:(g + 1) * 4 * HEAD],
                                     rw["y_out"][d, t, g].rearrange("o t h v -> (o t) (h v)")).then_inc(loaded[u], 16)
                    for c in range(2):
                        sp.dma_start(s[:, u, d, c], rw["s"][d, t, :, c if d == 0 else 1 - c]
                                     .rearrange("o k h v -> (o k) h v")).then_inc(loaded[u], 16)
                for j, name in enumerate(("bonus", "gate")):
                    sp.dma_start(ex[:, u, j], rw[name][:, bass.ds(i * P, P)].rearrange("(j p) t -> p j t", p=P))\
                        .then_inc(loaded[u], 16)

            steps(sp, LAT_TILES, 2, body)

        @block.tensor
        def _(pe):
            def body(i, u, r):
                pe.wait_ge(loaded[u], (r + 1) * (16 * LOADS))
                pe.wait_ge(y_made, i + 1)
                for h in range(HEADS):
                    for d in range(2):
                        op = nc.tensor.matmul(ps[:, u, h // 4, (h % 4) * P:(h % 4 + 1) * P], q[:, u, d, h, :],
                                              s[:, u, d, :, h, :], start=(d == 0), stop=(d == 1))
                op.then_inc(products, 1)
                pe.wait_ge(y_made, i + 3)
                pe.wait_ge(res_made, i + 1)
                for j in range(QT):
                    op = nc.tensor.transpose(pt[:, u, j * P:(j + 1) * P], y[:, u, j * P:(j + 1) * P], consts["ident"][:, :])
                op.then_inc(turned, 1)

            steps(pe, LAT_TILES, 2, body)

        @block.scalar
        def _(act):
            for u in range(2):
                act.sem_inc(stored[u], 16)

            def body(i, u, r):
                act.wait_ge(var_made, i + 1)
                nc.scalar.activation(stat[:, u, 2, :], stat[:, u, 1, :], ACT.Sqrt).then_inc(root_made, 1)
                act.wait_ge(res_made, i + 3)
                act.dma_start(mix[0:WID, bass.ds(i * P, P)].rearrange("(j p) t -> p j t", p=P), res[:, u])\
                    .then_inc(stored[u], 16)

            steps(act, LAT_TILES, 2, body)
            for u in range(2):
                act.wait_ge(stored[u], 16 * (LAT_TILES // 2 + 1))

        @block.vector
        def _(dve):
            dve.wait_ge(once, 32)
            dve.sem_inc(y_made, 2)
            dve.sem_inc(res_made, 2)

            def heads(ap):
                return ap.rearrange("p (h v) -> p h v", v=HEAD)

            def body(i, u, r):
                dve.wait_ge(loaded[u], (r + 1) * (16 * LOADS))
                yy = y[:, u, :]
                nc.vector.tensor_tensor(yo[:, u, 0, :], yo[:, u, 0, :], yo[:, u, 1, :], ALU.add)
                dve.drain()
                dve.wait_ge(products, i + 1)
                for c in range(2):
                    rows = slice(c * HEAD, (c + 1) * HEAD)
                    v = ps[rows, u].rearrange("t b (h c v) -> t (b h) c v", h=4, c=2)
                    nc.vector.tensor_tensor(heads(yy)[rows], v[:, :, c, :], heads(yo[rows, u, 0, :]), ALU.add)
                dve.drain()
                nc.vector.tensor_reduce(stat[:, u, 0, :], heads(yy), AX.X, ALU.add)
                dve.drain()
                nc.vector.tensor_scalar(stat[:, u, 0, :], stat[:, u, 0, :], 1.0 / HEAD, None, ALU.mult)
                dve.drain()
                nc.vector.tensor_tensor(heads(yy), heads(yy), last_of(stat[:, u, 0, :], HEAD), ALU.subtract)
                dve.drain()
                nc.vector.tensor_tensor(sq[:, :], yy, yy, ALU.mult)
                dve.drain()
                nc.vector.tensor_reduce(stat[:, u, 1, :], heads(sq[:, :]), AX.X, ALU.add)
                dve.drain()
                nc.vector.tensor_scalar(stat[:, u, 1, :], stat[:, u, 1, :], 1.0 / HEAD, RW_GN_EPS, ALU.mult, ALU.add)\
                    .then_inc(var_made, 1)
                dve.wait_ge(root_made, i + 1)
                nc.vector.reciprocal(stat[:, u, 3, :], stat[:, u, 2, :])
                dve.drain()
                nc.vector.tensor_tensor(heads(yy), heads(yy), last_of(stat[:, u, 3, :], HEAD), ALU.mult).then_inc(y_made, 1)
                dve.wait_ge(turned, i + 1)
                dve.wait_ge(stored[u], (r + 1) * 16)
                for j in range(QT):
                    nc.vector.tensor_scalar(res[:, u, j, :], pt[:, u, j * P:(j + 1) * P], lnx[:, 0, j:j + 1],
                                            lnx[:, 1, j:j + 1], ALU.mult, ALU.add)
                dve.drain()
                nc.vector.tensor_tensor(res[:, u], res[:, u], ex[:, u, 0], ALU.add)
                dve.drain()
                nc.vector.tensor_tensor(res[:, u], res[:, u], ex[:, u, 1], ALU.mult).then_inc(res_made, 1)

            steps(dve, LAT_TILES, 2, body)


def hgrn_prepare(nc, proj, par, hg):
    with Stage(nc, "hgprep") as st:
        q = st.sb("q", [P, TOK])
        f = st.sb("f", [P, 2, TOK])
        lb = st.sb("lb", [P, 4, 2])
        reset = st.sb("reset", [P, TOK])
        kf = st.sb("kf", [P, TOK])
        lf = st.sb("lf", [P, TOK])
        cum = st.sb("cum", [P, TOK])
        inc = st.sb("inc", [P, TOK])
        dq = st.sb("dq", [P, TOK])
        fac = st.sb("fac", [P, 2, 4, TOK])
        tot = st.sb("tot", [P, 2, HG_CHUNKS])
        loaded, in_used = st.sem("loaded"), st.sem("in_used")
        lb_ready, logs_ready, cums_ready, exps_ready = (st.sem("lb_ready"), st.sem("logs_ready"), st.sem("cums_ready"),
                                                      st.sem("exps_ready"))
        fac_ready, q_ready = st.sem("fac_ready"), st.sem("q_ready")
        stored = [st.sem(f"stored{d}") for d in range(2)]
        block = st.block()
        LOADS, STORES = 5, 5

        def by_chunk(ap):
            return ap.rearrange("p (c t) -> p c t", t=HG_CHUNK)

        @block.sync
        def _(sp):
            for d in range(2):
                sp.sem_inc(stored[d], 16 * STORES)

            def body(i, u, r):
                at = bass.ds(i * P, P)
                sp.wait_ge(in_used, i + 1)
                for dst, row in ((q[:, :], ROW_Q), (f[:, 0, :], ROW_FF), (f[:, 1, :], ROW_FB)):
                    sp.dma_start(dst, proj[bass.ds(i * P + row, P), :]).then_inc(loaded, 16)
                for layer in range(2):
                    sp.dma_start(lb[:, layer, :], par["lb"][:, layer, at].rearrange("d p -> p d")).then_inc(loaded, 16)
                for d in range(2):
                    sp.wait_ge(fac_ready, i * 2 + d + 1)
                    for j, name in enumerate(("qs", "ks", "qc", "kh")):
                        sp.dma_start(hg[name][d, at, :], fac[:, d, j, :]).then_inc(stored[d], 16)
                    sp.dma_start(hg["tot"][d, at, :], tot[:, d, :]).then_inc(stored[d], 16)

            steps(sp, QT, 1, body)
            for d in range(2):
                sp.wait_ge(stored[d], 16 * STORES * (QT + 1))

        @block.scalar
        def _(act):
            def body(i, u, r):
                act.wait_ge(lb_ready, i + 1)
                nc.scalar.activation(lb[:, 2, :], lb[:, 2, :], ACT.Sigmoid).then_inc(q_ready, 1)
                nc.scalar.activation(q[:, :], q[:, :], ACT.Silu).then_inc(q_ready, 1)
                for d in range(2):
                    act.wait_ge(cums_ready, i * 4 + 2 * d + 1)
                    nc.scalar.activation(kf[:, :], f[:, d, :], ACT.Sigmoid, scale=-1.0)
                    nc.scalar.activation(lf[:, :], f[:, d, :], ACT.Sigmoid)
                    act.drain()
                    nc.scalar.activation(lf[:, :], lf[:, :], ACT.Ln, scale=lb[:, 3, d:d + 1], bias=lb[:, 2, d:d + 1])\
                        .then_inc(logs_ready, 1)
                    act.wait_ge(cums_ready, i * 4 + 2 * d + 2)
                    act.wait_ge(stored[d], (i + 1) * (16 * STORES))
                    nc.scalar.activation(fac[:, d, 0, :], dq[:, :], ACT.Exp)
                    nc.scalar.activation(fac[:, d, 1, :], dq[:, :], ACT.Exp, scale=-1.0)
                    nc.scalar.activation(fac[:, d, 2, :], inc[:, :], ACT.Exp)
                    nc.scalar.activation(fac[:, d, 3, :], lf[:, :], ACT.Exp)
                    nc.scalar.activation(tot[:, d, :], by_chunk(cum[:, :])[:, :, HG_CHUNK - 1], ACT.Exp)\
                        .then_inc(exps_ready, 1)

            steps(act, QT, 1, body)

        @block.vector
        def _(dve):
            nc.vector.memset(reset[:, :], 1.0)
            dve.drain()
            nc.vector.memset(by_chunk(reset[:, :])[:, :, 0:1], 0.0)
            dve.drain()
            dve.sem_inc(in_used, 1)

            def body(i, u, r):
                dve.wait_ge(loaded, (i + 1) * (16 * LOADS))
                nc.vector.tensor_tensor(lb[:, 2, :], lb[:, 0, :], lb[:, 1, :], ALU.subtract).then_inc(lb_ready, 1)
                dve.wait_ge(q_ready, i * 2 + 1)
                nc.vector.tensor_scalar(lb[:, 3, :], lb[:, 2, :], -1.0, 1.0, ALU.mult, ALU.add).then_inc(cums_ready, 1)
                for d in range(2):
                    dve.wait_ge(logs_ready, i * 2 + d + 1)
                    nc.vector.tensor_scalar(kf[:, :], kf[:, :], lb[:, 3, d:d + 1], None, ALU.mult)
                    nc.vector.tensor_tensor_scan(cum[:, :], reset[:, :], lf[:, :], 0.0, ALU.mult, ALU.add)
                    dve.drain()
                    c = by_chunk(cum[:, :])
                    last = c[:, :, HG_CHUNK - 1:HG_CHUNK].broadcast_to([P, HG_CHUNKS, HG_CHUNK])
                    if d == 0:
                        nc.vector.tensor_copy(inc[:, :], cum[:, :])
                    else:
                        nc.vector.tensor_tensor(by_chunk(inc[:, :]), last, c, ALU.subtract)
                        dve.drain()
                        nc.vector.tensor_tensor(inc[:, :], inc[:, :], lf[:, :], ALU.add)
                    dve.drain()
                    mid = HG_CHUNK // 2 if d == 0 else HG_CHUNK // 2 - 1
                    nc.vector.tensor_tensor(by_chunk(lf[:, :]), last, by_chunk(inc[:, :]), ALU.subtract)
                    nc.vector.tensor_tensor(by_chunk(dq[:, :]), by_chunk(inc[:, :]),
                                            by_chunk(inc[:, :])[:, :, mid:mid + 1].broadcast_to([P, HG_CHUNKS, HG_CHUNK]),
                                            ALU.subtract).then_inc(cums_ready, 1)
                    dve.wait_ge(exps_ready, i * 2 + d + 1)
                    dve.wait_ge(q_ready, i * 2 + 2)
                    g = [fac[:, d, j, :] for j in range(4)]
                    nc.vector.scalar_tensor_tensor(g[0], q[:, :], HEAD ** -0.5, g[0], ALU.mult, ALU.mult)
                    nc.vector.tensor_tensor(g[1], kf[:, :], g[1], ALU.mult)
                    nc.vector.scalar_tensor_tensor(g[2], q[:, :], HEAD ** -0.5, g[2], ALU.mult, ALU.mult)
                    nc.vector.tensor_tensor(g[3], kf[:, :], g[3], ALU.mult).then_inc(fac_ready, 1)
                    dve.drain()
                    if d == 0:
                        dve.sem_inc(cums_ready, 1)
                dve.sem_inc(in_used, 1)

            steps(dve, QT, 1, body)


def hgrn_scan(nc, consts, proj, hg):
    NC = P // HG_CHUNK
    with Stage(nc, "hgscan") as st:
        def pair(name, shape):
            return [st.sb(f"{name}{d}", shape) for d in range(2)]

        flat = pair("flat", [P, 2, QT, P])
        qk = pair("qk", [HEAD, 3, HEADS, P])
        tot = pair("tot", [HEAD, HEADS, NC])
        kv_t = pair("kv_t", [P, 2, HEADS, HEAD])
        sc = pair("sc", [P, HEADS, P])
        s = pair("s", [HEAD, NC + 1, HEADS, HEAD])
        o = pair("o", [P, HEADS, HEAD])
        ps = st.psum("ps", [P, 8, BANK])
        loaded = [st.sem(f"loaded{d}") for d in range(2)]
        stored = [st.sem(f"stored{d}") for d in range(2)]
        turned, copied, kv_ready, state_ready = st.sem("turned"), st.sem("copied"), st.sem("kv_ready"), st.sem("state_ready")
        sc_ready, sc_used, o_ready, within, o_used = (st.sem("sc_ready"), st.sem("sc_used"), st.sem("o_ready"),
                                                      st.sem("within"), st.sem("o_used"))
        block = st.block()
        LOADS = 2 + 3 + 1

        def rounds(eng, body):
            for r in range(CTX_TILES):
                for d in range(2):
                    body(2 * r + d, r, d, r if d == 0 else CTX_TILES - 1 - r, False)
            with eng.Fori(0, LAT_TILES) as i:
                for d in range(2):
                    body(i * 2 + (2 * CTX_TILES + d), i + CTX_TILES, d,
                         i + CTX_TILES if d == 0 else i * -1 + (TILES - 1), True)

        def quarter(d, c):
            return c if d == 0 else NC - 1 - c

        @block.sync
        def _(sp):
            def body(n, r, d, t, out):
                tk = bass.ds(t * P, P)
                sp.wait_ge(o_used, n + 1)
                sp.dma_start(flat[d][:, 0], hg["kh"][d, :, tk].rearrange("(g p) t -> p g t", p=P)).then_inc(loaded[d], 16)
                sp.dma_start(flat[d][:, 1], proj[ROW_I:ROW_I + WID, tk].rearrange("(g p) t -> p g t", p=P))\
                    .then_inc(loaded[d], 16)
                for j, name in enumerate(("qs", "ks", "qc")):
                    sp.dma_start(qk[d][:, j], hg[name][d, :, tk].rearrange("(h k) t -> k h t", k=HEAD))\
                        .then_inc(loaded[d], 16)
                sp.dma_start(tot[d][:], hg["tot"][d, :, bass.ds(t * NC, NC)].rearrange("(h k) c -> k h c", k=HEAD))\
                    .then_inc(loaded[d], 16)

            rounds(sp, body)

        @block.tensor
        def _(pe):
            def body(n, r, d, t, out):
                pe.wait_ge(loaded[d], (r + 1) * (16 * LOADS))
                pe.wait_ge(o_used, n + 2)
                for j in range(2):
                    for g in range(QT):
                        op = nc.tensor.transpose(ps[:, j, g * P:(g + 1) * P], flat[d][:, j, g, :], consts["ident"][:, :])
                op.then_inc(turned, 1)
                for h in range(HEADS):
                    op = nc.tensor.matmul(ps[:, 6 + h // 4, (h % 4) * P:(h % 4 + 1) * P], qk[d][:, 1, h, :],
                                          qk[d][:, 0, h, :], start=True, stop=True)
                op.then_inc(sc_ready, 1)
                pe.wait_ge(copied, n + 1)
                for c in range(NC):
                    w = quarter(d, c)
                    rows = slice(w * HG_CHUNK, (w + 1) * HG_CHUNK)
                    for h in range(HEADS):
                        op = nc.tensor.matmul(ps[0:HEAD, 2 + c, h * HEAD:(h + 1) * HEAD], kv_t[d][rows, 0, h, :],
                                              kv_t[d][rows, 1, h, :], start=True, stop=True,
                                              tile_position=(w * HG_CHUNK, 0))
                op.then_inc(kv_ready, 1)
                pe.wait_ge(sc_used, n + 1)
                for h in range(HEADS):
                    op = nc.tensor.matmul(ps[:, 0, h * HEAD:(h + 1) * HEAD], sc[d][:, h, :], kv_t[d][:, 1, h, :],
                                          start=True, stop=True)
                op.then_inc(o_ready, 1)
                pe.wait_ge(state_ready, n + 1)
                for h in range(HEADS):
                    op = nc.tensor.matmul(ps[:, 2 + h // 2, (h % 2) * 4 * HEAD:(h % 2 + 1) * 4 * HEAD],
                                          qk[d][:, 2, h, :], s[d][:, 0:NC, h, :], start=True, stop=True)
                op.then_inc(o_ready, 1)

            rounds(pe, body)

        @block.scalar
        def _(act):
            for d in range(2):
                act.sem_inc(stored[d], 16)

            def body(n, r, d, t, out):
                act.wait_ge(turned, n + 1)
                op = nc.scalar.copy(kv_t[d][:].rearrange("p j h k -> p j (h k)"), ps[:, 0:2, :])
                op.then_inc(copied, 1)
                act.wait_ge(o_ready, n * 2 + 1)
                if out:
                    act.wait_ge(stored[d], (r + (1 - CTX_TILES)) * 16)
                nc.scalar.copy(o[d][:].rearrange("p h v -> p (h v)"), ps[:, 0, :]).then_inc(within, 1)
                if out:
                    act.wait_ge(o_used, n + 3)
                    act.dma_start(hg["o"][d, bass.ds(t * P - CTX, P), :], o[d][:].rearrange("p h v -> p (h v)"))\
                        .then_inc(stored[d], 16)

            rounds(act, body)
            for d in range(2):
                act.wait_ge(stored[d], 16 * (LAT_TILES + 1))

        @block.vector
        def _(dve):
            for d in range(2):
                nc.vector.memset(s[d][:, 0], 0.0)
            dve.drain()
            dve.sem_inc(o_used, 2)

            def body(n, r, d, t, out):
                dve.wait_ge(sc_ready, n + 1)
                for g in range(2):
                    op = nc.vector.tensor_tensor(sc[d][:, 4 * g:4 * g + 4, :],
                                                 ps[:, 6 + g, :].rearrange("p (h t) -> p h t", h=4),
                                                 over(consts["hg_from"][:, d, :], 4), ALU.mult)
                op.then_inc(sc_used, 1)
                dve.wait_ge(kv_ready, n + 1)
                for c in range(NC):
                    nc.vector.tensor_tensor(s[d][:, c + 1], s[d][:, c], tot[d][:, :, quarter(d, c):quarter(d, c) + 1]
                                            .broadcast_to([HEAD, HEADS, HEAD]), ALU.mult)
                    dve.drain()
                    op = nc.vector.tensor_tensor(s[d][:, c + 1], s[d][:, c + 1],
                                                 ps[0:HEAD, 2 + c, :].rearrange("k (h v) -> k h v", h=HEADS), ALU.add)
                    if c < NC - 1:
                        dve.drain()
                op.then_inc(state_ready, 1)
                dve.wait_ge(o_ready, n * 2 + 2)
                dve.wait_ge(within, n + 1)
                if out:
                    for c in range(NC):
                        w = quarter(d, c)
                        rows = slice(w * HG_CHUNK, (w + 1) * HG_CHUNK)
                        v = ps[rows, 2:6, :].rearrange("t b (h c v) -> t (b h) c v", h=2, c=NC)
                        nc.vector.tensor_tensor(o[d][rows], o[d][rows], v[:, :, c, :], ALU.add)
                nc.vector.tensor_copy(s[d][:, 0], s[d][:, NC])
                dve.drain()
                dve.sem_inc(o_used, 1)

            rounds(dve, body)


def hgrn_output(nc, consts, proj, hg, par, mix):
    with Stage(nc, "hgout") as st:
        o = st.sb("o", [P, 2, 2, WID])
        g = st.sb("g", [P, 2, QT, P])
        sq = st.sb("sq", [P, WID])
        stat = st.sb("stat", [P, 2, 3, HEADS])
        ng = st.sb("ng", [P, 1])
        res = st.sb("res", [P, 2, QT, P])
        pt = st.psum("pt", [P, 2, BANK])
        once = st.sem("once")
        loaded = [st.sem(f"loaded{u}") for u in range(2)]
        stored = [st.sem(f"stored{u}") for u in range(2)]
        var_made, root_made, o_made, turned, res_made = (st.sem("var_made"), st.sem("root_made"), st.sem("o_made"),
                                                         st.sem("turned"), st.sem("res_made"))
        block = st.block()

        @block.sync
        def _(sp):
            for h in range(2):
                sp.dma_start(ng[h * HEAD:(h + 1) * HEAD, :], par["norm_g"].rearrange("(p o) -> p o", o=1))\
                    .then_inc(once, 16)

            def body(i, u, r):
                sp.wait_ge(res_made, i + 1)
                for d in range(2):
                    sp.dma_start(o[:, u, d, :], hg["o"][d, bass.ds(i * P, P), :]).then_inc(loaded[u], 16)
                sp.dma_start(g[:, u], proj[ROW_G:ROW_G + WID, bass.ds(i * P + CTX, P)]
                             .rearrange("(j p) t -> p j t", p=P)).then_inc(loaded[u], 16)

            steps(sp, LAT_TILES, 2, body)

        @block.tensor
        def _(pe):
            def body(i, u, r):
                pe.wait_ge(o_made, i + 1)
                pe.wait_ge(res_made, i + 1)
                for j in range(QT):
                    op = nc.tensor.transpose(pt[:, u, j * P:(j + 1) * P], o[:, u, 0, j * P:(j + 1) * P],
                                             consts["ident"][:, :])
                op.then_inc(turned, 1)

            steps(pe, LAT_TILES, 2, body)

        @block.scalar
        def _(act):
            for u in range(2):
                act.sem_inc(stored[u], 16)

            def body(i, u, r):
                act.wait_ge(var_made, i + 1)
                nc.scalar.activation(stat[:, u, 1, :], stat[:, u, 0, :], ACT.Sqrt)
                nc.scalar.activation(g[:, u], g[:, u], ACT.Silu).then_inc(root_made, 1)
                act.wait_ge(res_made, i + 3)
                act.dma_start(mix[WID:2 * WID, bass.ds(i * P, P)].rearrange("(j p) t -> p j t", p=P), res[:, u])\
                    .then_inc(stored[u], 16)

            steps(act, LAT_TILES, 2, body)
            for u in range(2):
                act.wait_ge(stored[u], 16 * (LAT_TILES // 2 + 1))

        @block.vector
        def _(dve):
            dve.wait_ge(once, 32)
            dve.sem_inc(res_made, 2)

            def heads(ap):
                return ap.rearrange("p (h v) -> p h v", v=HEAD)

            def body(i, u, r):
                dve.wait_ge(loaded[u], (r + 1) * 48)
                oo = o[:, u, 0, :]
                nc.vector.tensor_tensor(oo, oo, o[:, u, 1, :], ALU.add)
                dve.drain()
                nc.vector.tensor_tensor(sq[:, :], oo, oo, ALU.mult)
                dve.drain()
                nc.vector.tensor_reduce(stat[:, u, 0, :], heads(sq[:, :]), AX.X, ALU.add)
                dve.drain()
                nc.vector.tensor_scalar(stat[:, u, 0, :], stat[:, u, 0, :], 1.0 / HEAD, EPS, ALU.mult, ALU.add)\
                    .then_inc(var_made, 1)
                dve.wait_ge(root_made, i + 1)
                nc.vector.reciprocal(stat[:, u, 2, :], stat[:, u, 1, :])
                dve.drain()
                nc.vector.tensor_tensor(heads(oo), heads(oo), last_of(stat[:, u, 2, :], HEAD), ALU.mult).then_inc(o_made, 1)
                dve.wait_ge(turned, i + 1)
                dve.wait_ge(stored[u], (r + 1) * 16)
                nc.vector.scalar_tensor_tensor(res[:, u].rearrange("p j t -> p (j t)"), pt[:, u, :], ng[:, 0:1],
                                               g[:, u].rearrange("p j t -> p (j t)"), ALU.mult, ALU.mult)\
                    .then_inc(res_made, 1)

            steps(dve, LAT_TILES, 2, body)


def linear_tokens(nc, name, act, w, resid, out, gain=None):
    K = w.shape[0]
    KT = K // P
    with Stage(nc, name) as st:
        wt = st.sb("w", [P, KT, D])
        a = st.sb("a", [P, 2, KT, P])
        x = st.sb("x", [P, 2, D])
        res = st.sb("res", [P, 2, D])
        g = st.sb("g", [P, D])
        ps = st.psum("ps", [P, 2, 2, BANK])
        once = st.sem("once")
        loaded = [st.sem(f"loaded{u}") for u in range(2)]
        stored = [st.sem(f"stored{u}") for u in range(2)]
        products, used = st.sem("products"), st.sem("used")
        block = st.block()
        n_once = 2 + (gain is not None)

        @block.sync
        def _(sp):
            def body(i, u, r):
                sp.wait_ge(used, i + 1)
                sp.dma_start(a[:, u], act[:, bass.ds(i * P, P)].rearrange("(k p) t -> p k t", p=P)).then_inc(loaded[u], 16)
                sp.dma_start(x[:, u, :], resid[bass.ds(i * P, P), :]).then_inc(loaded[u], 16)

            steps(sp, LAT_TILES, 2, body)

        @block.tensor
        def _(pe):
            pe.wait_ge(once, 16 * n_once)

            def body(i, u, r):
                pe.wait_ge(loaded[u], (r + 1) * 32)
                pe.wait_ge(used, i + 1)
                for n in range(2):
                    for k in range(KT):
                        op = nc.tensor.matmul(ps[:, u, n, :], a[:, u, k, :], wt[:, k, n * BANK:(n + 1) * BANK],
                                              start=(k == 0), stop=(k == KT - 1))
                op.then_inc(products, 1)

            steps(pe, LAT_TILES, 2, body)

        @block.vector
        def _(dve):
            dve.sem_inc(used, 2)
            dve.wait_ge(once, 16 * n_once)

            def body(i, u, r):
                dve.wait_ge(products, i + 1)
                dve.wait_ge(stored[u], (r + 1) * 16)
                y = ps[:, u].rearrange("p b n -> p (b n)")
                if gain is not None:
                    nc.vector.tensor_tensor(res[:, u, :], y, g[:, :], ALU.mult)
                    dve.drain()
                    y = res[:, u, :]
                nc.vector.tensor_tensor(res[:, u, :], y, x[:, u, :], ALU.add).then_inc(used, 1)

            steps(dve, LAT_TILES, 2, body)

        @block.scalar
        def _(act_e):
            for h in range(2):
                act_e.dma_start(wt[:, h * KT // 2:(h + 1) * KT // 2, :],
                                w[h * K // 2:(h + 1) * K // 2, :].rearrange("(k p) n -> p k n", p=P)).then_inc(once, 16)
            if gain is not None:
                act_e.dma_start(g[:, :], gain.broadcast_to([P, D])).then_inc(once, 16)
            for u in range(2):
                act_e.sem_inc(stored[u], 16)

            def body(i, u, r):
                act_e.wait_ge(used, i + 3)
                act_e.dma_start(out[bass.ds(i * P, P), :], res[:, u, :]).then_inc(stored[u], 16)

            steps(act_e, LAT_TILES, 2, body)
            for u in range(2):
                act_e.wait_ge(stored[u], 16 * (LAT_TILES // 2 + 1))


def route(nc, h2, router_w, router_b, gates):
    GE = N_EXPERTS // N_GROUPS
    with Stage(nc, "route") as st:
        w = st.sb("w", [P, KD, N_EXPERTS])
        bias = st.sb("bias", [P, N_EXPERTS])
        score = st.sb("score", [P, 2, N_EXPERTS])
        sel = st.sb("sel", [P, N_EXPERTS])
        best = st.sb("best", [P, N_GROUPS, 8])
        grp = st.sb("grp", [P, 4, N_GROUPS])
        top = st.sb("top", [P, 8])
        left = st.sb("left", [P, N_EXPERTS])
        tot = st.sb("tot", [P, 2])
        ps = st.psum("ps", [P, 2, BANK])
        once, products, scored, used = st.sem("once"), st.sem("products"), st.sem("scored"), st.sem("used")
        block = st.block()
        GONE = -1e30

        @block.sync
        def _(sp):
            sp.dma_start(w[:], router_w.rearrange("(k p) e -> p k e", p=P)).then_inc(once, 16)
            sp.dma_start(bias[:, :], router_b.rearrange("(o e) -> o e", o=1).broadcast_to([P, N_EXPERTS])).then_inc(once, 16)

        @block.tensor
        def _(pe):
            pe.wait_ge(once, 32)
            for t in range(LAT_TILES):
                if t >= 2:
                    pe.wait_ge(scored, t - 1)
                for k in range(KD):
                    op = nc.tensor.matmul(ps[:, t % 2, 0:N_EXPERTS], h2[:, k, t * P:(t + 1) * P], w[:, k, :],
                                          start=(k == 0), stop=(k == KD - 1))
                op.then_inc(products, 1)

        @block.scalar
        def _(act):
            for t in range(LAT_TILES):
                act.wait_ge(products, t + 1)
                if t >= 2:
                    act.wait_ge(used, t - 1)
                nc.scalar.activation(score[:, t % 2, :], ps[:, t % 2, 0:N_EXPERTS], ACT.Sigmoid).then_inc(scored, 1)

        @block.vector
        def _(dve):
            dve.wait_ge(once, 32)

            def body(t, u, r):
                sc = score[:, u, :]
                dve.wait_ge(scored, t + 1)
                nc.vector.tensor_tensor(sel[:, :], sc, bias[:, :], ALU.add)
                dve.drain()
                for g in range(N_GROUPS):
                    nc.vector.max(best[:, g, :], sel[:, g * GE:(g + 1) * GE])
                dve.drain()
                nc.vector.tensor_tensor(grp[:, 0, :], best[:, :, 0], best[:, :, 1], ALU.add)
                dve.drain()
                nc.vector.max(top[:, :], grp[:, 0, :])
                dve.drain()
                nc.vector.memset(top[:, TOPK_GROUPS:], 1e30)
                dve.drain()
                nc.vector.match_replace(grp[:, 1, :], top[:, :], grp[:, 0, :], GONE)
                dve.drain()
                nc.vector.tensor_tensor(grp[:, 2, :], grp[:, 1, :], grp[:, 0, :], ALU.is_equal)
                dve.drain()
                nc.vector.tensor_scalar(grp[:, 3, :], grp[:, 2, :], GONE, None, ALU.mult)
                dve.drain()
                nc.vector.tensor_tensor(sel[:, :].rearrange("p (g e) -> p g e", e=GE),
                                        sel[:, :].rearrange("p (g e) -> p g e", e=GE),
                                        last_of(grp[:, 3, :], GE), ALU.add)
                dve.drain()
                nc.vector.max(top[:, :], sel[:, :])
                dve.drain()
                nc.vector.match_replace(left[:, :], top[:, :], sel[:, :], 2 * GONE)
                dve.drain()
                nc.vector.tensor_tensor(left[:, :], left[:, :], sel[:, :], ALU.not_equal)
                dve.drain()
                nc.vector.tensor_tensor(left[:, :], left[:, :], sc, ALU.mult).then_inc(used, 1)
                dve.drain()
                nc.vector.reduce_sum(tot[:, 0:1], left[:, :], axis=AX.X)
                dve.drain()
                nc.vector.reciprocal(tot[:, 1:2], tot[:, 0:1])
                dve.drain()
                nc.vector.tensor_scalar(gates[:, t, :], left[:, :], tot[:, 1:2], ROUTE_SCALE, ALU.mult, ALU.mult)
                dve.drain()

            for t in range(LAT_TILES):
                body(t, t % 2, t // 2)


def experts(nc, h2, gates, acc, shared, routed):
    MT = D_EXPERT // P
    with Stage(nc, "moe") as st:
        wgu = st.sb("wgu", [P, 2, 2, KD, D_EXPERT])
        wd = st.sb("wd", [P, 2, MT, D])
        sg = st.sb("sg", [P, 2, BANK])
        hid = st.sb("hid", [P, MT, SEQ])
        pgu = st.psum("pgu", [P, 2, 2, BANK])
        pd = st.psum("pd", [P, 4, BANK])
        loaded = [st.sem(f"loaded{u}") for u in range(2)]
        gu_ready, sg_ready, hid_ready, y_ready, y_used = (st.sem("gu_ready"), st.sem("sg_ready"), st.sem("hid_ready"),
                                                        st.sem("y_ready"), st.sem("y_used"))
        block = st.block()
        PARTS = MT * (SEQ // BANK)
        DOWN = LAT_TILES * (D // BANK)

        def every(eng, body):
            body(0, 0, 0, None)
            with eng.Fori(0, N_EXPERTS // 2) as i:
                for v in range(2):
                    body(i * 2 + (v + 1), (v + 1) % 2, i + (v + 1) // 2, i * 2 + v)

        @block.sync
        def _(sp):
            def body(n, u, r, e):
                sp.wait_ge(y_ready, n * DOWN + DOWN)
                for j in range(2):
                    src = shared[j] if e is None else routed[j][bass.ds(e, 1)].rearrange("o k m -> (o k) m")
                    sp.dma_start(wgu[:, u, j], src.rearrange("(k p) m -> p k m", p=P)).then_inc(loaded[u], 16)
                src = shared[2] if e is None else routed[2][bass.ds(e, 1)].rearrange("o k m -> (o k) m")
                sp.dma_start(wd[:, u], src.rearrange("(k p) m -> p k m", p=P)).then_inc(loaded[u], 16)

            every(sp, body)

        @block.tensor
        def _(pe):
            pe.sem_inc(y_ready, 2 * DOWN)

            def body(n, u, r, e):
                pe.wait_ge(loaded[u], (r + 1) * 48)
                for c in range(PARTS):
                    m, h = c // 2, c % 2
                    pe.wait_ge(hid_ready, n * PARTS + (c + 1))
                    for j in range(2):
                        for k in range(KD):
                            op = nc.tensor.matmul(pgu[:, c % 2, j, :], wgu[:, u, j, k, m * P:(m + 1) * P],
                                                  h2[:, k, h * BANK:(h + 1) * BANK], start=(k == 0), stop=(k == KD - 1))
                    op.then_inc(gu_ready, 1)
                pe.wait_ge(hid_ready, n * PARTS + (PARTS + 2))
                for c in range(DOWN):
                    t, h = c // 2, c % 2
                    pe.wait_ge(y_used, n * DOWN + (c + 1))
                    for k in range(MT):
                        op = nc.tensor.matmul(pd[:, c % 4, :], hid[:, k, t * P:(t + 1) * P],
                                              wd[:, u, k, h * BANK:(h + 1) * BANK], start=(k == 0), stop=(k == MT - 1))
                    op.then_inc(y_ready, 1)

            every(pe, body)

        @block.scalar
        def _(act):
            def body(n, u, r, e):
                for c in range(PARTS):
                    act.wait_ge(gu_ready, n * PARTS + (c + 1))
                    act.wait_ge(hid_ready, n * PARTS + (c + 1))
                    nc.scalar.activation(sg[:, c % 2, :], pgu[:, c % 2, 0, :], ACT.Silu).then_inc(sg_ready, 1)

            every(act, body)

        @block.vector
        def _(dve):
            dve.sem_inc(hid_ready, 2)
            dve.sem_inc(y_used, 4)

            def body(n, u, r, e):
                dve.drain()
                for c in range(PARTS):
                    m, h = c // 2, c % 2
                    dve.wait_ge(sg_ready, n * PARTS + (c + 1))
                    nc.vector.tensor_tensor(hid[:, m, h * BANK:(h + 1) * BANK], sg[:, c % 2, :], pgu[:, c % 2, 1, :],
                                            ALU.mult).then_inc(hid_ready, 1)
                for c in range(DOWN):
                    t, h = c // 2, c % 2
                    dve.wait_ge(y_ready, n * DOWN + (c + 1 + 2 * DOWN))
                    to = acc[:, t, h * BANK:(h + 1) * BANK]
                    if e is None:
                        nc.vector.tensor_copy(to, pd[:, c % 4, :]).then_inc(y_used, 1)
                    else:
                        nc.vector.scalar_tensor_tensor(to, pd[:, c % 4, :], gates[:, t, bass.ds(e, 1)], to,
                                                       ALU.mult, ALU.add).then_inc(y_used, 1)

            every(dve, body)


def finish_block(nc, acc, gain, x1, norm_g, out):
    with Stage(nc, "finish") as st:
        x = st.sb("x", [P, LAT_TILES, D])
        sq = st.sb("sq", [P, D])
        ms = st.sb("ms", [P, LAT_TILES, 4])
        g = st.sb("g", [P, 2, D])
        once, summed, squared, mean, rooted, made, stored = (st.sem("once"), st.sem("summed"), st.sem("squared"),
                                                             st.sem("mean"), st.sem("rooted"), st.sem("made"), st.sem("stored"))
        block = st.block()

        @block.sync
        def _(sp):
            sp.dma_start(g[:, 0, :], gain.broadcast_to([P, D])).then_inc(once, 16)
            sp.dma_start(g[:, 1, :], norm_g.rearrange("(o e) -> o e", o=1).broadcast_to([P, D])).then_inc(once, 16)
            sp.dma_start(x[:], x1.rearrange("(t p) d -> p t d", p=P)).then_inc(once, 16)
            for t in range(LAT_TILES):
                sp.wait_ge(made, t + 1)
                sp.dma_start(out[t * P:(t + 1) * P, :], x[:, t, :]).then_inc(stored, 16)
            sp.wait_ge(stored, 16 * LAT_TILES)

        @block.scalar
        def _(act):
            for t in range(LAT_TILES):
                act.wait_ge(summed, t + 1)
                act.drain()
                nc.scalar.activation(sq[:, :], x[:, t, :], ACT.Square, accum_out=ms[:, t, 0:1]).then_inc(squared, 1)
            act.wait_ge(mean, 1)
            nc.scalar.activation(ms[:, :, 2], ms[:, :, 1], ACT.Sqrt).then_inc(rooted, 1)

        @block.vector
        def _(dve):
            dve.wait_ge(once, 48)
            for t in range(LAT_TILES):
                nc.vector.tensor_tensor(acc[:, t, :], acc[:, t, :], g[:, 0, :], ALU.mult)
                dve.drain()
                nc.vector.tensor_tensor(x[:, t, :], x[:, t, :], acc[:, t, :], ALU.add).then_inc(summed, 1)
            dve.wait_ge(squared, LAT_TILES)
            nc.vector.tensor_scalar(ms[:, :, 1], ms[:, :, 0], 1.0 / D, EPS, ALU.mult, ALU.add).then_inc(mean, 1)
            dve.wait_ge(rooted, 1)
            nc.vector.reciprocal(ms[:, :, 3], ms[:, :, 2])
            dve.drain()
            for t in range(LAT_TILES):
                nc.vector.scalar_tensor_tensor(x[:, t, :], x[:, t, :], ms[:, t, 3:4], g[:, 1, :], ALU.mult, ALU.mult)\
                    .then_inc(made, 1)


def modulated_norm(nc, consts, name, sources, norm_g, mods, shift_at, dst):
    def params(st, scale, bias):
        g = st.sb("g", [P, KD])
        n = 1 + max(i for _, _, i in sources)

        def make(dve):
            nc.vector.tensor_scalar(scale[:, 0:n, :], scale[:, 0:n, :], 1.0, None, ALU.add)
            dve.drain()
            for i in range(n):
                nc.vector.tensor_tensor(scale[:, i, :], scale[:, i, :], g[:, :], ALU.mult)

        loads = [(g[:, :], column(norm_g))]
        for i in range(n):
            loads += [(bias[:, i, :], column(mods[i, shift_at:shift_at + D])),
                      (scale[:, i, :], column(mods[i, shift_at + D:shift_at + 2 * D]))]
        return loads, make

    norm_columns(nc, consts, name, sources, params, dst)


def plain_norm(nc, consts, name, src, norm_g, dst):
    def params(st, scale, bias):
        return [(scale[:, 0, :], column(norm_g))], lambda dve: nc.vector.memset(bias[:], 0.0)

    norm_columns(nc, consts, name, [(src, 0, 0)], params, dst)


def first_block(nc, consts, i, s):
    mods, proj, mix, x1 = s["mods"], s["proj"], s["mix"], s["x1"]
    rw, hg = s["rw"], s["hg"]
    modulation(nc, i["c"], i["c_ctx"], i["w_mod"], i["b_mod"], mods)
    with nc.sbuf_tensor("hT", [P, KD, TOK], F32) as hT:
        modulated_norm(nc, consts, "norm1", [(i["ctx"][0], 0, 1), (i["x"][0], CTX, 0)], i["norm1_g"][0], mods, 0, hT)
        linear_columns(nc, "proj", i["w_in"][0], hT, TOK, proj)
    rwkv_prepare(nc, consts, proj, {
        "conv": i["rw_conv"][0].rearrange("y x c -> (y x) c"), "w0": i["rw_w0"][0], "a0": i["rw_a0"][0],
        "k_k": i["rw_k_k"][0], "k_a": i["rw_k_a"][0], "r_k": i["rw_r_k"][0].rearrange("h d -> (h d)"),
        "w2": i["rw_w2"][0].rearrange("d r c -> (d r) c"), "a2": i["rw_a2"][0].rearrange("d r c -> (d r) c"),
        "g2": i["rw_g2"][0]}, rw)
    for d in range(2):
        rwkv_chunks(nc, consts, rw, d)
    rwkv_states(nc, rw)
    rwkv_output(nc, consts, rw, {"lnx_g": i["rw_lnx_g"][0], "lnx_b": i["rw_lnx_b"][0]}, mix)
    hgrn_prepare(nc, proj, {"lb": i["hg_lb_logits"]}, hg)
    hgrn_scan(nc, consts, proj, hg)
    hgrn_output(nc, consts, proj, hg, {"norm_g": i["hg_norm_g"][0]}, mix)
    linear_tokens(nc, "out1", mix, i["w_out"][0], i["x"][0], x1, mods[0:1, 2 * D:3 * D])
    moe_block(nc, consts, i, s)


def moe_block(nc, consts, i, s):
    mods, x1 = s["mods"], s["x1"]
    with nc.sbuf_tensor("h2", [P, KD, SEQ], F32) as h2, nc.sbuf_tensor("gates", [P, LAT_TILES, N_EXPERTS], F32) as gates, \
            nc.sbuf_tensor("acc", [P, LAT_TILES, D], F32) as acc:
        modulated_norm(nc, consts, "norm2", [(x1, 0, 0)], i["norm2_g"][0], mods, 3 * D, h2)
        route(nc, h2, i["router_w"][0], i["router_b"][0], gates)
        experts(nc, h2, gates, acc, [i["sh_w_gate"][0], i["sh_w_up"][0], i["sh_w_down"][0]],
                [i["exp_w_gate"][0], i["exp_w_up"][0], i["exp_w_down"][0]])
        finish_block(nc, acc, mods[0:1, 5 * D:6 * D], x1, i["final_norm_g"], s["h"])


def log1p(nc, dve, out, e, z, z2):
    nc.vector.tensor_scalar(z, e, 2.0, None, ALU.add)
    dve.drain()
    nc.vector.reciprocal(z, z)
    dve.drain()
    nc.vector.tensor_tensor(z, z, e, ALU.mult)
    dve.drain()
    nc.vector.tensor_tensor(z2, z, z, ALU.mult)
    dve.drain()
    nc.vector.tensor_scalar(out, z2, 1.0 / 17, None, ALU.mult)
    for k in range(7, 0, -1):
        dve.drain()
        nc.vector.scalar_tensor_tensor(out, out, 1.0 / (2 * k + 1), z2, ALU.add, ALU.mult)
    dve.drain()
    nc.vector.scalar_tensor_tensor(out, out, 1.0, z, ALU.add, ALU.mult)
    dve.drain()
    nc.vector.tensor_scalar(out, out, 2.0, None, ALU.mult)
    dve.drain()


def attention_prepare(nc, consts, proj, par, at):
    with Stage(nc, "atprep") as st:
        x = st.sb("x", [P, 2, 2, SEQ])
        sq = st.sb("sq", [P, 2, SEQ])
        gcol = st.sb("gcol", [P, 2])
        f = st.sb("f", [HEADS, 6, SEQ])
        fb = st.sb("fb", [HEADS, 1])
        ps = st.psum("ps", [P, 2, 2 * BANK])
        once, sq_made, sums, guarded, rooted, made = (st.sem("once"), st.sem("sq_made"), st.sem("sums"), st.sem("guarded"),
                                                      st.sem("rooted"), st.sem("made"))
        f_abs, f_made, f_sent = st.sem("f_abs"), st.sem("f_made"), st.sem("f_sent")
        loaded = [st.sem(f"loaded{u}") for u in range(2)]
        stored = [st.sem(f"stored{u}") for u in range(2)]
        block = st.block()

        @block.sync
        def _(sp):
            for j, name in enumerate(("q_g", "k_g")):
                for h in range(2):
                    sp.dma_start(gcol[h * HEAD:(h + 1) * HEAD, j:j + 1], par[name].rearrange("(p o) -> p o", o=1))\
                        .then_inc(once, 16)
            sp.dma_start(f[:, 0, :], proj[ROW2_F:ROW2_F + HEADS, :]).then_inc(once, 16)
            sp.dma_start(fb[:, :], par["f_b"].rearrange("(p o) -> p o", o=1)).then_inc(once, 16)

            def body(i, u, r):
                sp.wait_ge(stored[u], (r + 1) * 64)
                for j, row in enumerate((ROW2_Q, ROW2_K)):
                    sp.dma_start(x[:, u, j, :], proj[bass.ds(i * P + row, P), :]).then_inc(loaded[u], 16)

            steps(sp, QT, 2, body)

        @block.tensor
        def _(pe):
            def body(i, u, r):
                for j in range(2):
                    pe.wait_ge(sq_made, i * 2 + (j + 1))
                    pe.wait_ge(guarded, i * 2 + (j + 1))
                    for a, n in chunks(SEQ):
                        op = nc.tensor.matmul(ps[:, j, a:a + n], consts["headsum"][:, :], sq[:, j, a:a + n],
                                              start=True, stop=True)
                    op.then_inc(sums, 1)

            steps(pe, QT, 2, body)

        @block.scalar
        def _(act):
            act.wait_ge(once, 96)
            nc.scalar.activation(f[:, 1, :], f[:, 0, :], ACT.Abs, bias=fb[:, 0:1])
            nc.scalar.activation(f[:, 2, :], f[:, 0, :], ACT.Identity, bias=fb[:, 0:1])
            act.drain()
            nc.scalar.activation(f[:, 1, :], f[:, 1, :], ACT.Exp, scale=-1.0).then_inc(f_abs, 1)
            for u in range(2):
                act.sem_inc(stored[u], 64)

            def body(i, u, r):
                act.wait_ge(loaded[u], (r + 1) * 32)
                for j in range(2):
                    act.wait_ge(made, i * 2 + (j + 1))
                    nc.scalar.activation(sq[:, j, :], x[:, u, j, :], ACT.Square).then_inc(sq_made, 1)
                for j in range(2):
                    act.wait_ge(guarded, i * 2 + (j + 3))
                    nc.scalar.activation(sq[:, j, :], sq[:, j, :], ACT.Sqrt).then_inc(rooted, 1)
                for j, name in enumerate(("q", "k")):
                    act.wait_ge(made, i * 2 + (j + 3))
                    for h in range(2):
                        act.dma_start(at[name][bass.ds(i * 2 + h, 1), 0:HEAD, :].rearrange("o k t -> (o k) t"),
                                      x[h * HEAD:(h + 1) * HEAD, u, j, :]).then_inc(stored[u], 16)

            steps(act, QT, 2, body)
            act.wait_ge(f_made, 1)
            for name, row, src in (("q", HEAD, 3), ("q", HEAD + 1, 4), ("k", HEAD, 4), ("k", HEAD + 1, 5)):
                act.dma_start(at[name][:, row, :], f[:, src, :]).then_inc(f_sent, 16)
            act.wait_ge(f_sent, 64)
            for u in range(2):
                act.wait_ge(stored[u], 64 * (QT // 2 + 1))

        @block.vector
        def _(dve):
            dve.sem_inc(guarded, 2)
            dve.sem_inc(made, 2)
            dve.wait_ge(once, 96)

            def body(i, u, r):
                for j in range(2):
                    dve.wait_ge(sums, i * 2 + (j + 1))
                    nc.vector.tensor_scalar(sq[:, j, :], ps[:, j, :], 1.0 / HEAD, EPS, ALU.mult, ALU.add)\
                        .then_inc(guarded, 1)
                for j in range(2):
                    dve.wait_ge(rooted, i * 2 + (j + 1))
                    nc.vector.reciprocal(sq[:, j, :], sq[:, j, :])
                    dve.drain()
                    nc.vector.scalar_tensor_tensor(x[:, u, j, :], x[:, u, j, :], gcol[:, j:j + 1], sq[:, j, :],
                                                   ALU.mult, ALU.mult)
                    dve.drain()
                    if j == 0:
                        nc.vector.tensor_scalar(x[:, u, j, :], x[:, u, j, :], HEAD ** -0.5, None, ALU.mult)
                        dve.drain()
                    dve.sem_inc(made, 1)

            steps(dve, QT, 2, body)
            dve.wait_ge(f_abs, 1)
            log1p(nc, dve, f[:, 3, :], f[:, 1, :], f[:, 4, :], f[:, 5, :])
            nc.vector.scalar_tensor_tensor(f[:, 5, :], f[:, 2, :], 0.0, f[:, 3, :], ALU.min, ALU.subtract)
            nc.vector.memset(f[:, 4, :], 1.0)
            dve.drain()
            nc.vector.tensor_tensor_scan(f[:, 3, :], f[:, 4, :], f[:, 5, :], 0.0, ALU.mult, ALU.add)
            dve.drain()
            nc.vector.tensor_scalar(f[:, 5, :], f[:, 3, :], -1.0, None, ALU.mult).then_inc(f_made, 1)


def attention(nc, consts, proj, at, out):
    KA = HEAD + 2
    NT = LAT_TILES
    with Stage(nc, "attn") as st:
        qk = st.sb("qk", [KA, 2, 2, SEQ])
        vf = st.sb("vf", [HEAD, 2, SEQ])
        v = st.sb("v", [P, NT, HEAD])
        p = st.sb("p", [P, 2, SEQ])
        pT = st.sb("pT", [P, NT, P])
        o = st.sb("o", [P, 2, NT, HEAD])
        after = st.sb("after", [P, P])
        stat = st.sb("stat", [P, 2, 3])
        ps = st.psum("ps", [P, 2, 2 * BANK])
        pt = st.psum("pt", [P, 2 * BANK])
        po = st.psum("po", [P, BANK])
        pv = st.psum("pv", [P, BANK])
        loaded = [st.sem(f"loaded{u}") for u in range(2)]
        stored = [st.sem(f"stored{u}") for u in range(2)]
        v_turned, v_made, logits, peak, p_made, p_turned, pT_made, o_ready, o_made = (
            st.sem(n) for n in ("v_turned", "v_made", "logits", "peak", "p_made", "p_turned", "pT_made", "o_ready", "o_made"))
        block = st.block()

        @block.sync
        def _(sp):
            def body(h, u, r):
                sp.wait_ge(o_made, (h + 1) * NT)
                for j, name in enumerate(("q", "k")):
                    sp.dma_start(qk[:, u, j, :], at[name][bass.ds(h, 1)].rearrange("o k t -> (o k) t")).then_inc(loaded[u], 16)
                sp.dma_start(vf[:, u, :], proj[bass.ds(h * HEAD + ROW2_V, HEAD), :]).then_inc(loaded[u], 16)

            steps(sp, HEADS, 2, body)

        @block.tensor
        def _(pe):
            def score(h, u, t):
                pe.wait_ge(p_made, h * NT + (t + 1))
                for a, n in chunks((t + 1) * P):
                    op = nc.tensor.matmul(ps[:, t % 2, a:a + n], qk[:, u, 0, t * P:(t + 1) * P], qk[:, u, 1, a:a + n],
                                          start=True, stop=True)
                op.then_inc(logits, 1)

            def body(h, u, r):
                pe.wait_ge(loaded[u], (r + 1) * 48)
                pe.wait_ge(v_made, h + 1)
                score(h, u, 0)
                for t in range(NT):
                    op = nc.tensor.transpose(pv[:, t * HEAD:(t + 1) * HEAD], vf[:, u, t * P:(t + 1) * P],
                                             consts["ident"][0:HEAD, 0:HEAD])
                op.then_inc(v_turned, 1)
                for t in range(NT):
                    if t + 1 < NT:
                        score(h, u, t + 1)
                    pe.wait_ge(p_made, h * NT + (t + 3))
                    pe.wait_ge(pT_made, h * NT + (t + 1))
                    for j in range(t + 1):
                        op = nc.tensor.transpose(pt[:, j * P:(j + 1) * P], p[:, t % 2, j * P:(j + 1) * P],
                                                 consts["ident"][:, :])
                    op.then_inc(p_turned, 1)
                    pe.wait_ge(pT_made, h * NT + (t + 2))
                    pe.wait_ge(o_made, h * NT + (t + 2 * NT))
                    if t == 0:
                        pe.wait_ge(v_made, h + 2)
                    for j in range(t + 1):
                        op = nc.tensor.matmul(po[:, 0:HEAD], pT[:, j, :], v[:, j, :], start=(j == 0), stop=(j == t))
                    op.then_inc(o_ready, 1)

            steps(pe, HEADS, 2, body)

        @block.scalar
        def _(act):
            act.sem_inc(p_made, 2)
            act.sem_inc(v_made, 1)
            act.sem_inc(pT_made, 1)
            for u in range(2):
                act.sem_inc(stored[u], 16)

            def body(h, u, r):
                act.wait_ge(v_turned, h + 1)
                nc.scalar.copy(v[:].rearrange("p t k -> p (t k)"), pv[:, :]).then_inc(v_made, 1)
                for t in range(NT):
                    act.wait_ge(peak, h * NT + (t + 1))
                    act.wait_ge(o_made, h * NT + (t + 2 * NT - 1))
                    act.wait_ge(p_turned, h * NT + (t + 1))
                    nc.scalar.activation(p[:, t % 2, 0:(t + 1) * P], ps[:, t % 2, 0:(t + 1) * P], ACT.Exp,
                                         bias=stat[:, t % 2, 0:1], accum_out=stat[:, t % 2, 1:2]).then_inc(p_made, 1)
                    act.wait_ge(p_turned, h * NT + (t + 3))
                    act.wait_ge(o_ready, h * NT + (t + 1))
                    nc.scalar.copy(pT[:, 0:t + 1, :].rearrange("p j t -> p (j t)"), pt[:, 0:(t + 1) * P])\
                        .then_inc(pT_made, 1)
                act.wait_ge(o_made, (h + 3) * NT)
                act.dma_start(out[:, bass.ds(h * HEAD, HEAD)].rearrange("(t p) k -> p t k", p=P), o[:, u])\
                    .then_inc(stored[u], 16)

            steps(act, HEADS, 2, body)
            for u in range(2):
                act.wait_ge(stored[u], 16 * (HEADS // 2 + 1))

        @block.vector
        def _(dve):
            nc.vector.tensor_tensor(after[:, :], consts["upto"][:, :], consts["ident"][:, :], ALU.subtract)
            dve.drain()
            nc.vector.tensor_scalar(after[:, :], after[:, :], -1e30, None, ALU.mult)
            dve.drain()
            dve.sem_inc(o_made, 2 * NT)

            def top(h, u, t):
                dve.wait_ge(logits, h * NT + (t + 1))
                diag = ps[:, t % 2, t * P:(t + 1) * P]
                nc.vector.tensor_tensor(diag, diag, after[:, :], ALU.add)
                dve.drain()
                nc.vector.tensor_reduce(stat[:, t % 2, 0:1], ps[:, t % 2, 0:(t + 1) * P], AX.X, ALU.max)
                dve.drain()
                nc.vector.tensor_scalar(stat[:, t % 2, 0:1], stat[:, t % 2, 0:1], -1.0, None, ALU.mult).then_inc(peak, 1)

            def body(h, u, r):
                dve.wait_ge(stored[u], (r + 1) * 16)
                top(h, u, 0)
                for t in range(NT):
                    if t + 1 < NT:
                        top(h, u, t + 1)
                    dve.wait_ge(o_ready, h * NT + (t + 2))
                    nc.vector.reciprocal(stat[:, t % 2, 2:3], stat[:, t % 2, 1:2])
                    dve.drain()
                    nc.vector.tensor_scalar(o[:, u, t, :], po[:, 0:HEAD], stat[:, t % 2, 2:3], None, ALU.mult)\
                        .then_inc(o_made, 1)

            steps(dve, HEADS, 2, body)

        @block.gpsimd
        def _(pool):
            pool.sem_inc(p_turned, 2)
            pool.sem_inc(o_ready, 1)


def gated_columns(nc, consts, src, gate, out):
    with Stage(nc, "gated") as st:
        o = st.sb("o", [P, 2, WID])
        g = st.sb("g", [P, 2, QT, P])
        res = st.sb("res", [P, 2, QT, P])
        pt = st.psum("pt", [P, 2, BANK])
        loaded = [st.sem(f"loaded{u}") for u in range(2)]
        stored = [st.sem(f"stored{u}") for u in range(2)]
        turned, silu_made, made = st.sem("turned"), st.sem("silu_made"), st.sem("made")
        block = st.block()

        @block.sync
        def _(sp):
            def body(i, u, r):
                sp.wait_ge(made, i + 1)
                sp.dma_start(o[:, u, :], src[bass.ds(i * P, P), :]).then_inc(loaded[u], 16)
                sp.dma_start(g[:, u], gate[:, bass.ds(i * P, P)].rearrange("(j p) t -> p j t", p=P)).then_inc(loaded[u], 16)

            steps(sp, LAT_TILES, 2, body)

        @block.tensor
        def _(pe):
            def body(i, u, r):
                pe.wait_ge(loaded[u], (r + 1) * 32)
                pe.wait_ge(made, i + 1)
                for j in range(QT):
                    op = nc.tensor.transpose(pt[:, u, j * P:(j + 1) * P], o[:, u, j * P:(j + 1) * P], consts["ident"][:, :])
                op.then_inc(turned, 1)

            steps(pe, LAT_TILES, 2, body)

        @block.scalar
        def _(act):
            for u in range(2):
                act.sem_inc(stored[u], 16)

            def body(i, u, r):
                act.wait_ge(loaded[u], (r + 1) * 32)
                nc.scalar.activation(g[:, u], g[:, u], ACT.Silu).then_inc(silu_made, 1)
                act.wait_ge(made, i + 3)
                act.dma_start(out[:, bass.ds(i * P, P)].rearrange("(j p) t -> p j t", p=P), res[:, u]).then_inc(stored[u], 16)

            steps(act, LAT_TILES, 2, body)
            for u in range(2):
                act.wait_ge(stored[u], 16 * (LAT_TILES // 2 + 1))

        @block.vector
        def _(dve):
            dve.sem_inc(made, 2)

            def body(i, u, r):
                dve.wait_ge(turned, i + 1)
                dve.wait_ge(silu_made, i + 1)
                dve.wait_ge(stored[u], (r + 1) * 16)
                nc.vector.tensor_tensor(res[:, u].rearrange("p j t -> p (j t)"), pt[:, u, :],
                                        g[:, u].rearrange("p j t -> p (j t)"), ALU.mult).then_inc(made, 1)

            steps(dve, LAT_TILES, 2, body)


def causal_conv(nc, dve, out, x, taps, bias):
    nc.vector.tensor_scalar(out, x, taps[:, CONV_WIDTH - 1:CONV_WIDTH], bias, ALU.mult, ALU.add)
    for j in range(1, CONV_WIDTH):
        dve.drain()
        nc.vector.scalar_tensor_tensor(out[:, j:], x[:, :SEQ - j], taps[:, CONV_WIDTH - 1 - j:CONV_WIDTH - j],
                                       out[:, j:], ALU.mult, ALU.add)


def ssd_prepare(nc, proj, par, sd):
    with Stage(nc, "ssdprep") as st:
        x = st.sb("x", [P, 2, SEQ])
        y = st.sb("y", [P, 2, SEQ])
        taps = st.sb("taps", [P, 2, CONV_WIDTH])
        bias = st.sb("bias", [P, 2, 1])
        t = st.sb("t", [SSD_HEADS, 6, SEQ])
        hp = st.sb("hp", [SSD_HEADS, 4])
        once, conv_made, silu_made, t_abs, t_made, t_sent = (st.sem(n) for n in (
            "once", "conv_made", "silu_made", "t_abs", "t_made", "t_sent"))
        loaded = [st.sem(f"loaded{u}") for u in range(2)]
        stored = [st.sem(f"stored{u}") for u in range(2)]
        n = SSD_CONV // P
        block = st.block()

        @block.sync
        def _(sp):
            sp.dma_start(t[:, 0, :], proj[ROW2_DT:ROW2_DT + SSD_HEADS, :]).then_inc(once, 16)
            for j, name in enumerate(("dt_bias", "a_log")):
                sp.dma_start(hp[:, j:j + 1], par[name].rearrange("(p o) -> p o", o=1)).then_inc(once, 16)

            def body(i, u, r):
                sp.wait_ge(conv_made, i + 1)
                at = bass.ds(i * P, P)
                sp.dma_start(x[:, u, :], proj[bass.ds(i * P + ROW2_XBC, P), :]).then_inc(loaded[u], 16)
                sp.dma_start(taps[:, u, :], par["conv_w"][:, at].rearrange("t p -> p t")).then_inc(loaded[u], 16)
                sp.dma_start(bias[:, u, :], par["conv_b"][at].rearrange("(p o) -> p o", o=1)).then_inc(loaded[u], 16)

            steps(sp, n, 2, body)

        @block.scalar
        def _(act):
            act.wait_ge(once, 48)
            nc.scalar.activation(t[:, 1, :], t[:, 0, :], ACT.Abs, bias=hp[:, 0:1])
            nc.scalar.activation(t[:, 2, :], t[:, 0, :], ACT.Identity, bias=hp[:, 0:1])
            act.drain()
            nc.scalar.activation(t[:, 1, :], t[:, 1, :], ACT.Exp, scale=-1.0)
            nc.scalar.activation(hp[:, 2:3], hp[:, 1:2], ACT.Exp).then_inc(t_abs, 1)
            for u in range(2):
                act.sem_inc(stored[u], 16)

            def body(i, u, r):
                act.wait_ge(conv_made, i + 3)
                nc.scalar.activation(y[:, u, :], y[:, u, :], ACT.Silu).then_inc(silu_made, 1)
                act.wait_ge(silu_made, i + 1)
                act.dma_start(sd["xbc"][bass.ds(i * P, P), :], y[:, u, :]).then_inc(stored[u], 16)

            steps(act, n, 2, body)
            act.wait_ge(t_made, 1)
            act.dma_start(sd["dt"], t[:, 3, :]).then_inc(t_sent, 16)
            act.dma_start(sd["acs"], t[:, 2, :]).then_inc(t_sent, 16)
            act.wait_ge(t_sent, 32)
            for u in range(2):
                act.wait_ge(stored[u], 16 * (n // 2 + 1))

        @block.vector
        def _(dve):
            dve.sem_inc(conv_made, 2)

            def body(i, u, r):
                dve.wait_ge(loaded[u], (r + 1) * 48)
                dve.wait_ge(stored[u], (r + 1) * 16)
                causal_conv(nc, dve, y[:, u, :], x[:, u, :], taps[:, u, :], bias[:, u, :])
                dve.drain()
                dve.sem_inc(conv_made, 1)

            steps(dve, n, 2, body)
            dve.wait_ge(t_abs, 1)
            log1p(nc, dve, t[:, 3, :], t[:, 1, :], t[:, 4, :], t[:, 5, :])
            nc.vector.scalar_tensor_tensor(t[:, 3, :], t[:, 2, :], 0.0, t[:, 3, :], ALU.max, ALU.add)
            nc.vector.memset(t[:, 5, :], 1.0)
            dve.drain()
            nc.vector.memset(t[:, 5, :].rearrange("p (c t) -> p c t", t=P)[:, :, 0:1], 0.0)
            nc.vector.tensor_scalar(t[:, 4, :], t[:, 3, :], hp[:, 2:3], -1.0, ALU.mult, ALU.mult)
            dve.drain()
            nc.vector.tensor_tensor_scan(t[:, 2, :], t[:, 5, :], t[:, 4, :], 0.0, ALU.mult, ALU.add).then_inc(t_made, 1)


def ssd_scan(nc, consts, proj, par, sd, mix):
    XT, G, HG = SSD_WIDTH // P, SSD_GROUPS, SSD_HEADS // SSD_GROUPS
    with Stage(nc, "ssd") as st:
        xf = st.sb("xf", [P, 2, XT, P])
        zf = st.sb("zf", [P, 2, XT, P])
        bc = st.sb("bc", [P, 2, 2, G, P])
        row = st.sb("row", [P, 2, SSD_HEADS, P])
        da = st.sb("da", [SSD_HEADS, 2, 2, P])
        dskip = st.sb("dskip", [P, SSD_HEADS])
        ng = st.sb("ng", [P, XT])
        x = st.sb("x", [P, SSD_WIDTH])
        z = st.sb("z", [P, SSD_WIDTH])
        bT = st.sb("bT", [P, G, P])
        col = st.sb("col", [P, 6, SSD_HEADS])
        xdt = st.sb("xdt", [P, SSD_WIDTH])
        xdd = st.sb("xdd", [P, SSD_WIDTH])
        cb = st.sb("cb", [P, G, P])
        L = st.sb("L", [P, SSD_HEADS, P])
        s = st.sb("s", [P, SSD_WIDTH])
        y = st.sb("y", [P, SSD_WIDTH])
        t1 = st.sb("t1", [P, SSD_WIDTH])
        stat = st.sb("stat", [P, 4, G])
        res = st.sb("res", [P, 2, XT, P])
        pa = st.psum("pa", [P, 2 * BANK])
        pb = st.psum("pb", [P, 2 * BANK])
        pc = st.psum("pc", [P, BANK])
        pd = st.psum("pd", [P, BANK])
        pe_s = st.psum("pe_s", [P, 2 * BANK])
        names = ("once", "z_silu", "turned", "x_made", "z_made", "small_made", "seg_made", "exp_made", "L_made", "M_made",
                 "xdt_made", "xdd_made", "diag_ready", "off_ready", "s_ready", "s_made", "var_made", "root_made", "y_made",
                 "y_turned", "res_made", "cb_made")
        (once, z_silu, turned, x_made, z_made, small_made, seg_made, exp_made, L_made, M_made, xdt_made, xdd_made,
         diag_ready, off_ready, s_ready, s_made, var_made, root_made, y_made, y_turned, res_made, cb_made) = (
            st.sem(n) for n in names)
        loaded = [st.sem(f"loaded{u}") for u in range(2)]
        stored = [st.sem(f"stored{u}") for u in range(2)]
        LOADS = 2 + 2 + 1 + 2
        block = st.block()

        def heads(ap):
            return ap.rearrange("p (h k) -> p h k", k=HEAD)

        @block.sync
        def _(sp):
            sp.dma_start(dskip[:, :], par["d"].rearrange("(o e) -> o e", o=1).broadcast_to([P, SSD_HEADS])).then_inc(once, 16)
            sp.dma_start(ng[:, :], column(par["norm_g"])).then_inc(once, 16)

            def body(i, u, r):
                tk = bass.ds(i * P, P)
                sp.wait_ge(y_made, i + 1)
                sp.dma_start(xf[:, u], sd["xbc"][0:SSD_WIDTH, tk].rearrange("(j p) t -> p j t", p=P)).then_inc(loaded[u], 16)
                for j in range(2):
                    a = SSD_WIDTH + j * G * SSD_STATE
                    sp.dma_start(bc[:, u, j], sd["xbc"][a:a + G * SSD_STATE, tk].rearrange("(g n) t -> n g t", n=P))\
                        .then_inc(loaded[u], 16)
                sp.dma_start(zf[:, u], proj[ROW2_ZS:ROW2_ZS + SSD_WIDTH, tk].rearrange("(j p) t -> p j t", p=P))\
                    .then_inc(loaded[u], 16)
                sp.dma_start(row[:, u], sd["acs"][:, tk].rearrange("(o h) t -> o h t", o=1).broadcast_to([P, SSD_HEADS, P]))\
                    .then_inc(loaded[u], 16)
                sp.dma_start(da[:, u, 0, :], sd["dt"][:, tk]).then_inc(loaded[u], 16)
                sp.dma_start(da[:, u, 1, :], sd["acs"][:, tk]).then_inc(loaded[u], 16)

            steps(sp, SSD_CHUNKS, 2, body)

        @block.tensor
        def _(pe):
            def body(i, u, r):
                ident = consts["ident"]
                pe.wait_ge(loaded[u], (r + 1) * (16 * LOADS))
                pe.wait_ge(res_made, i + 1)
                for j in range(XT):
                    op = nc.tensor.transpose(pa[:, j * P:(j + 1) * P], xf[:, u, j, :], ident[:, :])
                op.then_inc(turned, 1)
                for j in range(2):
                    nc.tensor.transpose(pc[:, 2 * P + 16 * j:2 * P + 16 * (j + 1)], da[:, u, j, :], ident[0:16, 0:16])
                for g in range(G):
                    op = nc.tensor.transpose(pc[:, g * P:(g + 1) * P], bc[:, u, 0, g, :], ident[:, :])
                op.then_inc(turned, 1)
                for g in range(G):
                    op = nc.tensor.matmul(pd[:, g * P:(g + 1) * P], bc[:, u, 0, g, :], bc[:, u, 1, g, :],
                                          start=True, stop=True)
                op.then_inc(turned, 1)
                pe.wait_ge(z_silu, i + 1)
                pe.wait_ge(y_made, i + 2)
                for j in range(XT):
                    op = nc.tensor.transpose(pb[:, j * P:(j + 1) * P], zf[:, u, j, :], ident[:, :])
                op.then_inc(turned, 1)
                pe.wait_ge(z_made, i + 1)
                pe.wait_ge(s_made, i + 1)
                for g in range(G):
                    op = nc.tensor.matmul(pb[:, g * BANK:(g + 1) * BANK], bc[:, u, 1, g, :], s[:, g * BANK:(g + 1) * BANK],
                                          start=True, stop=True)
                op.then_inc(off_ready, 1)
                pe.wait_ge(xdd_made, i + 1)
                for g in range(G):
                    op = nc.tensor.matmul(pe_s[:, g * BANK:(g + 1) * BANK], bT[:, g, :], xdd[:, g * BANK:(g + 1) * BANK],
                                          start=True, stop=True)
                op.then_inc(s_ready, 1)
                pe.wait_ge(M_made, i + 1)
                pe.wait_ge(xdt_made, i + 1)
                for h in range(SSD_HEADS):
                    op = nc.tensor.matmul(pa[:, h * HEAD:(h + 1) * HEAD], L[:, h, :], xdt[:, h * HEAD:(h + 1) * HEAD],
                                          start=True, stop=True)
                op.then_inc(diag_ready, 1)
                pe.wait_ge(y_made, i + 3)
                for j in range(XT):
                    op = nc.tensor.transpose(pa[:, j * P:(j + 1) * P], y[:, j * P:(j + 1) * P], ident[:, :])
                op.then_inc(y_turned, 1)

            steps(pe, SSD_CHUNKS, 2, body)

        @block.scalar
        def _(act):
            act.wait_ge(once, 32)
            act.sem_inc(res_made, 1)
            for u in range(2):
                act.sem_inc(stored[u], 16)

            def body(i, u, r):
                act.wait_ge(loaded[u], (r + 1) * (16 * LOADS))
                nc.scalar.activation(zf[:, u], zf[:, u], ACT.Silu).then_inc(z_silu, 1)
                act.wait_ge(y_made, i + 2)
                act.wait_ge(turned, i * 4 + 1)
                nc.scalar.copy(x[:, :], pa[:, :]).then_inc(x_made, 1)
                act.wait_ge(turned, i * 4 + 2)
                act.wait_ge(s_made, i + 1)
                nc.scalar.copy(col[:, 0:2, :].rearrange("p j h -> p (j h)"), pc[:, 2 * P:2 * P + 32])
                nc.scalar.copy(bT[:].rearrange("p g t -> p (g t)"), pc[:, 0:2 * P]).then_inc(small_made, 1)
                act.wait_ge(turned, i * 4 + 4)
                nc.scalar.copy(z[:, :], pb[:, :]).then_inc(z_made, 1)
                act.wait_ge(seg_made, i * 2 + 1)
                nc.scalar.activation(col[:, 2, :], col[:, 1, :], ACT.Exp)
                nc.scalar.activation(col[:, 4, :], col[:, 3, :], ACT.Exp)
                nc.scalar.activation(col[:, 5, :], row[:, u, :, P - 1], ACT.Exp).then_inc(exp_made, 1)
                act.wait_ge(seg_made, i * 2 + 2)
                nc.scalar.activation(L[:], L[:], ACT.Exp).then_inc(L_made, 1)
                act.wait_ge(var_made, i + 1)
                nc.scalar.activation(stat[:, 2, :], stat[:, 1, :], ACT.Sqrt).then_inc(root_made, 1)
                act.wait_ge(y_turned, i + 1)
                act.wait_ge(stored[u], (r + 1) * 16)
                for j in range(XT):
                    op = nc.scalar.activation(res[:, u, j, :], pa[:, j * P:(j + 1) * P], ACT.Identity,
                                              scale=ng[:, j:j + 1])
                op.then_inc(res_made, 1)
                act.wait_ge(res_made, i + 2)
                act.dma_start(mix[WID:WID + SSD_WIDTH, bass.ds(i * P, P)].rearrange("(j p) t -> p j t", p=P), res[:, u])\
                    .then_inc(stored[u], 16)

            steps(act, SSD_CHUNKS, 2, body)
            for u in range(2):
                act.wait_ge(stored[u], 16 * (SSD_CHUNKS // 2 + 1))

        @block.gpsimd
        def _(pool):
            def body(i, u, r):
                pool.wait_ge(L_made, i + 1)
                pool.wait_ge(cb_made, i + 1)
                for g in range(G):
                    part = L[:, g * HG:(g + 1) * HG, :]
                    op = nc.gpsimd.tensor_tensor(part, part, over(cb[:, g, :], HG), ALU.mult)
                op.then_inc(M_made, 1)

            steps(pool, SSD_CHUNKS, 2, body)

        @block.vector
        def _(dve):
            dve.wait_ge(once, 32)
            nc.vector.memset(s[:, :], 0.0)
            dve.drain()
            dve.sem_inc(s_made, 1)
            dve.sem_inc(y_made, 2)

            def body(i, u, r):
                dve.wait_ge(small_made, i + 1)
                last = row[:, u, :, P - 1]
                nc.vector.tensor_tensor(col[:, 3, :], last, col[:, 1, :], ALU.subtract).then_inc(seg_made, 1)
                for h in range(SSD_HEADS):
                    op = nc.vector.tensor_scalar(L[:, h, :], row[:, u, h, :], col[:, 1, h:h + 1], 0.0, ALU.subtract, ALU.min)
                op.then_inc(seg_made, 1)
                dve.wait_ge(turned, i * 4 + 3)
                nc.vector.tensor_tensor(cb[:], pd[:, 0:2 * P].rearrange("p (g t) -> p g t", g=G), over(consts["upto"][:, :], G),
                                        ALU.mult).then_inc(cb_made, 1)
                dve.wait_ge(x_made, i + 1)
                nc.vector.tensor_tensor(heads(xdt[:, :]), heads(x[:, :]), last_of(col[:, 0, :], HEAD), ALU.mult)\
                    .then_inc(xdt_made, 1)
                nc.vector.tensor_tensor(heads(y[:, :]), heads(x[:, :]), last_of(dskip[:, :], HEAD), ALU.mult)
                dve.drain()
                dve.wait_ge(exp_made, i + 1)
                nc.vector.tensor_tensor(heads(xdd[:, :]), heads(xdt[:, :]), last_of(col[:, 4, :], HEAD), ALU.mult)\
                    .then_inc(xdd_made, 1)
                dve.wait_ge(off_ready, i + 1)
                nc.vector.tensor_tensor(heads(t1[:, :]), heads(pb[:, :]), last_of(col[:, 2, :], HEAD), ALU.mult)
                nc.vector.tensor_tensor(heads(s[:, :]), heads(s[:, :]), last_of(col[:, 5, :], HEAD), ALU.mult)
                dve.drain()
                nc.vector.tensor_tensor(y[:, :], y[:, :], t1[:, :], ALU.add)
                dve.wait_ge(s_ready, i + 1)
                nc.vector.tensor_tensor(s[:, :], s[:, :], pe_s[:, :], ALU.add).then_inc(s_made, 1)
                dve.drain()
                dve.wait_ge(diag_ready, i + 1)
                nc.vector.tensor_tensor(y[:, :], y[:, :], pa[:, :], ALU.add)
                dve.drain()
                dve.wait_ge(z_made, i + 1)
                nc.vector.tensor_tensor(y[:, :], y[:, :], z[:, :], ALU.mult)
                dve.drain()
                nc.vector.tensor_tensor(t1[:, :], y[:, :], y[:, :], ALU.mult)
                dve.drain()
                nc.vector.tensor_reduce(stat[:, 0, :], t1[:, :].rearrange("p (g n) -> p g n", g=G), AX.X, ALU.add)
                dve.drain()
                nc.vector.tensor_scalar(stat[:, 1, :], stat[:, 0, :], float(G) / SSD_WIDTH, EPS, ALU.mult, ALU.add)\
                    .then_inc(var_made, 1)
                dve.wait_ge(root_made, i + 1)
                nc.vector.reciprocal(stat[:, 3, :], stat[:, 2, :])
                dve.drain()
                v = y[:, :].rearrange("p (g n) -> p g n", g=G)
                nc.vector.tensor_tensor(v, v, last_of(stat[:, 3, :], SSD_WIDTH // G), ALU.mult).then_inc(y_made, 1)

            steps(dve, SSD_CHUNKS, 2, body)


def rglru(nc, proj, par, mix):
    with Stage(nc, "lru") as st:
        x = st.sb("x", [P, SEQ])
        z = st.sb("z", [P, SEQ])
        xc = st.sb("xc", [P, SEQ])
        gi = st.sb("gi", [P, SEQ])
        th = st.sb("th", [P, SEQ])
        inv = st.sb("inv", [P, SEQ])
        root = st.sb("root", [P, SEQ])
        a = st.sb("a", [P, SEQ])
        h = st.sb("h", [P, SEQ])
        taps = st.sb("taps", [P, CONV_WIDTH])
        cols = st.sb("cols", [P, 3])
        w = st.sb("w", [P, 2, P])
        lam = st.sb("lam", [P, 6, QT])
        ps = st.psum("ps", [P, 4, BANK])
        once, loaded, conv_made, lam_abs, gates_ready, i_made, th_made, root_made, z_made, sent, used = (
            st.sem(n) for n in ("once", "loaded", "conv_made", "lam_abs", "gates_ready", "i_made", "th_made", "root_made",
                                "z_made", "sent", "used"))
        w_zero, lam_made = st.sem("w_zero"), st.sem("lam_made")
        block = st.block()
        LOADS = 2 + 1 + 3 + 4

        @block.sync
        def _(sp):
            sp.dma_start(lam[:, 0, :], column(par["lam"])).then_inc(once, 16)
            sp.wait_ge(w_zero, 1)

            for i in range(QT):
                at = slice(i * P, (i + 1) * P)
                if i:
                    sp.wait_ge(used, i)
                sp.dma_start(x[:, :], proj[ROW2_XL + i * P:ROW2_XL + (i + 1) * P, :]).then_inc(loaded, 16)
                sp.dma_start(z[:, :], proj[ROW2_ZL + i * P:ROW2_ZL + (i + 1) * P, :]).then_inc(loaded, 16)
                sp.dma_start(taps[:, :], par["conv_w"][:, at].rearrange("t p -> p t")).then_inc(loaded, 16)
                for j, name in enumerate(("conv_b", "b_a", "b_x")):
                    sp.dma_start(cols[:, j:j + 1], par[name][at].rearrange("(p o) -> p o", o=1)).then_inc(loaded, 16)
                for j, name in enumerate(("w_a", "w_x")):
                    for b in range(2):
                        sp.dma_start(w[b * HEAD:(b + 1) * HEAD, j, b * HEAD:(b + 1) * HEAD], par[name][2 * i + b])\
                            .then_inc(loaded, 16)

        @block.gpsimd
        def _(pool):
            nc.gpsimd.memset(w[:], 0.0).then_inc(w_zero, 1)

        @block.tensor
        def _(pe):
            for i in range(QT):
                pe.wait_ge(conv_made, i + 1)
                if i:
                    pe.wait_ge(i_made, i)
                    pe.wait_ge(th_made, 2 * i)
                for j in range(2):
                    for c, (at, n) in enumerate(chunks(SEQ)):
                        op = nc.tensor.matmul(ps[:, 2 * j + c, :], w[:, j, :], xc[:, at:at + n], start=True, stop=True)
                op.then_inc(gates_ready, 1)

        @block.scalar
        def _(act):
            act.wait_ge(once, 16)
            nc.scalar.activation(lam[:, 1, :], lam[:, 0, :], ACT.Abs)
            act.drain()
            nc.scalar.activation(lam[:, 1, :], lam[:, 1, :], ACT.Exp, scale=-1.0).then_inc(lam_abs, 1)
            act.wait_ge(lam_made, 1)
            for i in range(QT):
                act.wait_ge(gates_ready, i + 1)
                nc.scalar.activation(gi[:, :], ps[:, 2:4, :].rearrange("p b n -> p (b n)"), ACT.Sigmoid, bias=cols[:, 2:3])\
                    .then_inc(i_made, 1)
                nc.scalar.activation(th[:, :], ps[:, 0:2, :].rearrange("p b n -> p (b n)"), ACT.Sigmoid, bias=cols[:, 1:2])\
                    .then_inc(th_made, 1)
                act.drain()
                nc.scalar.activation(th[:, :], th[:, :], ACT.Tanh, scale=lam[:, 5, i:i + 1]).then_inc(th_made, 1)
                act.drain()
                nc.scalar.activation(root[:, :], th[:, :], ACT.Sqrt).then_inc(root_made, 1)
                nc.scalar.activation(z[:, :], z[:, :], ACT.Silu).then_inc(z_made, 1)
                act.wait_ge(used, i + 1)
                act.dma_start(mix[WID + SSD_WIDTH + i * P:WID + SSD_WIDTH + (i + 1) * P, :], h[:, :]).then_inc(sent, 16)
            act.wait_ge(sent, 16 * QT)

        @block.vector
        def _(dve):
            dve.wait_ge(lam_abs, 1)
            log1p(nc, dve, lam[:, 2, :], lam[:, 1, :], lam[:, 3, :], lam[:, 4, :])
            nc.vector.tensor_scalar(lam[:, 3, :], lam[:, 0, :], -1.0, 0.0, ALU.mult, ALU.max)
            dve.drain()
            nc.vector.tensor_tensor(lam[:, 4, :], lam[:, 3, :], lam[:, 2, :], ALU.add)
            dve.drain()
            nc.vector.tensor_scalar(lam[:, 5, :], lam[:, 4, :], 4.0, None, ALU.mult).then_inc(lam_made, 1)
            for i in range(QT):
                dve.wait_ge(loaded, (i + 1) * (16 * LOADS))
                causal_conv(nc, dve, xc[:, :], x[:, :], taps[:, :], cols[:, 0:1])
                dve.drain()
                dve.sem_inc(conv_made, 1)
                dve.wait_ge(th_made, 2 * i + 2)
                nc.vector.tensor_scalar(inv[:, :], th[:, :], 1.0, None, ALU.add)
                dve.drain()
                nc.vector.reciprocal(inv[:, :], inv[:, :])
                nc.vector.tensor_scalar(a[:, :], th[:, :], -1.0, 1.0, ALU.mult, ALU.add)
                dve.drain()
                nc.vector.tensor_tensor(a[:, :], a[:, :], inv[:, :], ALU.mult)
                dve.wait_ge(root_made, i + 1)
                nc.vector.scalar_tensor_tensor(root[:, :], root[:, :], 2.0, inv[:, :], ALU.mult, ALU.mult)
                dve.drain()
                nc.vector.memset(root[:, 0:1], 1.0)
                dve.wait_ge(i_made, i + 1)
                nc.vector.tensor_tensor(gi[:, :], gi[:, :], xc[:, :], ALU.mult)
                dve.drain()
                nc.vector.tensor_tensor(gi[:, :], gi[:, :], root[:, :], ALU.mult)
                dve.drain()
                if i:
                    dve.wait_ge(sent, 16 * i)
                nc.vector.tensor_tensor_scan(h[:, :], a[:, :], gi[:, :], 0.0, ALU.mult, ALU.add)
                dve.drain()
                dve.wait_ge(z_made, i + 1)
                nc.vector.tensor_tensor(h[:, :], h[:, :], z[:, :], ALU.mult).then_inc(used, 1)


def second_block(nc, consts, i, s, out):
    h, proj, mix = s["h"], s["proj2"], s["mix2"]
    with nc.sbuf_tensor("uT", [P, KD, SEQ], F32) as uT:
        plain_norm(nc, consts, "norm3", h, i["norm_g_2"][0], uT)
        linear_columns(nc, "proj2", i["w_in_2"][0], uT, SEQ, proj)
    second_mix(nc, consts, i, s)
    linear_tokens(nc, "out2", mix, i["w_out_2"][0], h, out[0])


def second_mix(nc, consts, i, s):
    proj, mix = s["proj2"], s["mix2"]
    attention_prepare(nc, consts, proj, {"q_g": i["q_norm_g_2"][0], "k_g": i["k_norm_g_2"][0], "f_b": i["forget_b_2"][0]},
                      s["at"])
    attention(nc, consts, proj, s["at"], s["att"])
    gated_columns(nc, consts, s["att"], proj[ROW2_ZA:ROW2_ZA + WID, :], mix[0:WID, :])
    ssd_prepare(nc, proj, {"conv_w": i["ssd_conv_w_2"][0], "conv_b": i["ssd_conv_b_2"][0],
                           "dt_bias": i["ssd_dt_bias_2"][0], "a_log": i["ssd_a_log_2"][0]}, s["sd"])
    ssd_scan(nc, consts, proj, {"d": i["ssd_d_2"][0], "norm_g": i["ssd_norm_g_2"][0]}, s["sd"], mix)
    rglru(nc, proj, {"conv_w": i["lru_conv_w_2"][0], "conv_b": i["lru_conv_b_2"][0], "w_a": i["lru_w_a_2"][0],
                     "b_a": i["lru_b_a_2"][0], "w_x": i["lru_w_x_2"][0], "b_x": i["lru_b_x_2"][0],
                     "lam": i["lru_lambda_2"][0]}, mix)


def two_blocks(nc, i, out):
    def dram(name, shape):
        return nc.dram_tensor(name, shape, F32, kind="Internal").ap()

    rw = {n: dram("rw_" + n, (2, WID, TOK)) for n in ("a", "r", "b", "k", "bh", "kh")}
    rw["tot"] = dram("rw_tot", (2, WID, RW_CHUNKS))
    rw["v"] = dram("rw_v", (WID, TOK))
    rw["bonus"] = dram("rw_bonus", (WID, SEQ))
    rw["gate"] = dram("rw_gate", (WID, SEQ))
    rw["q_out"] = dram("rw_q_out", (2, TILES, 2, HEAD, 4, P))
    rw["y_out"] = dram("rw_y_out", (2, TILES, 2, P, 4, HEAD))
    rw["m_out"] = dram("rw_m_out", (2, TILES, 2, HEAD, 8, HEAD))
    rw["n_out"] = dram("rw_n_out", (2, TILES, 2, HEAD, 8, HEAD))
    rw["s"] = dram("rw_s", (2, TILES, HEAD, 2, HEADS, HEAD))
    hg = {n: dram("hg_" + n, (2, WID, TOK)) for n in ("qs", "ks", "qc", "kh")}
    hg["tot"] = dram("hg_tot", (2, WID, HG_CHUNKS))
    hg["o"] = dram("hg_o", (2, SEQ, WID))
    s = {
        "mods": dram("mods", (2, N_MOD * D)), "proj": dram("proj", (P_IN, TOK)), "mix": dram("mix", (D, SEQ)),
        "x1": dram("x1", (SEQ, D)), "h": dram("h", (SEQ, D)), "rw": rw, "hg": hg,
        "proj2": dram("proj2", (D_IN, SEQ)), "mix2": dram("mix2", (MIX2, SEQ)), "att": dram("att", (SEQ, WID)),
        "at": {n: dram("at_" + n, (HEADS, HEAD + 2, SEQ)) for n in ("q", "k")},
        "sd": {"xbc": dram("sd_xbc", (SSD_CONV, SEQ)), "dt": dram("sd_dt", (SSD_HEADS, SEQ)),
               "acs": dram("sd_acs", (SSD_HEADS, SEQ))},
    }
    with ExitStack() as ctx:
        consts = build_constants(nc, ctx)
        first_block(nc, consts, i, s)
        second_block(nc, consts, i, s, out)


_INS = ["x", "c", "ctx", "c_ctx", "w_mod", "b_mod", "norm1_g", "norm2_g", "w_in", "rw_conv", "rw_w0", "rw_w2", "rw_a0",
        "rw_a2", "rw_g2", "rw_k_k", "rw_k_a", "rw_r_k", "rw_lnx_g", "rw_lnx_b", "hg_lb_logits", "hg_norm_g", "w_out",
        "router_w", "router_b", "exp_w_gate", "exp_w_up", "exp_w_down", "sh_w_gate", "sh_w_up", "sh_w_down",
        "final_norm_g", "norm_g_2", "w_in_2", "q_norm_g_2", "k_norm_g_2", "forget_b_2", "ssd_conv_w_2", "ssd_conv_b_2",
        "ssd_dt_bias_2", "ssd_a_log_2", "ssd_d_2", "ssd_norm_g_2", "lru_conv_w_2", "lru_conv_b_2", "lru_w_a_2",
        "lru_b_a_2", "lru_w_x_2", "lru_b_x_2", "lru_lambda_2", "w_out_2"]
_OUTS = [((1, SEQ, D), "float32")]


def kernel(**inputs):
    import numpy as _np
    import concourse.bacc as _bacc
    from concourse import mybir as _mybir
    from concourse.bass_utils import run_bass_kernel_spmd as _run

    nc = _bacc.Bacc("TRN2", target_bir_lowering=False, num_devices=1)
    arrays, args = {}, {}
    for name in _INS:
        a = _np.ascontiguousarray(inputs[name])
        arrays[f"in_{name}_dram"] = a
        args[name] = nc.dram_tensor(f"in_{name}_dram", a.shape, _mybir.dt.from_np(a.dtype), kind="ExternalInput").ap()
    shape, dtype = _OUTS[0]
    out = nc.dram_tensor("out_0_dram", shape, _mybir.dt.from_np(_np.dtype(dtype)), kind="ExternalOutput").ap()
    two_blocks(nc, args, out)
    r = _run(nc, [arrays], core_ids=[0])
    return r.results[0]["out_0_dram"]
```

```python
from contextlib import ExitStack

import concourse.bass as bass
from concourse import mybir
import numpy as np

F32 = mybir.dt.float32
F32R = mybir.dt.float32r
I32 = mybir.dt.int32
U32 = mybir.dt.uint32
ALU = mybir.AluOpType
ACT = mybir.ActivationFunctionType
AX = mybir.AxisListType
P = 128
BANK = 512

D = 1024
KD = D // P
SEQ = 1024
CTX = 256
TOK = CTX + SEQ
GRID_W = 64
GRID_H = SEQ // GRID_W
HEAD = 64
HEADS = 8
WID = HEADS * HEAD
QT = WID // P
EPS = 1e-6
RW_GN_EPS = 1e-5 * HEAD
RW_CHUNK = 64
RW_CHUNKS = TOK // RW_CHUNK
HG_CHUNK = 32
HG_CHUNKS = TOK // HG_CHUNK
TILES = TOK // P
LAT_TILES = SEQ // P
CTX_TILES = CTX // P
N_MOD = 6
P_IN = 3 * WID + 3 * P + 5 * WID
ROW_R, ROW_K, ROW_V = 0, WID, 2 * WID
ROW_WD, ROW_AD, ROW_GD = 3 * WID, 3 * WID + P, 3 * WID + 2 * P
ROW_Q = 3 * WID + 3 * P
ROW_FF, ROW_FB, ROW_I, ROW_G = ROW_Q + WID, ROW_Q + 2 * WID, ROW_Q + 3 * WID, ROW_Q + 4 * WID

N_EXPERTS = 64
N_GROUPS = 8
TOPK_GROUPS = 4
TOP_K = 8
D_EXPERT = 256
ROUTE_SCALE = 2.5

SSD_HEADS = 16
SSD_WIDTH = SSD_HEADS * HEAD
SSD_GROUPS = 2
SSD_STATE = 128
SSD_CONV = SSD_WIDTH + 2 * SSD_GROUPS * SSD_STATE
SSD_CHUNKS = SEQ // P
CONV_WIDTH = 4
MIX2 = 2 * D
ROW2_Q, ROW2_K, ROW2_V, ROW2_ZA, ROW2_F = 0, WID, 2 * WID, 3 * WID, 4 * WID
ROW2_ZS = ROW2_F + HEADS
ROW2_XBC = ROW2_ZS + SSD_WIDTH
ROW2_DT = ROW2_XBC + SSD_CONV
ROW2_XL = ROW2_DT + SSD_HEADS
ROW2_ZL = ROW2_XL + WID
D_IN = ROW2_ZL + WID


def chunks(n, size=BANK):
    return [(a, min(size, n - a)) for a in range(0, n, size)]


def steps(eng, n, unroll, body):
    if n >= 2 * unroll:
        with eng.Fori(0, n // unroll) as i:
            for u in range(unroll):
                body(i * unroll + u, u, i)
        done = n // unroll * unroll
    else:
        done = 0
    for s in range(done, n):
        body(s, s % unroll, s // unroll)


class Stage:

    def __init__(self, nc, name):
        self.nc, self.name, self.ctx, self.sems = nc, name, ExitStack(), []

    def __enter__(self):
        self.ctx.__enter__()
        self.ctx.enter_context(self.nc.allow_non_contiguous_dma(reason="columns of small parameters"))
        return self

    def __exit__(self, *a):
        return self.ctx.__exit__(*a)

    def sb(self, name, shape, dt=F32):
        return self.ctx.enter_context(self.nc.sbuf_tensor(f"{self.name}_{name}", shape, dt))

    def psum(self, name, shape):
        return self.ctx.enter_context(self.nc.psum_tensor(f"{self.name}_{name}", shape, F32))

    def sem(self, name):
        self.sems.append(self.ctx.enter_context(self.nc.semaphore(f"{self.name}_{name}")))
        return self.sems[-1]

    def block(self):
        self.ctx.callback(self.clear)
        return self.ctx.enter_context(self.nc.Block())

    def clear(self):
        for sem in self.sems:
            self.nc.gpsimd.sem_clear(sem)
        self.nc.all_engine_barrier()


def column(ap, n=P):
    return ap.rearrange("(k p) -> p k", p=n)


def build_constants(nc, ctx):
    def sb(name, shape):
        return ctx.enter_context(nc.sbuf_tensor(name, shape, F32))

    c = {
        "ident": sb("ident", [P, P]),
        "headsum": sb("headsum", [P, P]),
        "rw_after": sb("rw_after", [P, 2, P]),
        "rw_from": sb("rw_from", [P, 2, P]),
        "rw_level": sb("rw_level", [P, 2, 6, P]),
        "hg_from": sb("hg_from", [P, 2, P]),
        "upto": sb("upto", [P, P]),
        "ones": sb("ones", [P, P]),
    }
    with Stage(nc, "consts") as st:
        block = st.block()

        @block.gpsimd
        def _(pool):
            def keep(ap, pattern, base, mult, op=ALU.is_ge):
                pool.drain()
                nc.gpsimd.affine_select(out=ap, in_=ap, pattern=pattern, compare_op=op, fill=0.0,
                                        base=base, channel_multiplier=mult)

            def same(ap, size):
                view = ap.rearrange("p (b s) -> p b s", s=size)
                keep(view, [[-size, P // size], [0, size]], 0, 1)
                keep(view, [[size, P // size], [0, size]], size - 1, -1)

            for name in ("ident", "rw_level"):
                nc.gpsimd.memset(c[name][:], 0.0)
            for name in ("headsum", "rw_after", "rw_from", "hg_from", "upto", "ones"):
                nc.gpsimd.memset(c[name][:], 1.0)
            pool.drain()
            nc.gpsimd.affine_select(out=c["ident"][:, :], in_=c["ident"][:, :], pattern=[[-1, P]],
                                    compare_op=ALU.not_equal, fill=1.0, base=0, channel_multiplier=1)
            same(c["headsum"][:, :], HEAD)
            keep(c["upto"][:, :], [[1, P]], 0, -1)
            for d in range(2):
                sign = 1 if d == 0 else -1
                same(c["rw_after"][:, d, :], RW_CHUNK)
                keep(c["rw_after"][:, d, :], [[sign, P]], -1, -sign)
                same(c["rw_from"][:, d, :], RW_CHUNK)
                keep(c["rw_from"][:, d, :], [[sign, P]], 0, -sign)
                same(c["hg_from"][:, d, :], HG_CHUNK)
                keep(c["hg_from"][:, d, :], [[sign, P]], 0, -sign)
                for level in range(6):
                    s = 1 << level
                    view = c["rw_level"][:, d, level, :].rearrange("p (b h s) -> p b h s", h=2, s=s)[:, :, 1 - d, :]
                    nb = P // (2 * s)
                    pool.drain()
                    nc.gpsimd.memset(view, 1.0)
                    keep(view, [[-2 * s, nb], [0, s]], -s * d, 1)
                    keep(view, [[2 * s, nb], [0, s]], s * d + s - 1, -1)
            pool.drain()
    return c


def modulation(nc, c, c_ctx, w_mod, b_mod, mods):
    with Stage(nc, "mod") as st:
        cond = st.sb("cond", [P, 2, KD])
        act_c = st.sb("act_c", [P, KD, 2])
        w = st.sb("w", [P, 2, KD, BANK])
        bias = st.sb("bias", [2, N_MOD * D])
        res = st.sb("res", [2, N_MOD * D])
        ps = st.psum("ps", [P, 2, BANK])
        in_ready, w_used = st.sem("in_ready"), st.sem("w_used")
        w_ready = [st.sem(f"w_ready{u}") for u in range(2)]
        silu_ready, out_ready, stored = st.sem("silu_ready"), st.sem("out_ready"), st.sem("stored")
        n = N_MOD * D // BANK
        block = st.block()

        @block.sync
        def _(sp):
            sp.dma_start(cond[:, 0, :], column(c[0])).then_inc(in_ready, 16)
            sp.dma_start(cond[:, 1, :], column(c_ctx)).then_inc(in_ready, 16)
            sp.dma_start(bias[0:1, :], b_mod).then_inc(in_ready, 16)
            sp.dma_start(bias[1:2, :], b_mod).then_inc(in_ready, 16)
            for s in range(n):
                if s >= 2:
                    sp.wait_ge(w_used, s - 1)
                sp.dma_start(w[:, s % 2], w_mod[0, :, s * BANK:(s + 1) * BANK]
                             .rearrange("(k p) m -> p k m", p=P)).then_inc(w_ready[s % 2], 16)
            sp.wait_ge(out_ready, n)
            sp.dma_start(mods, res[:, :]).then_inc(stored, 16)
            sp.wait_ge(stored, 16)

        @block.scalar
        def _(act):
            act.wait_ge(in_ready, 64)
            nc.scalar.activation(act_c[:].rearrange("p k t -> p t k"), cond[:], ACT.Silu).then_inc(silu_ready, 1)

        @block.tensor
        def _(pe):
            pe.wait_ge(silu_ready, 1)
            for s in range(n):
                pe.wait_ge(w_ready[s % 2], 16 * (s // 2 + 1))
                if s >= 2:
                    pe.wait_ge(out_ready, s - 1)
                for k in range(KD):
                    mm = nc.tensor.matmul(ps[0:2, s % 2, :], act_c[:, k, :], w[:, s % 2, k, :],
                                          start=(k == 0), stop=(k == KD - 1))
                mm.then_inc(w_used, 1)

        @block.vector
        def _(dve):
            for s in range(n):
                dve.wait_ge(w_used, s + 1)
                at = slice(s * BANK, (s + 1) * BANK)
                nc.vector.tensor_tensor(res[:, at], ps[0:2, s % 2, :], bias[:, at], ALU.add).then_inc(out_ready, 1)


def norm_columns(nc, consts, name, sources, params, dst, keep=None, tiles=None):
    with Stage(nc, name) as st:
        scale, bias = tiles or (st.sb("scale", [P, 2, KD]), st.sb("bias", [P, 2, KD]))
        kept = [st.sem(f"kept{u}") for u in range(2)]
        x = st.sb("x", [P, 2, D])
        y = st.sb("y", [P, 2, D])
        sq = st.sb("sq", [P, D])
        ms = st.sb("ms", [P, 2, 4])
        ps = st.psum("ps", [P, 2, KD, P])
        par_ready, par_made = st.sem("par_ready"), st.sem("par_made")
        x_ready, x_used = [st.sem(f"x_ready{u}") for u in range(2)], st.sem("x_used")
        var_ready, root_ready = st.sem("var_ready"), st.sem("root_ready")
        y_ready, turned, out_ready = st.sem("y_ready"), st.sem("turned"), st.sem("out_ready")
        loads, make = params(st, scale, bias)
        block = st.block()
        total = sum(a.shape[0] // P for a, _, _ in sources)

        def each(eng, body):
            done = 0
            for src, col, idx in sources:
                steps(eng, src.shape[0] // P, 2, lambda s, u, r: body(s, u, r, done, src, col, idx))
                done += src.shape[0] // P

        @block.sync
        def _(sp):
            for a, b in loads:
                sp.dma_start(a, b).then_inc(par_ready, 16)

            def load(s, u, r, done, src, col, idx):
                sp.wait_ge(x_used, s + done + 1)
                sp.dma_start(x[:, u, :], src[bass.ds(s * P, P), :]).then_inc(x_ready[u], 16)

            each(sp, load)

        @block.scalar
        def _(act):
            act.wait_ge(par_made, 1)

            def body(s, u, r, done, src, col, idx):
                act.drain()
                act.wait_ge(x_ready[u], (r + done // 2 + 1) * 16)
                nc.scalar.activation(sq[:, :], x[:, u, :], ACT.Square, accum_out=ms[:, u, 0:1]).then_inc(var_ready, 1)
                act.wait_ge(root_ready, s + done + 1)
                nc.scalar.activation(ms[:, u, 2:3], ms[:, u, 1:2], ACT.Sqrt).then_inc(var_ready, 1)
                if keep is not None:
                    act.wait_ge(y_ready, s + done + 1)
                    act.dma_start(keep[bass.ds(s * P, P), :], y[:, u, :]).then_inc(kept[u], 16)
                act.wait_ge(turned, s + done + 1)
                for k in range(KD):
                    op = nc.scalar.activation(dst[:, k, bass.ds(s * P + col, P)], ps[:, u, k, :], ACT.Identity,
                                              bias=bias[:, idx, k:k + 1], scale=scale[:, idx, k:k + 1])
                op.then_inc(out_ready, 1)

            if keep is not None:
                for u in range(2):
                    act.sem_inc(kept[u], 16)
            each(act, body)
            if keep is not None:
                for u in range(2):
                    act.wait_ge(kept[u], 16 * (total // 2 + 1))

        @block.vector
        def _(dve):
            dve.wait_ge(par_ready, 16 * len(loads))
            make(dve)
            dve.drain()
            dve.sem_inc(par_made, 1)
            dve.sem_inc(x_used, 2)

            def body(s, u, r, done, src, col, idx):
                dve.wait_ge(var_ready, (s + done) * 2 + 1)
                nc.vector.tensor_scalar(ms[:, u, 1:2], ms[:, u, 0:1], 1.0 / D, EPS, ALU.mult, ALU.add)\
                    .then_inc(root_ready, 1)
                dve.wait_ge(var_ready, (s + done) * 2 + 2)
                nc.vector.reciprocal(ms[:, u, 3:4], ms[:, u, 2:3])
                dve.drain()
                if keep is not None:
                    dve.wait_ge(kept[u], (r + 1) * 16)
                nc.vector.tensor_scalar(y[:, u, :], x[:, u, :], ms[:, u, 3:4], None, ALU.mult).then_inc(y_ready, 1)
                dve.wait_ge(y_ready, s + done + 1)
                dve.sem_inc(x_used, 1)

            each(dve, body)

        @block.tensor
        def _(pe):
            def body(s, u, r, done, src, col, idx):
                pe.wait_ge(y_ready, s + done + 1)
                for k in range(KD):
                    tr = nc.tensor.transpose(ps[:, u, k, :], y[:, u, k * P:(k + 1) * P], consts["ident"][:, :])
                tr.then_inc(turned, 1)

            each(pe, body)


def linear_columns(nc, name, w, act, tokens, out):
    K, M = w.shape
    KT = K // P
    parts = chunks(tokens)
    full, rest = M // P, M % P
    with Stage(nc, name) as st:
        wt = st.sb("w", [P, 2, KT, P])
        w_high, w_low = (st.sb(n, [P, 2, KT, P], F32R) for n in ("w_high", "w_low"))
        a_high, a_low = (st.sb(n, [P, KT, tokens], F32R) for n in ("a_high", "a_low"))
        res = st.sb("res", [P, 2, tokens])
        ps = st.psum("ps", [P, 2, len(parts), BANK])
        w_split, a_rounded, a_split = st.sem("w_split"), st.sem("a_rounded"), st.sem("a_split")
        split_turn = st.sem("split_turn")
        w_ready, mm_done = [st.sem(f"w_ready{u}") for u in range(2)], st.sem("mm_done")
        act_read, dve_read = st.sem("act_read"), st.sem("dve_read")
        stored = [st.sem(f"stored{u}") for u in range(2)]
        block = st.block()
        waits = full + (1 if rest else 0)

        def each(eng, body):
            steps(eng, full, 2, lambda s, u, r: body(s, u, r, P))
            if rest:
                body(full, full % 2, full // 2, rest)

        @block.sync
        def _(sp):
            sp.sem_inc(w_split, 2)

            def load(s, u, r, m):
                sp.wait_ge(w_split, s + 1)
                sp.dma_start(wt[:, u, :, 0:m], w[:, bass.ds(s * P, m)].rearrange("(k p) m -> p k m", p=P))\
                    .then_inc(w_ready[u], 16)

            each(sp, load)

        @block.gpsimd
        def _(pool):
            pool.sem_inc(mm_done, 2)

            def split(s, u, r, m):
                pool.wait_ge(w_ready[u], (r + 1) * 16)
                pool.wait_ge(mm_done, s + 1)
                pool.sem_inc(split_turn, 1)
                nc.gpsimd.tensor_copy(w_high[:, u, :, 0:m], wt[:, u, :, 0:m])
                pool.drain()
                nc.gpsimd.tensor_tensor(w_low[:, u, :, 0:m], wt[:, u, :, 0:m], w_high[:, u, :, 0:m], ALU.subtract)\
                    .then_inc(w_split, 1)

            each(pool, split)

        @block.tensor
        def _(pe):
            pe.wait_ge(a_split, KT)

            def body(s, u, r, m):
                pe.wait_ge(w_split, s + 3)
                pe.wait_ge(act_read, s + 1)
                pe.wait_ge(dve_read, s + 1)
                for n, (at, size) in enumerate(parts):
                    for k in range(KT):
                        for j, (w_part, a_part) in enumerate(((w_high, a_high), (w_high, a_low), (w_low, a_high))):
                            mm = nc.tensor.matmul(ps[0:m, u, n, 0:size], w_part[:, u, k, 0:m], a_part[:, k, at:at + size],
                                                  start=(k == 0 and j == 0), stop=(k == KT - 1 and j == 2))
                mm.then_inc(mm_done, 1)

            each(pe, body)

        @block.scalar
        def _(eng):
            eng.sem_inc(act_read, 2)
            for k in range(KT):
                nc.scalar.copy(a_high[:, k, :], act[:, k, :]).then_inc(a_rounded, 1)
            for u in range(2):
                eng.sem_inc(stored[u], 16)

            def body(s, u, r, m):
                eng.wait_ge(mm_done, s + 3)
                eng.wait_ge(stored[u], (r + 1) * 16)
                at, size = parts[0]
                nc.scalar.copy(res[0:m, u, at:at + size], ps[0:m, u, 0, 0:size]).then_inc(act_read, 1)
                eng.wait_ge(act_read, s + 3)
                eng.wait_ge(dve_read, s + 3)
                eng.dma_start(out[bass.ds(s * P, m), :], res[0:m, u, :]).then_inc(stored[u], 16)

            each(eng, body)
            for u in range(2):
                eng.wait_ge(stored[u], 16 * ((waits - u + 1) // 2 + 1))

        @block.vector
        def _(eng):
            eng.sem_inc(dve_read, 2)
            for k in range(KT):
                eng.wait_ge(a_rounded, k + 1)
                nc.vector.tensor_tensor(a_low[:, k, :], act[:, k, :], a_high[:, k, :], ALU.subtract).then_inc(a_split, 1)

            def body(s, u, r, m):
                eng.wait_ge(mm_done, s + 3)
                eng.wait_ge(stored[u], (r + 1) * 16)
                for n, (at, size) in enumerate(parts[1:], 1):
                    cp = nc.vector.tensor_copy(res[0:m, u, at:at + size], ps[0:m, u, n, 0:size])
                cp.then_inc(dve_read, 1)

            each(eng, body)


def rwkv_prepare(nc, consts, proj, par, rw):
    with Stage(nc, "rwprep") as st:
        raw = st.sb("raw", [P, 3, TOK])
        rkv = st.sb("rkv", [P, 3, TOK])
        term = st.sb("term", [P, 2, TOK])
        wd = st.sb("wd", [P, TOK])
        ad = st.sb("ad", [P, TOK])
        gd = st.sb("gd", [P, SEQ])
        cols = st.sb("cols", [P, 10])
        taps = st.sb("taps", [P, 3, 9])
        w2 = st.sb("w2", [P, 3, P])
        reset = st.sb("reset", [P, TOK])
        kk = st.sb("kk", [P, TOK])
        sq = st.sb("sq", [P, TOK])
        kd = st.sb("kd", [P, 2, TOK])
        sig_w = st.sb("sig_w", [P, TOK])
        sig_a = st.sb("sig_a", [P, TOK])
        inc = st.sb("inc", [P, TOK])
        exc = st.sb("exc", [P, TOK])
        cum = st.sb("cum", [P, TOK])
        fac = st.sb("fac", [P, 2, 6, TOK])
        tot = st.sb("tot", [P, 2, RW_CHUNKS])
        gate = st.sb("gate", [P, SEQ])
        bonus = st.sb("bonus", [P, SEQ])
        ps = st.psum("ps", [P, 2, 3 * BANK])
        once, in_ready, par_ready = st.sem("once"), st.sem("in_ready"), st.sem("par_ready")
        rk_made, v_made, v_turn, sig_gd = st.sem("rk_made"), st.sem("v_made"), st.sem("v_turn"), st.sem("sig_gd")
        sq_ready, sum_ready, sum_used, root_ready = (st.sem("sq_ready"), st.sem("sum_ready"), st.sem("sum_used"),
                                                    st.sem("root_ready"))
        z_ready, z_used, al_ready, al_used = st.sem("z_ready"), st.sem("z_used"), st.sem("al_ready"), st.sem("al_used")
        logs_ready, exps_ready, fac_ready = st.sem("logs_ready"), st.sem("exps_ready"), st.sem("fac_ready")
        fac_sent = [st.sem(f"fac_sent{d}") for d in range(2)]
        prod_ready, bsum_ready, bsum_used = st.sem("prod_ready"), st.sem("bsum_ready"), st.sem("bsum_used")
        g_ready, g_used, extra_sent = st.sem("g_ready"), st.sem("g_used"), st.sem("extra_sent")
        W0, A0, KK, KA, RK, OMKA = 0, 2, 4, 5, 6, 7
        tok = chunks(TOK)
        lat = chunks(SEQ)
        block = st.block()

        def by_chunk(ap):
            return ap.rearrange("p (c t) -> p c t", t=RW_CHUNK)

        def grid(ap):
            return ap[:, CTX:TOK].rearrange("p (y x) -> p y x", x=GRID_W)

        @block.sync
        def _(sp):
            for d in range(2):
                sp.sem_inc(fac_sent[d], 112)
            sp.sem_inc(extra_sent, 48)
            sp.dma_start(wd[:, :], proj[ROW_WD:ROW_WD + P, :]).then_inc(once, 16)
            sp.dma_start(ad[:, :], proj[ROW_AD:ROW_AD + P, :]).then_inc(once, 16)
            sp.dma_start(gd[:, :], proj[ROW_GD:ROW_GD + P, CTX:TOK]).then_inc(once, 16)

            def load_raw(i):
                for j, row in enumerate((ROW_R, ROW_K, ROW_V)):
                    sp.dma_start(raw[:, j, :], proj[bass.ds(i * P + row, P), :]).then_inc(in_ready, 16)
                    sp.dma_start(taps[:, j, :], par["conv"][:, bass.ds(i * P + row, P)].rearrange("t p -> p t"))\
                        .then_inc(in_ready, 16)

            def body(i, last):
                at = bass.ds(i * P, P)
                sp.dma_start(cols[:, W0:W0 + 2], par["w0"][:, at].rearrange("d p -> p d")).then_inc(par_ready, 16)
                sp.dma_start(cols[:, A0:A0 + 2], par["a0"][:, at].rearrange("d p -> p d")).then_inc(par_ready, 16)
                for j, name in ((KK, "k_k"), (KA, "k_a"), (RK, "r_k")):
                    sp.dma_start(cols[:, j:j + 1], par[name][at].rearrange("(p o) -> p o", o=1))\
                        .then_inc(par_ready, 16)
                sp.dma_start(w2[:, 0, :], par["w2"][:, at]).then_inc(par_ready, 16)
                sp.dma_start(w2[:, 1, :], par["a2"][:, at]).then_inc(par_ready, 16)
                sp.dma_start(w2[:, 2, :], par["g2"][:, at]).then_inc(par_ready, 16)

                if not last:
                    sp.wait_ge(rk_made, i + 1)
                    sp.wait_ge(v_made, i + 1)
                    load_raw(i + 1)
                for d in range(2):
                    sp.wait_ge(fac_ready, i * 2 + d + 2)
                    for j, name in enumerate(("a", "r", "b", "k", "bh", "kh")):
                        sp.dma_start(rw[name][d, at, :], fac[:, d, j, :]).then_inc(fac_sent[d], 16)
                    sp.dma_start(rw["tot"][d, at, :], tot[:, d, :]).then_inc(fac_sent[d], 16)
                sp.wait_ge(bsum_used, i + 2)
                sp.wait_ge(g_used, i + 2)
                sp.dma_start(rw["v"][at, :], rkv[:, 2, :]).then_inc(extra_sent, 16)
                sp.dma_start(rw["bonus"][at, :], bonus[:, :]).then_inc(extra_sent, 16)
                sp.dma_start(rw["gate"][at, :], gate[:, :]).then_inc(extra_sent, 16)

            load_raw(0)
            with sp.Fori(0, QT - 1) as i:
                body(i, False)
            body(QT - 1, True)
            for d in range(2):
                sp.wait_ge(fac_sent[d], 112 * (QT + 1))
            sp.wait_ge(extra_sent, 48 * (QT + 1))

        @block.tensor
        def _(pe):
            pe.wait_ge(sig_gd, 1)

            def body(i, u, r):
                pe.wait_ge(sq_ready, i + 1)
                pe.wait_ge(g_used, i + 1)
                for at, n in tok:
                    mm = nc.tensor.matmul(ps[:, 0, at:at + n], consts["headsum"][:, :], sq[:, at:at + n],
                                          start=True, stop=True)
                mm.then_inc(sum_ready, 1)
                pe.wait_ge(par_ready, (i + 1) * (16 * 8))
                for d in range(2):
                    rows = slice(d * HEAD, (d + 1) * HEAD)
                    pe.wait_ge(bsum_used, i + 1) if d == 0 else pe.wait_ge(z_used, i * 2 + 1)
                    for at, n in tok:
                        mm = nc.tensor.matmul(ps[:, 1, at:at + n], w2[rows, 0, :], wd[rows, at:at + n],
                                              start=True, stop=True)
                    mm.then_inc(z_ready, 1)
                    pe.wait_ge(sum_used, i + 1) if d == 0 else pe.wait_ge(al_used, i * 2 + 1)
                    for at, n in tok:
                        mm = nc.tensor.matmul(ps[:, 0, at:at + n], w2[rows, 1, :], ad[rows, at:at + n],
                                              start=True, stop=True)
                    mm.then_inc(al_ready, 1)
                pe.wait_ge(prod_ready, i + 1)
                pe.wait_ge(z_used, i * 2 + 2)
                for at, n in lat:
                    mm = nc.tensor.matmul(ps[:, 1, at:at + n], consts["headsum"][:, :],
                                          sq[:, CTX + at:CTX + at + n], start=True, stop=True)
                mm.then_inc(bsum_ready, 1)
                pe.wait_ge(al_used, i * 2 + 2)
                for at, n in lat:
                    mm = nc.tensor.matmul(ps[:, 0, at:at + n], w2[:, 2, :], gd[:, at:at + n],
                                          start=True, stop=True)
                mm.then_inc(g_ready, 1)

            steps(pe, QT, 1, body)

        @block.scalar
        def _(act):
            act.wait_ge(once, 48)
            nc.scalar.activation(wd[:, :], wd[:, :], ACT.Tanh)
            nc.scalar.activation(gd[:, :], gd[:, :], ACT.Sigmoid).then_inc(sig_gd, 1)
            act.sem_inc(g_used, 1)

            def body(i, u, r):
                act.wait_ge(root_ready, i * 2 + 1)
                nc.scalar.activation(sq[:, :], kk[:, :], ACT.Square).then_inc(sq_ready, 1)
                act.wait_ge(root_ready, i * 2 + 2)
                nc.scalar.activation(sq[:, :], sq[:, :], ACT.Sqrt).then_inc(sum_used, 1)
                for d in range(2):
                    act.drain()
                    act.wait_ge(z_ready, i * 2 + d + 1)
                    act.wait_ge(logs_ready, i * 2 + d + 1)
                    nc.scalar.activation(sig_w[:, :], ps[:, 1, 0:TOK], ACT.Sigmoid, bias=cols[:, W0 + d:W0 + d + 1])\
                        .then_inc(z_used, 1)
                    act.wait_ge(al_ready, i * 2 + d + 1)
                    act.wait_ge(fac_ready, i * 2 + d + 1)
                    nc.scalar.activation(sig_a[:, :], ps[:, 0, 0:TOK], ACT.Sigmoid, bias=cols[:, A0 + d:A0 + d + 1])\
                        .then_inc(al_used, 1)
                    act.wait_ge(logs_ready, i * 2 + d + 2)
                    act.wait_ge(fac_sent[d], (i + 1) * 112)
                    nc.scalar.activation(fac[:, d, 0, :], exc[:, :], ACT.Exp)
                    nc.scalar.activation(fac[:, d, 1, :], inc[:, :], ACT.Exp)
                    nc.scalar.activation(fac[:, d, 2, :], inc[:, :], ACT.Exp, scale=-1.0)
                    nc.scalar.activation(fac[:, d, 4, :], sig_w[:, :], ACT.Exp)
                    nc.scalar.activation(tot[:, d, :], by_chunk(cum[:, :])[:, :, RW_CHUNK - 1], ACT.Exp)\
                        .then_inc(exps_ready, 1)
                act.wait_ge(g_ready, i + 1)
                act.wait_ge(extra_sent, (i + 1) * 48)
                nc.scalar.copy(gate[:, :], ps[:, 0, 0:SEQ]).then_inc(g_used, 1)

            steps(act, QT, 1, body)

        def shifted(j, dy, dx):
            ya, yb, xa, xb = max(0, -dy), max(0, dy), max(0, -dx), max(0, dx)
            return (lambda ap: grid(ap)[:, ya:GRID_H - yb, xa:GRID_W - xb]), \
                grid(raw[:, j, :])[:, yb:GRID_H - ya, xb:GRID_W - xa], (dy + 1) * 3 + dx + 1

        def along(j, dx):
            a, b = max(0, -dx), max(0, dx)
            return (lambda ap: ap[:, a:CTX - b]), raw[:, j, b:CTX - a], 4 + dx

        AROUND = [(along, (dx,)) for dx in (-1, 1)] + \
            [(shifted, (dy, dx)) for dy in (-1, 0, 1) for dx in (-1, 0, 1) if dy or dx]

        @block.gpsimd
        def _(pool):
            def body(i, u, r):
                pool.wait_ge(in_ready, (i + 1) * 96)
                pool.wait_ge(bsum_used, i + 1)
                pool.wait_ge(extra_sent, (i + 1) * 48)
                pool.sem_inc(v_turn, 1)
                nc.gpsimd.tensor_scalar(rkv[:, 2, :], raw[:, 2, :], taps[:, 2, 4:5], None, ALU.mult)
                for n, (where, step) in enumerate(AROUND):
                    dst, src, t = where(2, *step)
                    nc.gpsimd.tensor_scalar(dst(term[:, n % 2, :]), src, taps[:, 2, t:t + 1], None, ALU.mult)
                    pool.drain()
                    nc.gpsimd.tensor_tensor(dst(rkv[:, 2, :]), dst(rkv[:, 2, :]), dst(term[:, n % 2, :]), ALU.add)
                pool.drain()
                pool.sem_inc(v_made, 1)

            steps(pool, QT, 1, body)

        @block.vector
        def _(dve):
            nc.vector.memset(reset[:, :], 1.0)
            dve.drain()
            nc.vector.memset(by_chunk(reset[:, :])[:, :, 0:1], 0.0)
            dve.drain()
            dve.sem_inc(logs_ready, 1)
            dve.sem_inc(fac_ready, 1)
            dve.sem_inc(bsum_used, 1)

            def body(i, u, r):
                dve.wait_ge(in_ready, (i + 1) * 96)
                for j in range(2):
                    nc.vector.tensor_scalar(rkv[:, j, :], raw[:, j, :], taps[:, j, 4:5], None, ALU.mult)
                for where, step in AROUND:
                    dve.drain()
                    for j in range(2):
                        dst, src, t = where(j, *step)
                        nc.vector.scalar_tensor_tensor(dst(rkv[:, j, :]), src, taps[:, j, t:t + 1], dst(rkv[:, j, :]),
                                                       ALU.mult, ALU.add)
                dve.drain()
                dve.sem_inc(rk_made, 1)
                rr, k, v = (rkv[:, j, :] for j in range(3))
                dve.wait_ge(par_ready, (i + 1) * (16 * 8))
                nc.vector.tensor_scalar(kk[:, :], k, cols[:, KK:KK + 1], None, ALU.mult).then_inc(root_ready, 1)
                nc.vector.tensor_scalar(cols[:, OMKA:OMKA + 1], cols[:, KA:KA + 1], -1.0, 1.0, ALU.mult, ALU.add)
                dve.wait_ge(sum_ready, i + 1)
                nc.vector.tensor_scalar(sq[:, :], ps[:, 0, 0:TOK], 1e-24, None, ALU.max).then_inc(root_ready, 1)
                dve.wait_ge(sum_used, i + 1)
                nc.vector.reciprocal(sq[:, :], sq[:, :])
                dve.drain()
                nc.vector.tensor_tensor(kk[:, :], kk[:, :], sq[:, :], ALU.mult)
                for d in range(2):
                    dve.wait_ge(z_used, i * 2 + d + 1)
                    nc.vector.tensor_scalar(sig_w[:, :], sig_w[:, :], -float(np.exp(-0.5)), None, ALU.mult)
                    dve.drain()
                    nc.vector.tensor_tensor_scan(cum[:, :], reset[:, :], sig_w[:, :], 0.0, ALU.mult, ALU.add)
                    dve.drain()
                    last = by_chunk(cum[:, :])[:, :, RW_CHUNK - 1:RW_CHUNK].broadcast_to([P, RW_CHUNKS, RW_CHUNK])
                    if d == 0:
                        nc.vector.tensor_tensor(exc[:, :], cum[:, :], sig_w[:, :], ALU.subtract)
                        nc.vector.tensor_copy(inc[:, :], cum[:, :])
                    else:
                        nc.vector.tensor_tensor(by_chunk(exc[:, :]), last, by_chunk(cum[:, :]), ALU.subtract)
                        dve.drain()
                        nc.vector.tensor_tensor(inc[:, :], exc[:, :], sig_w[:, :], ALU.add)
                    dve.drain()
                    nc.vector.tensor_tensor(by_chunk(sig_w[:, :]), last, by_chunk(inc[:, :]), ALU.subtract)
                    dve.wait_ge(al_used, i * 2 + d + 1)
                    nc.vector.tensor_scalar(kd[:, d, :], sig_a[:, :], cols[:, KA:KA + 1], cols[:, OMKA:OMKA + 1],
                                            ALU.mult, ALU.add)
                    nc.vector.tensor_tensor(sig_a[:, :], sig_a[:, :], kk[:, :], ALU.mult)
                    dve.drain()
                    nc.vector.tensor_tensor(kd[:, d, :], kd[:, d, :], k, ALU.mult).then_inc(logs_ready, 1)
                    dve.drain()
                    dve.wait_ge(exps_ready, i * 2 + d + 1)
                    f = [fac[:, d, j, :] for j in range(6)]
                    nc.vector.scalar_tensor_tensor(f[0], kk[:, :], -1.0, f[0], ALU.mult, ALU.mult)
                    nc.vector.tensor_tensor(f[1], rr, f[1], ALU.mult)
                    nc.vector.tensor_tensor(f[3], kd[:, d, :], f[2], ALU.mult)
                    nc.vector.tensor_tensor(f[5], kd[:, d, :], f[4], ALU.mult)
                    dve.drain()
                    nc.vector.tensor_tensor(f[2], sig_a[:, :], f[2], ALU.mult)
                    nc.vector.tensor_tensor(f[4], sig_a[:, :], f[4], ALU.mult).then_inc(fac_ready, 1)
                nc.vector.tensor_tensor(sq[:, :], kd[:, 0, :], kd[:, 1, :], ALU.add)
                dve.drain()
                nc.vector.scalar_tensor_tensor(sq[:, :], sq[:, :], cols[:, RK:RK + 1], rr, ALU.mult, ALU.mult)\
                    .then_inc(prod_ready, 1)
                dve.wait_ge(bsum_ready, i + 1)
                dve.wait_ge(v_made, i + 1)
                dve.wait_ge(extra_sent, (i + 1) * 48)
                nc.vector.tensor_tensor(bonus[:, :], ps[:, 1, 0:SEQ], rkv[:, 2, CTX:TOK], ALU.mult)\
                    .then_inc(bsum_used, 1)

            steps(dve, QT, 1, body)


def over(ap, n):
    return ap.rearrange("p (o t) -> p o t", o=1).broadcast_to([ap.shape[0], n, ap.shape[1]])


def last_of(ap, n):
    return ap.rearrange("p (h o) -> p h o", o=1).broadcast_to([ap.shape[0], ap.shape[1], n])


class Turns:

    def __init__(self, sem, phases, ahead=0):
        self.sem, self.phases, self.ahead = sem, phases, ahead

    def after(self, rnd, phase):
        return rnd * len(self.phases) + sum(p <= phase for p in self.phases) + self.ahead


def rwkv_chunks(nc, consts, rw, d):
    HQ = 4
    with Stage(nc, f"rwchunk{d}") as st:
        def pair(name, shape):
            return [st.sb(f"{name}{u}", shape) for u in range(2)]

        ar = pair("ar", [HEAD, 2, HQ, 2, P])
        bk = pair("bk", [HEAD, 2, 2, HQ, P])
        flat = pair("flat", [P, 2, 4, 2, P])
        tot = pair("tot", [HEAD, 2, 2, HQ])
        rT = pair("rT", [HEAD, HQ, P])
        az = pair("az", [P, HQ, P])
        bkv = pair("bkv", [P, 3, HQ, HEAD])
        at = pair("at", [P, HQ, P])
        cb = pair("cb", [P, HQ, P])
        bkT = pair("bkT", [P, HQ, P])
        ck = pair("ck", [P, HQ, P])
        T = pair("T", [P, HQ, P])
        TT = pair("TT", [P, HQ, P])
        X = pair("X", [P, 2, HQ, P])
        W = pair("W", [P, HQ, P])
        wu = pair("wu", [P, HQ, P])
        diag = pair("diag", [HEAD, HQ * 2, HEAD])
        q_out = pair("q_out", [HEAD, HQ, P])
        y_out = pair("y_out", [P, HQ, HEAD])
        m_out = pair("m_out", [HEAD, HQ * 2, HEAD])
        n_out = pair("n_out", [HEAD, HQ * 2, HEAD])
        ps = [st.psum(f"ps{u}", [P, 4, BANK]) for u in range(2)]

        TURN, BKCK, FIRST, LAST, ZED, WUP, OUT = 0, 1, 2, 11, 12, 13, 14
        level_w = {2 * l: l for l in range(1, 6)}
        level_t = {2 * l + 1: l for l in range(1, 6)}
        loaded = [[st.sem(f"loaded{u}{z}") for z in range(2)] for u in range(2)]
        stored = [st.sem(f"stored{u}") for u in range(2)]
        mm = [Turns(st.sem(f"products{u}"), list(range(15))) for u in range(2)]
        vec = [Turns(st.sem(f"read_by_vector{u}"), [TURN, BKCK, *level_t, OUT], 1) for u in range(2)]
        sca = [Turns(st.sem(f"read_by_scalar{u}"), [TURN, *level_w, ZED, WUP, OUT], 10) for u in range(2)]
        lev = [Turns(st.sem(f"levels{u}"), [TURN, *level_w], 7) for u in range(2)]
        t_products = [st.sem(f"t_products{u}") for u in range(2)]
        t_summed = [st.sem(f"t_summed{u}") for u in range(2)]
        LOADS, STORES = 10, 4
        block = st.block()

        def rounds(eng, body):
            with eng.Fori(0, TILES // 2) as i:
                for z in range(2):
                    body(i * 2 + z, z, i + 1)

        @block.sync
        def _(sp):
            def body(t, z, n):
                tk = bass.ds(t * P, P)
                for u in range(2):
                    rows = slice(u * HQ * HEAD, (u + 1) * HQ * HEAD)
                    sp.wait_ge(mm[u].sem, t * 15 + 2)
                    sp.wait_ge(sca[u].sem, t * 9 + 1)
                    sp.wait_ge(lev[u].sem, t * 6 + 1)
                    for j, name in enumerate(("a", "r")):
                        sp.dma_start(ar[u][:, z, :, j, :], rw[name][d, rows, tk].rearrange("(h k) t -> k h t", k=HEAD))\
                            .then_inc(loaded[u][z], 16)
                    for j, name in enumerate(("b", "k")):
                        sp.dma_start(bk[u][:, z, j], rw[name][d, rows, tk].rearrange("(h k) t -> k h t", k=HEAD))\
                            .then_inc(loaded[u][z], 16)
                    for j, name in enumerate(("a", "bh", "kh")):
                        sp.dma_start(flat[u][:, z, j], rw[name][d, rows, tk].rearrange("(g p) t -> p g t", p=P))\
                            .then_inc(loaded[u][z], 16)
                    sp.dma_start(flat[u][:, z, 3], rw["v"][rows, tk].rearrange("(g p) t -> p g t", p=P))\
                        .then_inc(loaded[u][z], 16)
                    for c in range(2):
                        sp.dma_start(tot[u][:, z, c, :], rw["tot"][d, rows, bass.ds(t * 2 + c, 1)]
                                     .rearrange("(h k) c -> k (h c)", k=HEAD)).then_inc(loaded[u][z], 16)

            for u in range(2):
                sp.sem_inc(mm[u].sem, 17)
            rounds(sp, body)

        for u in range(2):
            mm[u].ahead = 17

        @block.tensor
        def _(pe):
            def phase(p, t, z, n, u):
                b = ps[u]
                if p == TURN:
                    pe.wait_ge(loaded[u][z], n * (16 * LOADS))
                if p in level_w and level_w[p] > 1:
                    pe.wait_ge(t_summed[u], t * 4 + (level_w[p] - 1))
                else:
                    pe.wait_ge(vec[u].sem, vec[u].after(t, BKCK if p == ZED else p - 1))
                pe.wait_ge(sca[u].sem, sca[u].after(t, p - 1))
                if p == TURN:
                    for j in range(4):
                        for g in range(2):
                            nc.tensor.transpose(b[:, j // 2, ((j % 2) * 2 + g) * P:((j % 2) * 2 + g + 1) * P],
                                                flat[u][:, z, j, g, :], consts["ident"][:, :])
                    for h in range(HQ):
                        op = nc.tensor.matmul(b[:, 2 + h // 2, (h % 2) * 2 * P:(h % 2 + 1) * 2 * P],
                                              bk[u][:, z, 0, h, :], ar[u][:, z, h], start=True, stop=True)
                elif p == BKCK:
                    for h in range(HQ):
                        nc.tensor.matmul(b[:, h // 2, (h % 2) * 2 * P:(h % 2 + 1) * 2 * P],
                                         bk[u][:, z, 1, h, :], ar[u][:, z, h], start=True, stop=True)
                    for h in range(HQ):
                        op = nc.tensor.matmul(b[:, 2, h * P:(h + 1) * P], ar[u][:, z, h, 0, :], bk[u][:, z, 0, h, :],
                                              start=True, stop=True)
                elif p in level_w:
                    l = level_w[p]
                    pe.wait_ge(lev[u].sem, lev[u].after(t, p))
                    for h in range(HQ):
                        op = nc.tensor.matmul(b[:, 3, h * P:(h + 1) * P], X[u][:, l % 2, h, :], T[u][:, h, :],
                                              start=True, stop=True)
                elif p in level_t:
                    if level_t[p] < 5:
                        for h in range(HQ):
                            op = nc.tensor.matmul(b[:, 0, h * P:(h + 1) * P], TT[u][:, h, :], W[u][:, h, :],
                                                  start=True, stop=True)
                        op.then_inc(t_products[u], 1)
                    for h in range(HQ):
                        op = nc.tensor.matmul(b[:, 1, h * P:(h + 1) * P], W[u][:, h, :], TT[u][:, h, :],
                                              start=True, stop=True)
                elif p == ZED:
                    for h in range(HQ):
                        op = nc.tensor.matmul(b[:, 2, h * HEAD:(h + 1) * HEAD], bkT[u][:, h, :], bkv[u][:, 2, h, :],
                                              start=True, stop=True)
                elif p == WUP:
                    for h in range(HQ):
                        op = nc.tensor.matmul(b[:, 3, h * P:(h + 1) * P], TT[u][:, h, :], az[u][:, h, :],
                                              start=True, stop=True)
                else:
                    for h in range(HQ):
                        nc.tensor.matmul(b[0:HEAD, 0, h * P:(h + 1) * P], wu[u][:, h, 0:HEAD], cb[u][:, h, :],
                                         start=True, stop=True)
                    for h in range(HQ):
                        y = b[:, 1, h * HEAD:(h + 1) * HEAD]
                        nc.tensor.matmul(y, cb[u][:, h, :], wu[u][:, h, HEAD:P], start=True, stop=False)
                        nc.tensor.matmul(y, ck[u][:, h, :], bkv[u][:, 2, h, :], start=False, stop=True)
                    for h in range(HQ):
                        for c in range(2):
                            rows = slice(c * HEAD, (c + 1) * HEAD)
                            m, n = (b[0:HEAD, 2 + c, (j * HQ + h) * HEAD:(j * HQ + h + 1) * HEAD] for j in range(2))
                            nc.tensor.matmul(m, wu[u][rows, h, 0:HEAD], bkv[u][rows, 0, h, :],
                                             start=True, stop=True)
                            nc.tensor.matmul(n, bkv[u][rows, 0, h, :], wu[u][rows, h, HEAD:P],
                                             start=True, stop=False)
                            op = nc.tensor.matmul(n, bkv[u][rows, 1, h, :], bkv[u][rows, 2, h, :],
                                                  start=False, stop=True)
                op.then_inc(mm[u].sem, 1)

            rounds(pe, lambda t, z, n: [phase(p, t, z, n, u) for p in range(15) for u in range(2)])

        @block.gpsimd
        def _(pool):
            for u in range(2):
                pool.sem_inc(lev[u].sem, 7)

            def body(t, z, n):
                for u in range(2):
                    pool.wait_ge(loaded[u][z], n * (16 * LOADS))
                    pool.wait_ge(vec[u].sem, vec[u].after(t, -1))
                    nc.gpsimd.tensor_tensor(diag[u][:], over(consts["ident"][0:HEAD, 0:HEAD], 2 * HQ),
                                            last_of(tot[u][:, z].rearrange("k c h -> k (c h)"), HEAD), ALU.mult)\
                        .then_inc(lev[u].sem, 1)
                for p, l in level_w.items():
                    for u in range(2):
                        pool.wait_ge(vec[u].sem, vec[u].after(t, TURN))
                        if l > 2:
                            pool.wait_ge(mm[u].sem, mm[u].after(t, 2 * (l - 2)))
                        nc.gpsimd.tensor_tensor(X[u][:, l % 2], at[u][:], over(consts["rw_level"][:, d, l, :], HQ),
                                                ALU.mult).then_inc(lev[u].sem, 1)

            rounds(pool, body)

        @block.scalar
        def _(act):
            for u in range(2):
                act.sem_inc(sca[u].sem, 10)
                act.sem_inc(stored[u], 16 * STORES)

            def phase(p, t, z, u):
                b = ps[u]
                act.wait_ge(mm[u].sem, mm[u].after(t, p))
                if p == TURN:
                    nc.scalar.copy(az[u][:, :, 0:HEAD], b[:, 0, 0:2 * P].rearrange("t (h k) -> t h k", k=HEAD))
                    nc.scalar.copy(bkv[u][:, 0], b[:, 0, 2 * P:4 * P].rearrange("t (h k) -> t h k", k=HEAD))
                    nc.scalar.copy(bkv[u][:, 1:3], b[:, 1, :].rearrange("t (j h k) -> t j h k", j=2, k=HEAD))
                    act.wait_ge(vec[u].sem, vec[u].after(t, -1))
                    op = nc.scalar.copy(rT[u][:], ar[u][:, z, :, 1, :])
                elif p in level_w:
                    op = nc.scalar.copy(W[u][:], b[:, 3, :].rearrange("p (h t) -> p h t", h=HQ))
                elif p == ZED:
                    op = nc.scalar.copy(az[u][:, :, HEAD:P], b[:, 2, 0:HQ * HEAD].rearrange("p (h t) -> p h t", h=HQ))
                elif p == WUP:
                    op = nc.scalar.copy(wu[u][:], b[:, 3, :].rearrange("p (h t) -> p h t", h=HQ))
                else:
                    act.wait_ge(stored[u], (t + 1) * (16 * STORES))
                    nc.scalar.copy(y_out[u][:], b[:, 1, 0:HQ * HEAD].rearrange("p (h t) -> p h t", h=HQ))
                    op = nc.scalar.copy(n_out[u][:].rearrange("p (c h) t -> p c (h t)", c=2), b[0:HEAD, 2:4, HQ * HEAD:])
                op.then_inc(sca[u].sem, 1)
                if p == OUT:
                    act.wait_ge(sca[u].sem, sca[u].after(t, p))
                    act.wait_ge(vec[u].sem, vec[u].after(t, p))
                    for name, src in (("q", q_out), ("y", y_out), ("m", m_out), ("n", n_out)):
                        act.dma_start(rw[name + "_out"][d, bass.ds(t, 1), u].rearrange("o p h n -> (o p) h n"),
                                      src[u][:]).then_inc(stored[u], 16)

            rounds(act, lambda t, z, n: [phase(p, t, z, u) for p in sca[0].phases for u in range(2)])
            for u in range(2):
                act.wait_ge(stored[u], 16 * STORES * (TILES + 1))

        @block.vector
        def _(dve):
            for u in range(2):
                dve.sem_inc(vec[u].sem, 1)
            eye = over(consts["ident"][:, :], HQ)

            def quad(ap):
                return ap.rearrange("p (h t) -> p h t", h=HQ)

            def phase(p, t, z, u):
                b = ps[u]
                if p in level_t and level_t[p] < 5:
                    dve.wait_ge(t_products[u], t * 4 + level_t[p])
                    nc.vector.tensor_tensor(T[u][:], T[u][:], quad(b[:, 0, :]), ALU.add).then_inc(t_summed[u], 1)
                dve.wait_ge(mm[u].sem, mm[u].after(t, p))
                if p in (TURN, BKCK):
                    banks = b[:, 2:4, :] if p == TURN else b[:, 0:2, :]
                    v = banks.rearrange("p b (g j t) -> p (b g) j t", g=2, j=2)
                    strict, upto = (at, cb) if p == TURN else (bkT, ck)
                    nc.vector.tensor_tensor(strict[u][:], v[:, :, 0, :], over(consts["rw_after"][:, d, :], HQ), ALU.mult)
                    if p == BKCK:
                        nc.vector.tensor_tensor(TT[u][:], at[u][:], over(consts["rw_level"][:, d, 0, :], HQ), ALU.mult)
                        nc.vector.tensor_tensor(T[u][:], quad(b[:, 2, :]), over(consts["rw_level"][:, 1 - d, 0, :], HQ),
                                                ALU.mult)
                        dve.drain()
                        nc.vector.tensor_tensor(TT[u][:], TT[u][:], eye, ALU.add)
                        nc.vector.tensor_tensor(T[u][:], T[u][:], eye, ALU.add)
                    op = nc.vector.tensor_tensor(upto[u][:], v[:, :, 1, :], over(consts["rw_from"][:, d, :], HQ), ALU.mult)
                elif p in level_t:
                    op = nc.vector.tensor_tensor(TT[u][:], TT[u][:], quad(b[:, 1, :]), ALU.add)
                else:
                    dve.wait_ge(stored[u], (t + 1) * (16 * STORES))
                    nc.vector.tensor_tensor(q_out[u][:], rT[u][:], quad(b[0:HEAD, 0, :]), ALU.add)
                    dve.wait_ge(sca[u].sem, sca[u].after(t, OUT))
                    op = nc.vector.tensor_tensor(m_out[u][:].rearrange("p (c h) t -> p c (h t)", c=2),
                                                 diag[u][:].rearrange("p (c h) t -> p c (h t)", c=2),
                                                 b[0:HEAD, 2:4, 0:HQ * HEAD], ALU.add)
                op.then_inc(vec[u].sem, 1)

            rounds(dve, lambda t, z, n: [phase(p, t, z, u) for p in vec[0].phases for u in range(2)])


def rwkv_states(nc, rw):
    with Stage(nc, "rwstate") as st:
        m = st.sb("m", [HEAD, 2, 2, 2, 4 * 2 * HEAD])
        n = st.sb("n", [HEAD, 2, 2, 2, 4 * 2 * HEAD])
        s = st.sb("s", [HEAD, 2, 2, 3, HEADS, HEAD])
        ps = st.psum("ps", [P, 2, 2, HEADS * HEAD])
        loaded = [st.sem(f"loaded{u}") for u in range(2)]
        stored = [st.sem(f"stored{u}") for u in range(2)]
        products, added = st.sem("products"), st.sem("added")
        block = st.block()

        def tile_of(d, r):
            return r if d == 0 else ((CTX_TILES - 1 - r) if r < CTX_TILES else TILES - 1 + CTX_TILES - r)

        @block.sync
        def _(sp):
            for r in range(TILES):
                u = r % 2
                if r >= 2:
                    sp.wait_ge(added, 2 * r - 1)
                for d in range(2):
                    for dst, name in ((m, "m_out"), (n, "n_out")):
                        sp.dma_start(dst[:, u, d], rw[name][d, tile_of(d, r)].rearrange("q k h v -> k q (h v)"))\
                            .then_inc(loaded[u], 16)

        @block.tensor
        def _(pe):
            for r in range(TILES):
                pe.wait_ge(loaded[r % 2], 64 * (r // 2 + 1))
                for c in range(2):
                    pe.wait_ge(added, 2 * r + c + 1)
                    for d in range(2):
                        part = c if d == 0 else 1 - c
                        for h in range(HEADS):
                            at = (part * 4 + h % 4) * HEAD
                            op = nc.tensor.matmul(ps[0:HEAD, c, d, h * HEAD:(h + 1) * HEAD],
                                                  m[:, r % 2, d, h // 4, at:at + HEAD],
                                                  s[:, r % 2, d, c, h, :], start=True, stop=True)
                    op.then_inc(products, 1)

        @block.vector
        def _(dve):
            nc.vector.memset(s[:, 0, :, 0], 0.0).then_inc(added, 1)
            for r in range(TILES):
                u = r % 2
                if r >= 2:
                    dve.wait_ge(stored[u], 32 * (r // 2))
                for c in range(2):
                    dve.wait_ge(products, 2 * r + c + 1)
                    if c == 1 and r >= 1:
                        dve.wait_ge(stored[1 - u], 32 * ((r - 1) // 2 + 1))
                    for d in range(2):
                        part = c if d == 0 else 1 - c
                        dst = s[:, u, d, 1] if c == 0 else s[:, 1 - u, d, 0]
                        for q in range(2):
                            op = nc.vector.tensor_tensor(
                                dst[:, 4 * q:4 * q + 4, :],
                                ps[0:HEAD, c, d, q * 4 * HEAD:(q + 1) * 4 * HEAD].rearrange("k (h v) -> k h v", h=4),
                                n[:, u, d, q].rearrange("k (c h v) -> k c h v", h=4, c=2)[:, part], ALU.add)
                    op.then_inc(added, 1)

        @block.scalar
        def _(act):
            for r in range(TILES):
                act.wait_ge(added, 2 * r + 2)
                for d in range(2):
                    act.dma_start(rw["s"][d, tile_of(d, r)], s[:, r % 2, d, 0:2]).then_inc(stored[r % 2], 16)
            for u in range(2):
                act.wait_ge(stored[u], 32 * (TILES // 2))


def rwkv_output(nc, consts, rw, par, mix):
    with Stage(nc, "rwout") as st:
        q = st.sb("q", [HEAD, 2, 2, HEADS, P])
        s = st.sb("s", [HEAD, 2, 2, 2, HEADS, HEAD])
        yo = st.sb("yo", [P, 2, 2, WID])
        y = st.sb("y", [P, 2, WID])
        sq = st.sb("sq", [P, WID])
        stat = st.sb("stat", [P, 2, 4, HEADS])
        ex = st.sb("ex", [P, 2, 2, QT, P])
        res = st.sb("res", [P, 2, QT, P])
        lnx = st.sb("lnx", [P, 2, QT])
        ps = st.psum("ps", [P, 2, 2, BANK])
        pt = st.psum("pt", [P, 2, BANK])
        once = st.sem("once")
        loaded = [st.sem(f"loaded{u}") for u in range(2)]
        stored = [st.sem(f"stored{u}") for u in range(2)]
        products, y_made, var_made, root_made = st.sem("products"), st.sem("y_made"), st.sem("var_made"), st.sem("root_made")
        turned, res_made = st.sem("turned"), st.sem("res_made")
        block = st.block()
        LOADS = 2 * (2 + 2 + 2) + 2

        @block.sync
        def _(sp):
            sp.dma_start(lnx[:, 0, :], column(par["lnx_g"])).then_inc(once, 16)
            sp.dma_start(lnx[:, 1, :], column(par["lnx_b"])).then_inc(once, 16)

            def body(i, u, r):
                sp.wait_ge(res_made, i + 1)
                t = bass.ds(i + CTX_TILES, 1)
                for d in range(2):
                    for g in range(2):
                        sp.dma_start(q[:, u, d, g * 4:g * 4 + 4, :],
                                     rw["q_out"][d, t, g].rearrange("o k h t -> (o k) h t")).then_inc(loaded[u], 16)
                        sp.dma_start(yo[:, u, d, g * 4 * HEAD:(g + 1) * 4 * HEAD],
                                     rw["y_out"][d, t, g].rearrange("o t h v -> (o t) (h v)")).then_inc(loaded[u], 16)
                    for c in range(2):
                        sp.dma_start(s[:, u, d, c], rw["s"][d, t, :, c if d == 0 else 1 - c]
                                     .rearrange("o k h v -> (o k) h v")).then_inc(loaded[u], 16)
                for j, name in enumerate(("bonus", "gate")):
                    sp.dma_start(ex[:, u, j], rw[name][:, bass.ds(i * P, P)].rearrange("(j p) t -> p j t", p=P))\
                        .then_inc(loaded[u], 16)

            steps(sp, LAT_TILES, 2, body)

        @block.tensor
        def _(pe):
            def body(i, u, r):
                pe.wait_ge(loaded[u], (r + 1) * (16 * LOADS))
                pe.wait_ge(y_made, i + 1)
                for h in range(HEADS):
                    for d in range(2):
                        op = nc.tensor.matmul(ps[:, u, h // 4, (h % 4) * P:(h % 4 + 1) * P], q[:, u, d, h, :],
                                              s[:, u, d, :, h, :], start=(d == 0), stop=(d == 1))
                op.then_inc(products, 1)
                pe.wait_ge(y_made, i + 3)
                pe.wait_ge(res_made, i + 1)
                for j in range(QT):
                    op = nc.tensor.transpose(pt[:, u, j * P:(j + 1) * P], y[:, u, j * P:(j + 1) * P], consts["ident"][:, :])
                op.then_inc(turned, 1)

            steps(pe, LAT_TILES, 2, body)

        @block.scalar
        def _(act):
            for u in range(2):
                act.sem_inc(stored[u], 16)

            def body(i, u, r):
                act.wait_ge(var_made, i + 1)
                nc.scalar.activation(stat[:, u, 2, :], stat[:, u, 1, :], ACT.Sqrt).then_inc(root_made, 1)
                act.wait_ge(res_made, i + 3)
                act.dma_start(mix[0:WID, bass.ds(i * P, P)].rearrange("(j p) t -> p j t", p=P), res[:, u])\
                    .then_inc(stored[u], 16)

            steps(act, LAT_TILES, 2, body)
            for u in range(2):
                act.wait_ge(stored[u], 16 * (LAT_TILES // 2 + 1))

        @block.vector
        def _(dve):
            dve.wait_ge(once, 32)
            dve.sem_inc(y_made, 2)
            dve.sem_inc(res_made, 2)

            def heads(ap):
                return ap.rearrange("p (h v) -> p h v", v=HEAD)

            def body(i, u, r):
                dve.wait_ge(loaded[u], (r + 1) * (16 * LOADS))
                yy = y[:, u, :]
                nc.vector.tensor_tensor(yo[:, u, 0, :], yo[:, u, 0, :], yo[:, u, 1, :], ALU.add)
                dve.drain()
                dve.wait_ge(products, i + 1)
                for c in range(2):
                    rows = slice(c * HEAD, (c + 1) * HEAD)
                    v = ps[rows, u].rearrange("t b (h c v) -> t (b h) c v", h=4, c=2)
                    nc.vector.tensor_tensor(heads(yy)[rows], v[:, :, c, :], heads(yo[rows, u, 0, :]), ALU.add)
                dve.drain()
                nc.vector.tensor_reduce(stat[:, u, 0, :], heads(yy), AX.X, ALU.add)
                dve.drain()
                nc.vector.tensor_scalar(stat[:, u, 0, :], stat[:, u, 0, :], 1.0 / HEAD, None, ALU.mult)
                dve.drain()
                nc.vector.tensor_tensor(heads(yy), heads(yy), last_of(stat[:, u, 0, :], HEAD), ALU.subtract)
                dve.drain()
                nc.vector.tensor_tensor(sq[:, :], yy, yy, ALU.mult)
                dve.drain()
                nc.vector.tensor_reduce(stat[:, u, 1, :], heads(sq[:, :]), AX.X, ALU.add)
                dve.drain()
                nc.vector.tensor_scalar(stat[:, u, 1, :], stat[:, u, 1, :], 1.0 / HEAD, RW_GN_EPS, ALU.mult, ALU.add)\
                    .then_inc(var_made, 1)
                dve.wait_ge(root_made, i + 1)
                nc.vector.reciprocal(stat[:, u, 3, :], stat[:, u, 2, :])
                dve.drain()
                nc.vector.tensor_tensor(heads(yy), heads(yy), last_of(stat[:, u, 3, :], HEAD), ALU.mult).then_inc(y_made, 1)
                dve.wait_ge(turned, i + 1)
                dve.wait_ge(stored[u], (r + 1) * 16)
                for j in range(QT):
                    nc.vector.tensor_scalar(res[:, u, j, :], pt[:, u, j * P:(j + 1) * P], lnx[:, 0, j:j + 1],
                                            lnx[:, 1, j:j + 1], ALU.mult, ALU.add)
                dve.drain()
                nc.vector.tensor_tensor(res[:, u], res[:, u], ex[:, u, 0], ALU.add)
                dve.drain()
                nc.vector.tensor_tensor(res[:, u], res[:, u], ex[:, u, 1], ALU.mult).then_inc(res_made, 1)

            steps(dve, LAT_TILES, 2, body)


def hgrn_prepare(nc, proj, par, hg):
    with Stage(nc, "hgprep") as st:
        q = st.sb("q", [P, 2, TOK])
        f = st.sb("f", [P, 2, 2, TOK])
        lb = st.sb("lb", [P, 2, 4, 2])
        reset = st.sb("reset", [P, TOK])
        kf = st.sb("kf", [P, 2, TOK])
        lf = st.sb("lf", [P, 2, TOK])
        cum = st.sb("cum", [P, 2, TOK])
        inc = st.sb("inc", [P, 2, TOK])
        dq = st.sb("dq", [P, 2, TOK])
        fac = st.sb("fac", [P, 2, 4, TOK])
        tot = st.sb("tot", [P, 2, HG_CHUNKS])
        loaded, in_used = [st.sem(f"loaded{u}") for u in range(2)], st.sem("in_used")
        lb_made = st.sem("lb_made")
        lb_ready, logs_ready, cums_ready, exps_ready = (st.sem("lb_ready"), st.sem("logs_ready"), st.sem("cums_ready"),
                                                      st.sem("exps_ready"))
        fac_ready, q_ready = st.sem("fac_ready"), st.sem("q_ready")
        stored = [st.sem(f"stored{d}") for d in range(2)]
        block = st.block()
        LOADS, STORES = 5, 5

        def by_chunk(ap):
            return ap.rearrange("p (c t) -> p c t", t=HG_CHUNK)

        @block.sync
        def _(sp):
            for d in range(2):
                sp.sem_inc(stored[d], 16 * STORES)

            def load(i, u):
                at = bass.ds(i * P, P)
                sp.wait_ge(in_used, i + 1)
                for dst, row in ((q[:, u, :], ROW_Q), (f[:, u, 0, :], ROW_FF), (f[:, u, 1, :], ROW_FB)):
                    sp.dma_start(dst, proj[bass.ds(i * P + row, P), :]).then_inc(loaded[u], 16)
                for layer in range(2):
                    sp.dma_start(lb[:, u, layer, :], par["lb"][:, layer, at].rearrange("d p -> p d")).then_inc(loaded[u], 16)

            def body(i, u, last=False):
                if not last:
                    load(i + 1, 1 - u)
                at = bass.ds(i * P, P)
                for d in range(2):
                    sp.wait_ge(fac_ready, i * 2 + d + 2)
                    for j, name in enumerate(("qs", "ks", "qc", "kh")):
                        sp.dma_start(hg[name][d, at, :], fac[:, d, j, :]).then_inc(stored[d], 16)
                    sp.dma_start(hg["tot"][d, at, :], tot[:, d, :]).then_inc(stored[d], 16)

            load(0, 0)
            with sp.Fori(0, QT // 2 - 1) as i:
                for u in range(2):
                    body(i * 2 + u, u)
            body(QT - 2, 0)
            body(QT - 1, 1, last=True)
            for d in range(2):
                sp.wait_ge(stored[d], 16 * STORES * (QT + 1))

        @block.scalar
        def _(act):
            def body(i, u, r):
                act.wait_ge(lb_ready, i + 1)
                nc.scalar.activation(lb[:, u, 2, :], lb[:, u, 2, :], ACT.Sigmoid).then_inc(q_ready, 1)
                nc.scalar.activation(q[:, u, :], q[:, u, :], ACT.Silu).then_inc(q_ready, 1)
                act.wait_ge(lb_made, i + 1)
                act.wait_ge(fac_ready, i * 2 + 1)
                for d in range(2):
                    nc.scalar.activation(kf[:, d, :], f[:, u, d, :], ACT.Sigmoid, scale=-1.0)
                    nc.scalar.activation(lf[:, d, :], f[:, u, d, :], ACT.Sigmoid)
                act.drain()
                for d in range(2):
                    nc.scalar.activation(lf[:, d, :], lf[:, d, :], ACT.Ln, scale=lb[:, u, 3, d:d + 1],
                                         bias=lb[:, u, 2, d:d + 1]).then_inc(logs_ready, 1)
                for d in range(2):
                    act.wait_ge(cums_ready, i * 2 + d + 1)
                    act.wait_ge(stored[d], (i + 1) * (16 * STORES))
                    nc.scalar.activation(fac[:, d, 0, :], dq[:, d, :], ACT.Exp)
                    nc.scalar.activation(fac[:, d, 1, :], dq[:, d, :], ACT.Exp, scale=-1.0)
                    nc.scalar.activation(fac[:, d, 2, :], inc[:, d, :], ACT.Exp)
                    nc.scalar.activation(fac[:, d, 3, :], lf[:, d, :], ACT.Exp)
                    nc.scalar.activation(tot[:, d, :], by_chunk(cum[:, d, :])[:, :, HG_CHUNK - 1], ACT.Exp)\
                        .then_inc(exps_ready, 1)

            steps(act, QT, 2, body)

        @block.vector
        def _(dve):
            nc.vector.memset(reset[:, :], 1.0)
            dve.drain()
            nc.vector.memset(by_chunk(reset[:, :])[:, :, 0:1], 0.0)
            dve.drain()
            dve.sem_inc(in_used, 2)
            dve.sem_inc(fac_ready, 1)

            def body(i, u, r):
                dve.wait_ge(loaded[u], (r + 1) * (16 * LOADS))
                nc.vector.tensor_tensor(lb[:, u, 2, :], lb[:, u, 0, :], lb[:, u, 1, :], ALU.subtract).then_inc(lb_ready, 1)
                dve.wait_ge(q_ready, i * 2 + 1)
                nc.vector.tensor_scalar(lb[:, u, 3, :], lb[:, u, 2, :], -1.0, 1.0, ALU.mult, ALU.add).then_inc(lb_made, 1)
                for d in range(2):
                    dve.wait_ge(logs_ready, i * 2 + d + 1)
                    nc.vector.tensor_scalar(kf[:, d, :], kf[:, d, :], lb[:, u, 3, d:d + 1], None, ALU.mult)
                    nc.vector.tensor_tensor_scan(cum[:, d, :], reset[:, :], lf[:, d, :], 0.0, ALU.mult, ALU.add)
                    dve.drain()
                    c, by = by_chunk(cum[:, d, :]), by_chunk(inc[:, d, :])
                    last = c[:, :, HG_CHUNK - 1:HG_CHUNK].broadcast_to([P, HG_CHUNKS, HG_CHUNK])
                    if d == 0:
                        nc.vector.tensor_copy(inc[:, d, :], cum[:, d, :])
                    else:
                        nc.vector.tensor_tensor(by, last, c, ALU.subtract)
                        dve.drain()
                        nc.vector.tensor_tensor(inc[:, d, :], inc[:, d, :], lf[:, d, :], ALU.add)
                    dve.drain()
                    mid = HG_CHUNK // 2 if d == 0 else HG_CHUNK // 2 - 1
                    nc.vector.tensor_tensor(by_chunk(lf[:, d, :]), last, by, ALU.subtract)
                    nc.vector.tensor_tensor(by_chunk(dq[:, d, :]), by, by[:, :, mid:mid + 1]
                                            .broadcast_to([P, HG_CHUNKS, HG_CHUNK]), ALU.subtract).then_inc(cums_ready, 1)
                dve.wait_ge(q_ready, i * 2 + 2)
                for d in range(2):
                    dve.wait_ge(exps_ready, i * 2 + d + 1)
                    g = [fac[:, d, j, :] for j in range(4)]
                    nc.vector.scalar_tensor_tensor(g[0], q[:, u, :], HEAD ** -0.5, g[0], ALU.mult, ALU.mult)
                    nc.vector.tensor_tensor(g[1], kf[:, d, :], g[1], ALU.mult)
                    nc.vector.scalar_tensor_tensor(g[2], q[:, u, :], HEAD ** -0.5, g[2], ALU.mult, ALU.mult)
                    nc.vector.tensor_tensor(g[3], kf[:, d, :], g[3], ALU.mult).then_inc(fac_ready, 1)
                dve.drain()
                dve.sem_inc(in_used, 1)

            steps(dve, QT, 2, body)


def hgrn_scan(nc, consts, proj, hg):
    NC = P // HG_CHUNK
    with Stage(nc, "hgscan") as st:
        def pair(name, shape):
            return [st.sb(f"{name}{d}", shape) for d in range(2)]

        flat = pair("flat", [P, 2, QT, P])
        qk = pair("qk", [HEAD, 3, HEADS, P])
        tot = pair("tot", [HEAD, HEADS, NC])
        kv_t = pair("kv_t", [P, 2, HEADS, HEAD])
        sc = pair("sc", [P, HEADS, P])
        s = pair("s", [HEAD, NC + 1, HEADS, HEAD])
        o = pair("o", [P, HEADS, HEAD])
        ps = st.psum("ps", [P, 8, BANK])
        loaded = [st.sem(f"loaded{d}") for d in range(2)]
        stored = [st.sem(f"stored{d}") for d in range(2)]
        turned, copied, kv_ready, state_ready = st.sem("turned"), st.sem("copied"), st.sem("kv_ready"), st.sem("state_ready")
        sc_ready, sc_used, o_ready, within, o_used = (st.sem("sc_ready"), st.sem("sc_used"), st.sem("o_ready"),
                                                      st.sem("within"), st.sem("o_used"))
        block = st.block()
        LOADS = 2 + 3 + 1

        def rounds(eng, body):
            for r in range(CTX_TILES):
                for d in range(2):
                    body(2 * r + d, r, d, r if d == 0 else CTX_TILES - 1 - r, False, r + d)

            def latents(i, last=False):
                for d in range(2):
                    r = i + CTX_TILES
                    body(i * 2 + (2 * CTX_TILES + d), r, d, r if d == 0 else i * -1 + (TILES - 1), True,
                         None if last and d == 1 else r + d)

            with eng.Fori(0, LAT_TILES - 1) as i:
                latents(i)
            latents(LAT_TILES - 1, last=True)

        def quarter(d, c):
            return c if d == 0 else NC - 1 - c

        @block.sync
        def _(sp):
            def body(n, r, d, t, out, nxt):
                tk = bass.ds(t * P, P)
                sp.wait_ge(o_used, n + 1)
                sp.dma_start(flat[d][:, 0], hg["kh"][d, :, tk].rearrange("(g p) t -> p g t", p=P)).then_inc(loaded[d], 16)
                sp.dma_start(flat[d][:, 1], proj[ROW_I:ROW_I + WID, tk].rearrange("(g p) t -> p g t", p=P))\
                    .then_inc(loaded[d], 16)
                for j, name in enumerate(("qs", "ks", "qc")):
                    sp.dma_start(qk[d][:, j], hg[name][d, :, tk].rearrange("(h k) t -> k h t", k=HEAD))\
                        .then_inc(loaded[d], 16)
                sp.dma_start(tot[d][:], hg["tot"][d, :, bass.ds(t * NC, NC)].rearrange("(h k) c -> k h c", k=HEAD))\
                    .then_inc(loaded[d], 16)

            rounds(sp, body)

        @block.tensor
        def _(pe):
            def start(n, r, d):
                pe.wait_ge(loaded[d], (r + 1) * (16 * LOADS))
                if not isinstance(n, int) or n >= 1:
                    pe.wait_ge(within, n)
                for j in range(2):
                    for g in range(QT):
                        op = nc.tensor.transpose(ps[:, j, g * P:(g + 1) * P], flat[d][:, j, g, :], consts["ident"][:, :])
                op.then_inc(turned, 1)
                for h in range(HEADS):
                    op = nc.tensor.matmul(ps[:, 6 + h // 4, (h % 4) * P:(h % 4 + 1) * P], qk[d][:, 1, h, :],
                                          qk[d][:, 0, h, :], start=True, stop=True)
                op.then_inc(sc_ready, 1)

            def body(n, r, d, t, out, nxt):
                pe.wait_ge(copied, n + 1)
                pe.wait_ge(o_used, n + 2)
                for c in range(NC):
                    w = quarter(d, c)
                    rows = slice(w * HG_CHUNK, (w + 1) * HG_CHUNK)
                    for h in range(HEADS):
                        op = nc.tensor.matmul(ps[0:HEAD, 2 + c, h * HEAD:(h + 1) * HEAD], kv_t[d][rows, 0, h, :],
                                              kv_t[d][rows, 1, h, :], start=True, stop=True,
                                              tile_position=(w * HG_CHUNK, 0))
                op.then_inc(kv_ready, 1)
                pe.wait_ge(sc_used, n + 1)
                if out:
                    for h in range(HEADS):
                        op = nc.tensor.matmul(ps[:, 0, h * HEAD:(h + 1) * HEAD], sc[d][:, h, :], kv_t[d][:, 1, h, :],
                                              start=True, stop=True)
                    op.then_inc(o_ready, 1)
                else:
                    pe.sem_inc(o_ready, 1)
                if nxt is not None:
                    start(n + 1, nxt, 1 - d)
                pe.wait_ge(state_ready, n + 1)
                if out:
                    for h in range(HEADS):
                        op = nc.tensor.matmul(ps[:, 2 + h // 2, (h % 2) * 4 * HEAD:(h % 2 + 1) * 4 * HEAD],
                                              qk[d][:, 2, h, :], s[d][:, 0:NC, h, :], start=True, stop=True)
                    op.then_inc(o_ready, 1)
                else:
                    pe.sem_inc(o_ready, 1)

            start(0, 0, 0)
            rounds(pe, body)

        @block.scalar
        def _(act):
            for d in range(2):
                act.sem_inc(stored[d], 16)

            def start(n, d):
                act.wait_ge(turned, n + 1)
                nc.scalar.copy(kv_t[d][:].rearrange("p j h k -> p j (h k)"), ps[:, 0:2, :]).then_inc(copied, 1)

            def body(n, r, d, t, out, nxt):
                act.wait_ge(o_ready, n * 2 + 1)
                if out:
                    act.wait_ge(stored[d], (r + (1 - CTX_TILES)) * 16)
                    nc.scalar.copy(o[d][:].rearrange("p h v -> p (h v)"), ps[:, 0, :]).then_inc(within, 1)
                else:
                    act.sem_inc(within, 1)
                if nxt is not None:
                    start(n + 1, 1 - d)
                if out:
                    act.wait_ge(o_used, n + 3)
                    act.dma_start(hg["o"][d, bass.ds(t * P - CTX, P), :], o[d][:].rearrange("p h v -> p (h v)"))\
                        .then_inc(stored[d], 16)

            start(0, 0)
            rounds(act, body)
            for d in range(2):
                act.wait_ge(stored[d], 16 * (LAT_TILES + 1))

        @block.vector
        def _(dve):
            for d in range(2):
                nc.vector.memset(s[d][:, 0], 0.0)
            dve.drain()
            dve.sem_inc(o_used, 2)

            def start(n, d):
                dve.wait_ge(sc_ready, n + 1)
                for g in range(2):
                    op = nc.vector.tensor_tensor(sc[d][:, 4 * g:4 * g + 4, :],
                                                 ps[:, 6 + g, :].rearrange("p (h t) -> p h t", h=4),
                                                 over(consts["hg_from"][:, d, :], 4), ALU.mult)
                op.then_inc(sc_used, 1)

            def body(n, r, d, t, out, nxt):
                dve.wait_ge(kv_ready, n + 1)
                for c in range(NC):
                    nc.vector.tensor_tensor(s[d][:, c + 1], s[d][:, c], tot[d][:, :, quarter(d, c):quarter(d, c) + 1]
                                            .broadcast_to([HEAD, HEADS, HEAD]), ALU.mult)
                    dve.drain()
                    op = nc.vector.tensor_tensor(s[d][:, c + 1], s[d][:, c + 1],
                                                 ps[0:HEAD, 2 + c, :].rearrange("k (h v) -> k h v", h=HEADS), ALU.add)
                    if c < NC - 1:
                        dve.drain()
                op.then_inc(state_ready, 1)
                if nxt is not None:
                    start(n + 1, 1 - d)
                dve.wait_ge(o_ready, n * 2 + 2)
                dve.wait_ge(within, n + 1)
                if out:
                    for c in range(NC):
                        w = quarter(d, c)
                        rows = slice(w * HG_CHUNK, (w + 1) * HG_CHUNK)
                        v = ps[rows, 2:6, :].rearrange("t b (h c v) -> t (b h) c v", h=2, c=NC)
                        nc.vector.tensor_tensor(o[d][rows], o[d][rows], v[:, :, c, :], ALU.add)
                nc.vector.tensor_copy(s[d][:, 0], s[d][:, NC])
                dve.drain()
                dve.sem_inc(o_used, 1)

            start(0, 0)
            rounds(dve, body)


def hgrn_output(nc, consts, proj, hg, par, mix):
    with Stage(nc, "hgout") as st:
        o = st.sb("o", [P, 2, 2, WID])
        g = st.sb("g", [P, 2, QT, P])
        sq = st.sb("sq", [P, WID])
        stat = st.sb("stat", [P, 2, 3, HEADS])
        ng = st.sb("ng", [P, 1])
        res = st.sb("res", [P, 2, QT, P])
        pt = st.psum("pt", [P, 2, BANK])
        once = st.sem("once")
        loaded = [st.sem(f"loaded{u}") for u in range(2)]
        stored = [st.sem(f"stored{u}") for u in range(2)]
        var_made, root_made, o_made, turned, res_made = (st.sem("var_made"), st.sem("root_made"), st.sem("o_made"),
                                                         st.sem("turned"), st.sem("res_made"))
        block = st.block()

        @block.sync
        def _(sp):
            for h in range(2):
                sp.dma_start(ng[h * HEAD:(h + 1) * HEAD, :], par["norm_g"].rearrange("(p o) -> p o", o=1))\
                    .then_inc(once, 16)

            def body(i, u, r):
                sp.wait_ge(res_made, i + 1)
                for d in range(2):
                    sp.dma_start(o[:, u, d, :], hg["o"][d, bass.ds(i * P, P), :]).then_inc(loaded[u], 16)
                sp.dma_start(g[:, u], proj[ROW_G:ROW_G + WID, bass.ds(i * P + CTX, P)]
                             .rearrange("(j p) t -> p j t", p=P)).then_inc(loaded[u], 16)

            steps(sp, LAT_TILES, 2, body)

        @block.tensor
        def _(pe):
            def body(i, u, r):
                pe.wait_ge(o_made, i + 1)
                pe.wait_ge(res_made, i + 1)
                for j in range(QT):
                    op = nc.tensor.transpose(pt[:, u, j * P:(j + 1) * P], o[:, u, 0, j * P:(j + 1) * P],
                                             consts["ident"][:, :])
                op.then_inc(turned, 1)

            steps(pe, LAT_TILES, 2, body)

        @block.scalar
        def _(act):
            for u in range(2):
                act.sem_inc(stored[u], 16)

            def body(i, u, r):
                act.wait_ge(var_made, i + 1)
                nc.scalar.activation(stat[:, u, 1, :], stat[:, u, 0, :], ACT.Sqrt)
                nc.scalar.activation(g[:, u], g[:, u], ACT.Silu).then_inc(root_made, 1)
                act.wait_ge(res_made, i + 3)
                act.dma_start(mix[WID:2 * WID, bass.ds(i * P, P)].rearrange("(j p) t -> p j t", p=P), res[:, u])\
                    .then_inc(stored[u], 16)

            steps(act, LAT_TILES, 2, body)
            for u in range(2):
                act.wait_ge(stored[u], 16 * (LAT_TILES // 2 + 1))

        @block.vector
        def _(dve):
            dve.wait_ge(once, 32)
            dve.sem_inc(res_made, 2)

            def heads(ap):
                return ap.rearrange("p (h v) -> p h v", v=HEAD)

            def body(i, u, r):
                dve.wait_ge(loaded[u], (r + 1) * 48)
                oo = o[:, u, 0, :]
                nc.vector.tensor_tensor(oo, oo, o[:, u, 1, :], ALU.add)
                dve.drain()
                nc.vector.tensor_tensor(sq[:, :], oo, oo, ALU.mult)
                dve.drain()
                nc.vector.tensor_reduce(stat[:, u, 0, :], heads(sq[:, :]), AX.X, ALU.add)
                dve.drain()
                nc.vector.tensor_scalar(stat[:, u, 0, :], stat[:, u, 0, :], 1.0 / HEAD, EPS, ALU.mult, ALU.add)\
                    .then_inc(var_made, 1)
                dve.wait_ge(root_made, i + 1)
                nc.vector.reciprocal(stat[:, u, 2, :], stat[:, u, 1, :])
                dve.drain()
                nc.vector.tensor_tensor(heads(oo), heads(oo), last_of(stat[:, u, 2, :], HEAD), ALU.mult).then_inc(o_made, 1)
                dve.wait_ge(turned, i + 1)
                dve.wait_ge(stored[u], (r + 1) * 16)
                nc.vector.scalar_tensor_tensor(res[:, u].rearrange("p j t -> p (j t)"), pt[:, u, :], ng[:, 0:1],
                                               g[:, u].rearrange("p j t -> p (j t)"), ALU.mult, ALU.mult)\
                    .then_inc(res_made, 1)

            steps(dve, LAT_TILES, 2, body)


def linear_tokens(nc, name, act, w, resid, out, gain=None):
    K = w.shape[0]
    KT = K // P
    with Stage(nc, name) as st:
        wt = st.sb("w", [P, KT, D])
        a = st.sb("a", [P, 2, KT, P])
        x = st.sb("x", [P, 2, D])
        res = st.sb("res", [P, 2, D])
        g = st.sb("g", [P, D])
        ps = st.psum("ps", [P, 2, 2, BANK])
        once = st.sem("once")
        PARTS = 4
        w_loaded = [st.sem(f"w_loaded{h}") for h in range(PARTS)]
        loaded = [st.sem(f"loaded{u}") for u in range(2)]
        stored = [st.sem(f"stored{u}") for u in range(2)]
        products, used = st.sem("products"), st.sem("used")
        block = st.block()
        @block.sync
        def _(sp):
            def body(i, u, r):
                sp.wait_ge(used, i + 1)
                sp.dma_start(a[:, u], act[:, bass.ds(i * P, P)].rearrange("(k p) t -> p k t", p=P)).then_inc(loaded[u], 16)
                sp.dma_start(x[:, u, :], resid[bass.ds(i * P, P), :]).then_inc(loaded[u], 16)

            steps(sp, LAT_TILES, 2, body)

        @block.tensor
        def _(pe):
            def body(i, u, r):
                pe.wait_ge(loaded[u], (r + 1) * 32)
                pe.wait_ge(used, i + 1)
                for n in range(2):
                    for k in range(KT):
                        if isinstance(i, int) and i == 0 and n == 0 and k % (KT // PARTS) == 0:
                            pe.wait_ge(w_loaded[k // (KT // PARTS)], 16)
                        op = nc.tensor.matmul(ps[:, u, n, :], a[:, u, k, :], wt[:, k, n * BANK:(n + 1) * BANK],
                                              start=(k == 0), stop=(k == KT - 1))
                op.then_inc(products, 1)

            for u in range(2):
                body(u, u, 0)
            with pe.Fori(1, LAT_TILES // 2) as i:
                for u in range(2):
                    body(i * 2 + u, u, i)

        @block.vector
        def _(dve):
            dve.sem_inc(used, 2)
            if gain is not None:
                dve.wait_ge(once, 16)

            def body(i, u, r):
                dve.wait_ge(products, i + 1)
                dve.wait_ge(stored[u], (r + 1) * 16)
                y = ps[:, u].rearrange("p b n -> p (b n)")
                if gain is not None:
                    nc.vector.tensor_tensor(res[:, u, :], y, g[:, :], ALU.mult)
                    dve.drain()
                    y = res[:, u, :]
                nc.vector.tensor_tensor(res[:, u, :], y, x[:, u, :], ALU.add).then_inc(used, 1)

            steps(dve, LAT_TILES, 2, body)

        @block.scalar
        def _(act_e):
            for h in range(PARTS):
                act_e.dma_start(wt[:, h * KT // PARTS:(h + 1) * KT // PARTS, :],
                                w[h * K // PARTS:(h + 1) * K // PARTS, :].rearrange("(k p) n -> p k n", p=P))\
                    .then_inc(w_loaded[h], 16)
            if gain is not None:
                act_e.dma_start(g[:, :], gain.broadcast_to([P, D])).then_inc(once, 16)
            for u in range(2):
                act_e.sem_inc(stored[u], 16)

            def body(i, u, r):
                act_e.wait_ge(used, i + 3)
                act_e.dma_start(out[bass.ds(i * P, P), :], res[:, u, :]).then_inc(stored[u], 16)

            steps(act_e, LAT_TILES, 2, body)
            for u in range(2):
                act_e.wait_ge(stored[u], 16 * (LAT_TILES // 2 + 1))


def route(nc, h2, router_w, router_b, gates, chosen):
    GE = N_EXPERTS // N_GROUPS
    with Stage(nc, "route") as st:
        w = st.sb("w", [P, KD, N_EXPERTS])
        bias = st.sb("bias", [P, N_EXPERTS])
        score = st.sb("score", [P, 2, N_EXPERTS])
        sel = st.sb("sel", [P, N_EXPERTS])
        best = st.sb("best", [P, N_GROUPS, 8])
        grp = st.sb("grp", [P, 4, N_GROUPS])
        top = st.sb("top", [P, 8])
        left = st.sb("left", [P, N_EXPERTS])
        tot = st.sb("tot", [P, 2])
        ps = st.psum("ps", [P, 2, BANK])
        once, products, scored, used = st.sem("once"), st.sem("products"), st.sem("scored"), st.sem("used")
        block = st.block()
        GONE = -1e30

        @block.sync
        def _(sp):
            sp.dma_start(w[:], router_w.rearrange("(k p) e -> p k e", p=P)).then_inc(once, 16)
            sp.dma_start(bias[:, :], router_b.rearrange("(o e) -> o e", o=1).broadcast_to([P, N_EXPERTS])).then_inc(once, 16)

        @block.tensor
        def _(pe):
            pe.wait_ge(once, 32)
            for t in range(LAT_TILES):
                if t >= 2:
                    pe.wait_ge(scored, t - 1)
                for k in range(KD):
                    op = nc.tensor.matmul(ps[:, t % 2, 0:N_EXPERTS], h2[:, k, t * P:(t + 1) * P], w[:, k, :],
                                          start=(k == 0), stop=(k == KD - 1))
                op.then_inc(products, 1)

        @block.scalar
        def _(act):
            for t in range(LAT_TILES):
                act.wait_ge(products, t + 1)
                if t >= 2:
                    act.wait_ge(used, t - 1)
                nc.scalar.activation(score[:, t % 2, :], ps[:, t % 2, 0:N_EXPERTS], ACT.Sigmoid).then_inc(scored, 1)

        @block.vector
        def _(dve):
            dve.wait_ge(once, 32)

            def body(t, u, r):
                sc = score[:, u, :]
                dve.wait_ge(scored, t + 1)
                nc.vector.tensor_tensor(sel[:, :], sc, bias[:, :], ALU.add)
                dve.drain()
                for g in range(N_GROUPS):
                    nc.vector.max(best[:, g, :], sel[:, g * GE:(g + 1) * GE])
                dve.drain()
                nc.vector.tensor_tensor(grp[:, 0, :], best[:, :, 0], best[:, :, 1], ALU.add)
                dve.drain()
                nc.vector.max(top[:, :], grp[:, 0, :])
                dve.drain()
                nc.vector.memset(top[:, TOPK_GROUPS:], 1e30)
                dve.drain()
                nc.vector.match_replace(grp[:, 1, :], top[:, :], grp[:, 0, :], GONE)
                dve.drain()
                nc.vector.tensor_tensor(grp[:, 2, :], grp[:, 1, :], grp[:, 0, :], ALU.is_equal)
                dve.drain()
                nc.vector.tensor_scalar(grp[:, 3, :], grp[:, 2, :], GONE, None, ALU.mult)
                dve.drain()
                nc.vector.tensor_tensor(sel[:, :].rearrange("p (g e) -> p g e", e=GE),
                                        sel[:, :].rearrange("p (g e) -> p g e", e=GE),
                                        last_of(grp[:, 3, :], GE), ALU.add)
                dve.drain()
                nc.vector.max(top[:, :], sel[:, :])
                dve.drain()
                nc.vector.match_replace(left[:, :], top[:, :], sel[:, :], 2 * GONE)
                dve.drain()
                nc.vector.tensor_tensor(chosen[:, t, :], left[:, :], sel[:, :], ALU.not_equal)
                dve.drain()
                nc.vector.tensor_tensor(left[:, :], chosen[:, t, :], sc, ALU.mult).then_inc(used, 1)
                dve.drain()
                nc.vector.reduce_sum(tot[:, 0:1], left[:, :], axis=AX.X)
                dve.drain()
                nc.vector.reciprocal(tot[:, 1:2], tot[:, 0:1])
                dve.drain()
                nc.vector.tensor_scalar(gates[:, t, :], left[:, :], tot[:, 1:2], ROUTE_SCALE, ALU.mult, ALU.mult)
                dve.drain()

            for t in range(LAT_TILES):
                body(t, t % 2, t // 2)


def shared_expert(nc, h2, acc, wg, wu, wdn):
    MT = D_EXPERT // P
    with Stage(nc, "shared") as st:
        wgu = st.sb("wgu", [P, 2, KD, D_EXPERT])
        wd = st.sb("wd", [P, MT, D])
        sg = st.sb("sg", [P, 2, BANK])
        hid = st.sb("hid", [P, MT, SEQ])
        pgu = st.psum("pgu", [P, 2, 2, BANK])
        pd = st.psum("pd", [P, 4, BANK])
        loaded, gu_ready, sg_ready, hid_ready, y_ready, y_used = (
            st.sem(n) for n in ("loaded", "gu_ready", "sg_ready", "hid_ready", "y_ready", "y_used"))
        block = st.block()
        PARTS = MT * (SEQ // BANK)
        DOWN = LAT_TILES * (D // BANK)

        @block.sync
        def _(sp):
            for j, src in enumerate((wg, wu)):
                sp.dma_start(wgu[:, j], src.rearrange("(k p) m -> p k m", p=P)).then_inc(loaded, 16)
            sp.dma_start(wd[:], wdn.rearrange("(k p) m -> p k m", p=P)).then_inc(loaded, 16)

        @block.tensor
        def _(pe):
            pe.wait_ge(loaded, 48)
            for c in range(PARTS):
                m, h = c // 2, c % 2
                if c >= 2:
                    pe.wait_ge(hid_ready, c - 1)
                for j in range(2):
                    for k in range(KD):
                        op = nc.tensor.matmul(pgu[:, c % 2, j, :], wgu[:, j, k, m * P:(m + 1) * P],
                                              h2[:, k, h * BANK:(h + 1) * BANK], start=(k == 0), stop=(k == KD - 1))
                op.then_inc(gu_ready, 1)
            pe.wait_ge(hid_ready, PARTS)
            for c in range(DOWN):
                t, h = c // 2, c % 2
                if c >= 4:
                    pe.wait_ge(y_used, c - 3)
                for k in range(MT):
                    op = nc.tensor.matmul(pd[:, c % 4, :], hid[:, k, t * P:(t + 1) * P],
                                          wd[:, k, h * BANK:(h + 1) * BANK], start=(k == 0), stop=(k == MT - 1))
                op.then_inc(y_ready, 1)

        @block.scalar
        def _(act):
            for c in range(PARTS):
                act.wait_ge(gu_ready, c + 1)
                if c >= 2:
                    act.wait_ge(hid_ready, c - 1)
                nc.scalar.activation(sg[:, c % 2, :], pgu[:, c % 2, 0, :], ACT.Silu).then_inc(sg_ready, 1)

        @block.vector
        def _(dve):
            for c in range(PARTS):
                m, h = c // 2, c % 2
                dve.wait_ge(sg_ready, c + 1)
                nc.vector.tensor_tensor(hid[:, m, h * BANK:(h + 1) * BANK], sg[:, c % 2, :], pgu[:, c % 2, 1, :],
                                        ALU.mult).then_inc(hid_ready, 1)
            for c in range(DOWN):
                t, h = c // 2, c % 2
                dve.wait_ge(y_ready, c + 1)
                nc.vector.tensor_copy(acc[:, t, h * BANK:(h + 1) * BANK], pd[:, c % 4, :]).then_inc(y_used, 1)


MAX_BLOCKS = SEQ * TOP_K // P + N_EXPERTS


def dispatch(nc, consts, gates, chosen, tb):
    BIG = float(1 << 20)
    NE = N_EXPERTS
    T8 = SEQ // P
    with Stage(nc, "dispatch") as st:
        before = st.sb("before", [P, P])
        pos = st.sb("pos", [P, T8, NE])
        cnt = st.sb("cnt", [P, NE])
        nb = st.sb("nb", [P, NE])
        cmp = st.sb("cmp", [P, NE])
        end = st.sb("end", [P, NE])
        start = st.sb("start", [P, NE])
        one = st.sb("one", [P, NE])
        rank = st.sb("rank", [P, T8, NE])
        tok = st.sb("tok", [P, T8])
        own = st.sb("own", [P, 2])
        ps = st.psum("ps", [P, 2, BANK])
        pt = st.psum("pt", [P, BANK])
        ready, counted, own_made, turned = st.sem("ready"), st.sem("counted"), st.sem("own_made"), st.sem("turned")
        iotas = st.sem("iotas")
        block = st.block()
        info = tb["info"]

        @block.gpsimd
        def _(pool):
            nc.gpsimd.iota(tok[:, :], [[P, T8]], base=0, channel_multiplier=1, allow_small_or_imprecise_dtypes=True)
            nc.gpsimd.iota(tb["slot"][:, :], [[1, P]], base=0, channel_multiplier=0, allow_small_or_imprecise_dtypes=True)
            nc.gpsimd.iota(tb["lane"][:, 0:1], [[0, 1]], base=0, channel_multiplier=1,
                           allow_small_or_imprecise_dtypes=True).then_inc(iotas, 1)

        @block.tensor
        def _(pe):
            pe.wait_ge(ready, 1)
            for t in range(T8):
                out = ps[:, 0, t * NE:(t + 1) * NE]
                for b in range(t):
                    nc.tensor.matmul(out, consts["ones"][:, :], chosen[:, b, :], start=(b == 0), stop=False)
                nc.tensor.matmul(out, before[:, :], chosen[:, t, :], start=(t == 0), stop=True)
            for b in range(T8):
                op = nc.tensor.matmul(ps[:, 1, 0:NE], consts["ones"][:, :], chosen[:, b, :], start=(b == 0), stop=(b == T8 - 1))
            op.then_inc(counted, 1)
            pe.wait_ge(own_made, 1)
            nc.tensor.transpose(pt[0:1, 0:P], own[:, 0:1], consts["ident"][:, :]).then_inc(turned, 1)

        @block.vector
        def _(dve):
            nc.vector.tensor_tensor(before[:, :], consts["upto"][:, :], consts["ident"][:, :], ALU.subtract)
            nc.vector.memset(one[:, :], 1.0)
            nc.vector.memset(nb[:, :], 0.0)
            dve.drain()
            dve.sem_inc(ready, 1)
            dve.wait_ge(iotas, 1)
            for t in range(T8):
                nc.vector.tensor_tensor_scan(rank[:, t, :], one[:, :], chosen[:, t, :], 0.0, ALU.mult, ALU.add)
            dve.drain()
            nc.vector.tensor_tensor(rank[:], rank[:], chosen[:], ALU.subtract)
            dve.drain()
            nc.vector.tensor_scalar(rank[:], rank[:], float(SEQ), None, ALU.mult)
            nc.vector.memset(info[:, :, :, 3], 1.0)
            nc.vector.tensor_copy(info[:, :, :, 2], gates[:])
            dve.drain()
            nc.vector.tensor_tensor(info[:, :, :, 1], rank[:], last_of(tok[:, :], NE), ALU.add)
            nc.vector.tensor_scalar(rank[:], rank[:], 0.0, None, ALU.mult)
            dve.drain()
            nc.vector.tensor_tensor(info[:, :, :, 0], rank[:], last_of(tok[:, :], NE), ALU.add)
            dve.wait_ge(counted, 1)
            nc.vector.tensor_copy(cnt[:, :], ps[:, 1, 0:NE])
            for k in range(SEQ // P):
                dve.drain()
                nc.vector.tensor_scalar(cmp[:, :], cnt[:, :], float(k * P) + 0.5, None, ALU.is_gt)
                dve.drain()
                nc.vector.tensor_tensor(nb[:, :], nb[:, :], cmp[:, :], ALU.add)
            dve.drain()
            nc.vector.tensor_tensor_scan(end[:, :], one[:, :], nb[:, :], 0.0, ALU.mult, ALU.add)
            dve.drain()
            nc.vector.tensor_tensor(start[:, :], end[:, :], nb[:, :], ALU.subtract)
            nc.vector.tensor_scalar(cmp[:, :], end[:, :], tb["lane"][:, 0:1], None, ALU.is_le)
            dve.drain()
            nc.vector.reduce_sum(own[:, 1:2], cmp[:, :], axis=AX.X)
            nc.vector.tensor_copy(tb["start"][0:1, :], start[0:1, :])
            dve.drain()
            nc.vector.tensor_scalar(start[:, :], start[:, :], float(P), BIG, ALU.mult, ALU.add)
            dve.drain()
            nc.vector.tensor_scalar(own[:, 0:1], own[:, 1:2], float(NE - 1), None, ALU.min).then_inc(own_made, 1)
            nc.vector.tensor_tensor(pos[:], ps[:, 0, :].rearrange("p (t e) -> p t e", t=T8), over(start[:, :], T8), ALU.add)
            dve.drain()
            nc.vector.tensor_tensor(pos[:], pos[:], chosen[:], ALU.mult)
            dve.drain()
            nc.vector.tensor_scalar(tb["place"][:], pos[:], -BIG, None, ALU.add)
            nc.vector.tensor_scalar(tb["lane"][:, 1:2], tb["lane"][:, 0:1], float(SEQ * TOP_K), None, ALU.add)
            dve.drain()
            nc.vector.tensor_scalar(tb["lane"][:, 2:3], tb["lane"][:, 1:2], -1.0, None, ALU.mult)
            dve.wait_ge(turned, 1)
            nc.vector.tensor_copy(tb["owner"][0:1, 0:MAX_BLOCKS], pt[0:1, 0:P])
            nc.vector.memset(tb["owner"][0:1, MAX_BLOCKS:], N_EXPERTS - 1)
            dve.drain()


def routed_experts(nc, consts, yn, scale, bias, tb, routed, results):
    T8 = SEQ // P
    NB = MAX_BLOCKS
    MT = D_EXPERT // P
    WS = 4
    BS = 4
    with Stage(nc, "routed") as st:
        wgu = st.sb("wgu", [P, WS, KD, 2, D_EXPERT])
        wd = st.sb("wd", [P, WS, MT, D])
        rel = st.sb("rel", [P, T8])
        base = st.sb("base", [P, 1])
        hot = st.sb("hot", [P, T8, P])
        rows = st.sb("rows", [P, BS, 4])
        srow = st.sb("srow", [P, 1])
        yrow = st.sb("yrow", [P, BS])
        idx = [st.sb(f"idx{b}", [P, 1], U32) for b in range(BS)]
        yidx = [st.sb(f"yidx{u}", [P, 1], U32) for u in range(2)]
        xg = st.sb("xg", [P, 2, D])
        xT = st.sb("xT", [P, 2, KD, P])
        sg = st.sb("sg", [P, D_EXPERT])
        hid = st.sb("hid", [P, D_EXPERT])
        hT = st.sb("hT", [P, MT, P])
        y = st.sb("y", [P, 2, D])
        p_row = st.psum("p_row", [P, BANK])
        p_x = st.psum("p_x", [P, 2, BANK])
        p_gu = st.psum("p_gu", [P, BANK])
        p_h = st.psum("p_h", [P, BANK])
        p_y = st.psum("p_y", [P, 2, BANK])
        loaded = [st.sem(f"loaded{w}") for w in range(WS)]
        gathered = [st.sem(f"gathered{u}") for u in range(2)]
        scattered = [st.sem(f"scattered{u}") for u in range(2)]
        (hot_made, row_sums, idx_made, x_turned, xT_made, gu_ready, sg_made, hid_made, h_turned, hT_made, y_ready,
         y_made) = (st.sem(n) for n in ("hot_made", "row_sums", "idx_made", "x_turned", "xT_made", "gu_ready", "sg_made",
                                        "hid_made", "h_turned", "hT_made", "y_ready", "y_made"))
        gather_turn, scatter_turn = st.sem("gather_turn"), st.sem("scatter_turn")
        block = st.block()
        lane = tb["lane"]

        def turns(eng, body):
            for b in range(BS):
                body(b, b, 0)
            with eng.Fori(1, NB // BS) as i:
                for b in range(BS):
                    body(i * BS + b, b, i)

        def owner(eng, j):
            return eng.value_load(tb["owner"][0:1, bass.ds(j, 1)], min_val=0, max_val=N_EXPERTS - 1)

        def uses(r, b):
            return r * (BS // 2) + (b // 2 + 1)

        @block.sync
        def _(sp):
            def load(e, w):
                for j in range(2):
                    sp.dma_start(wgu[:, w, :, j, :], routed[j][bass.ds(e, 1)].rearrange("o (k p) m -> p (o k) m", p=P))\
                        .then_inc(loaded[w], 16)
                sp.dma_start(wd[:, w], routed[2][bass.ds(e, 1)].rearrange("o (k p) m -> p (o k) m", p=P))\
                    .then_inc(loaded[w], 16)

            for w in range(WS):
                if w:
                    sp.sem_inc(loaded[w], 16)
                load(w, w)
            with sp.Fori(1, N_EXPERTS // WS) as i:
                for w in range(WS):
                    first = sp.value_load(tb["start"][0:1, bass.ds(i * WS + (w - WS + 1), 1)], min_val=0, max_val=NB)
                    sp.wait_ge(y_ready, first + 1)
                    load(i * WS + w, w)

        @block.gpsimd
        def _(pool):
            def gather(j, b, r):
                pool.wait_ge(idx_made, j + 1)
                if not isinstance(j, int) or j >= 2:
                    pool.wait_ge(x_turned, j - 1)
                pool.sem_inc(gather_turn, 1)
                nc.gpsimd.indirect_dma_start(xg[:, b % 2, :], None, yn, bass.IndirectOffsetOnAxis(ap=idx[b][:, :], axis=0))\
                    .then_inc(gathered[b % 2], 16)

            def scatter(j, b, r):
                pool.wait_ge(y_made, j + 1)
                if not isinstance(j, int) or j >= 1:
                    pool.wait_ge(scattered[(b - 1) % 2], 16 * uses(r + (b - 1) // BS, (b - 1) % BS))
                pool.sem_inc(scatter_turn, 1)
                nc.gpsimd.indirect_dma_start(results, bass.IndirectOffsetOnAxis(ap=yidx[b % 2][:, :], axis=0),
                                             y[:, b % 2, :], None).then_inc(scattered[b % 2], 16)

            for b in range(3):
                gather(b, b, 0)

            def body(j, b, r):
                if not isinstance(j, int) or j >= 1:
                    scatter(j - 1, (b - 1) % BS, r + (b - 1) // BS)
                gather(j + 3, (b + 3) % BS, r + (b + 3) // BS)

            turns(pool, body)
            scatter(NB - 1, BS - 1, NB // BS - 1)
            for u in range(2):
                pool.wait_ge(scattered[u], 16 * (NB // 2))
                pool.wait_ge(gathered[u], 16 * (NB // 2 + 2 - u))

        @block.tensor
        def _(pe):
            def sums(j):
                e = owner(pe, j)
                pe.wait_ge(hot_made, j + 1)
                for t in range(T8):
                    op = nc.tensor.matmul(p_row[:, 0:4], hot[:, t, :], tb["info"][:, t, bass.ds(e, 1), :],
                                          start=(t == 0), stop=(t == T8 - 1))
                op.then_inc(row_sums, 1)

            def turn(j, b, r):
                pe.wait_ge(gathered[b % 2], 16 * uses(r, b))
                if not isinstance(j, int) or j >= 1:
                    pe.wait_ge(xT_made, j)
                for k in range(KD):
                    op = nc.tensor.transpose(p_x[:, k // 4, (k % 4) * P:(k % 4 + 1) * P], xg[:, b % 2, k * P:(k + 1) * P],
                                             consts["ident"][:, :])
                op.then_inc(x_turned, 1)

            def down(j):
                e = owner(pe, j)
                pe.wait_ge(hT_made, j + 1)
                if not isinstance(j, int) or j >= 1:
                    pe.wait_ge(y_made, j)
                for h in range(2):
                    for k in range(MT):
                        op = nc.tensor.matmul(p_y[:, h, :], hT[:, k, :], wd[:, bass.ds(e % WS, 1), k, h * BANK:(h + 1) * BANK],
                                              start=(k == 0), stop=(k == MT - 1))
                op.then_inc(y_ready, 1)

            pe.sem_inc(y_ready, 1)
            for j in range(3):
                sums(j)
            turn(0, 0, 0)

            def body(j, b, r):
                first = isinstance(j, int) and j == 0
                turn(j + 1, (b + 1) % BS, r + (b + 1) // BS)
                e = owner(pe, j)
                for w in range(WS):
                    pe.wait_ge(loaded[w], (e + (WS - w)) // WS * 48 + (16 if w else 0))
                pe.wait_ge(xT_made, j + 1)
                if not first:
                    pe.wait_ge(hid_made, j)
                for k in range(KD):
                    op = nc.tensor.matmul(p_gu[:, :], xT[:, b % 2, k, :], wgu[:, bass.ds(e % WS, 1), k, :, :],
                                          start=(k == 0), stop=(k == KD - 1))
                op.then_inc(gu_ready, 1)
                if not first:
                    down(j - 1)
                sums(j + 3)
                pe.wait_ge(hid_made, j + 1)
                if not first:
                    pe.wait_ge(hT_made, j)
                for k in range(MT):
                    op = nc.tensor.transpose(p_h[:, k * P:(k + 1) * P], hid[:, k * P:(k + 1) * P], consts["ident"][:, :])
                op.then_inc(h_turned, 1)

            turns(pe, body)
            down(NB - 1)

        @block.scalar
        def _(act):
            def columns(j, b):
                act.wait_ge(x_turned, j + 1)
                for k in range(KD):
                    op = nc.scalar.activation(xT[:, b % 2, k, :], p_x[:, k // 4, (k % 4) * P:(k % 4 + 1) * P], ACT.Identity,
                                              bias=bias[:, 0, k:k + 1], scale=scale[:, 0, k:k + 1])
                op.then_inc(xT_made, 1)

            columns(0, 0)

            def body(j, b, r):
                columns(j + 1, b + 1)
                act.wait_ge(gu_ready, j + 1)
                if not isinstance(j, int) or j >= 1:
                    act.wait_ge(hid_made, j)
                nc.scalar.activation(sg[:, :], p_gu[:, 0:D_EXPERT], ACT.Silu).then_inc(sg_made, 1)
                act.wait_ge(h_turned, j + 1)
                nc.scalar.copy(hT[:].rearrange("p m t -> p (m t)"), p_h[:, 0:MT * P]).then_inc(hT_made, 1)

            turns(act, body)

        @block.vector
        def _(dve):
            nc.vector.memset(base[:, :], 0.0)
            dve.drain()

            def one_hot(j):
                e = owner(dve, j)
                nc.vector.tensor_scalar(rel[:, :], tb["place"][:, :, bass.ds(e, 1)].rearrange("p t o -> p (t o)"),
                                        base[:, 0:1], None, ALU.subtract)
                dve.drain()
                nc.vector.tensor_scalar(base[:, :], base[:, :], float(P), None, ALU.add)
                nc.vector.tensor_tensor(hot[:], over(tb["slot"][:, :], T8), last_of(rel[:, :], P), ALU.is_equal)\
                    .then_inc(hot_made, 1)

            def indices(j, b):
                dve.wait_ge(row_sums, j + 1)
                nc.vector.tensor_copy(rows[:, b, :], p_row[:, 0:4])
                dve.drain()
                nc.vector.scalar_tensor_tensor(srow[:, :], rows[:, b, 3:4], lane[:, 2:3], rows[:, b, 1:2],
                                               ALU.mult, ALU.add)
                dve.drain()
                nc.vector.tensor_scalar(yrow[:, b:b + 1], srow[:, :], lane[:, 1:2], None, ALU.add)
                nc.vector.tensor_copy(idx[b][:, :], rows[:, b, 0:1]).then_inc(idx_made, 1)
                dve.drain()

            def result(j, b, r):
                if not isinstance(j, int) or j >= 2:
                    dve.wait_ge(scattered[b % 2], 16 * (uses(r, b) - 1))
                nc.vector.tensor_copy(yidx[b % 2][:, :], yrow[:, b:b + 1])
                dve.wait_ge(y_ready, j + 2)
                nc.vector.tensor_scalar(y[:, b % 2, :], p_y[:].rearrange("p h n -> p (h n)"), rows[:, b, 2:3], None,
                                        ALU.mult).then_inc(y_made, 1)
                dve.drain()

            for j in range(3):
                one_hot(j)
                indices(j, j)
            one_hot(3)

            def body(j, b, r):
                dve.wait_ge(sg_made, j + 1)
                nc.vector.tensor_tensor(hid[:, :], sg[:, :], p_gu[:, D_EXPERT:2 * D_EXPERT], ALU.mult).then_inc(hid_made, 1)
                if not isinstance(j, int) or j >= 1:
                    result(j - 1, (b - 1) % BS, r + (b - 1) // BS)
                    dve.wait_ge(gathered[(b - 1) % 2], 16 * uses(r + (b - 1) // BS, (b - 1) % BS))
                indices(j + 3, (b + 3) % BS)
                one_hot(j + 4)

            turns(dve, body)
            result(NB - 1, BS - 1, NB // BS - 1)


def gather_results(nc, acc, results):
    with Stage(nc, "sum") as st:
        part = st.sb("part", [P, 2, TOP_K, D])
        loaded = [st.sem(f"loaded{u}") for u in range(2)]
        summed, pool_sum = st.sem("summed"), st.sem("pool_sum")
        block = st.block()
        HALF = TOP_K // 2

        @block.sync
        def _(sp):
            for t in range(LAT_TILES):
                if t >= 2:
                    sp.wait_ge(summed, t - 1)
                sp.dma_start(part[:, t % 2], results[0:TOP_K * SEQ, :].rearrange("(r t) d -> t r d", r=TOP_K)
                             [t * P:(t + 1) * P]).then_inc(loaded[t % 2], 16)

        def halve(eng, lib, u, at, n):
            while n > 1:
                n //= 2
                lib.tensor_tensor(part[:, u, at:at + n], part[:, u, at:at + n], part[:, u, at + n:at + 2 * n], ALU.add)
                eng.drain()

        @block.gpsimd
        def _(pool):
            for t in range(LAT_TILES):
                pool.wait_ge(loaded[t % 2], 16 * (t // 2 + 1))
                halve(pool, nc.gpsimd, t % 2, TOP_K - 2, 2)
                pool.sem_inc(pool_sum, 1)

        @block.vector
        def _(dve):
            for t in range(LAT_TILES):
                u = t % 2
                dve.wait_ge(loaded[u], 16 * (t // 2 + 1))
                halve(dve, nc.vector, u, 0, HALF)
                nc.vector.tensor_tensor(part[:, u, HALF], part[:, u, HALF], part[:, u, HALF + 1], ALU.add)
                nc.vector.tensor_tensor(acc[:, t, :], acc[:, t, :], part[:, u, 0], ALU.add)
                dve.drain()
                nc.vector.tensor_tensor(acc[:, t, :], acc[:, t, :], part[:, u, HALF], ALU.add)
                dve.drain()
                dve.wait_ge(pool_sum, t + 1)
                nc.vector.tensor_tensor(acc[:, t, :], acc[:, t, :], part[:, u, TOP_K - 2], ALU.add).then_inc(summed, 1)


def finish_block(nc, acc, gain, x1, norm_g, out):
    with Stage(nc, "finish") as st:
        x = st.sb("x", [P, LAT_TILES, D])
        sq = st.sb("sq", [P, D])
        ms = st.sb("ms", [P, LAT_TILES, 4])
        g = st.sb("g", [P, 2, D])
        once, summed, squared, mean, rooted, made, stored = (st.sem("once"), st.sem("summed"), st.sem("squared"),
                                                             st.sem("mean"), st.sem("rooted"), st.sem("made"), st.sem("stored"))
        block = st.block()

        @block.sync
        def _(sp):
            sp.dma_start(g[:, 0, :], gain.broadcast_to([P, D])).then_inc(once, 16)
            sp.dma_start(g[:, 1, :], norm_g.rearrange("(o e) -> o e", o=1).broadcast_to([P, D])).then_inc(once, 16)
            sp.dma_start(x[:], x1.rearrange("(t p) d -> p t d", p=P)).then_inc(once, 16)
            for t in range(LAT_TILES):
                sp.wait_ge(made, t + 1)
                sp.dma_start(out[t * P:(t + 1) * P, :], x[:, t, :]).then_inc(stored, 16)
            sp.wait_ge(stored, 16 * LAT_TILES)

        @block.scalar
        def _(act):
            for t in range(LAT_TILES):
                act.wait_ge(summed, t + 1)
                act.drain()
                nc.scalar.activation(sq[:, :], x[:, t, :], ACT.Square, accum_out=ms[:, t, 0:1]).then_inc(squared, 1)
            act.wait_ge(mean, 1)
            nc.scalar.activation(ms[:, :, 2], ms[:, :, 1], ACT.Sqrt).then_inc(rooted, 1)

        @block.vector
        def _(dve):
            dve.wait_ge(once, 48)
            for t in range(LAT_TILES):
                nc.vector.tensor_tensor(acc[:, t, :], acc[:, t, :], g[:, 0, :], ALU.mult)
                dve.drain()
                nc.vector.tensor_tensor(x[:, t, :], x[:, t, :], acc[:, t, :], ALU.add).then_inc(summed, 1)
            dve.wait_ge(squared, LAT_TILES)
            nc.vector.tensor_scalar(ms[:, :, 1], ms[:, :, 0], 1.0 / D, EPS, ALU.mult, ALU.add).then_inc(mean, 1)
            dve.wait_ge(rooted, 1)
            nc.vector.reciprocal(ms[:, :, 3], ms[:, :, 2])
            dve.drain()
            for t in range(LAT_TILES):
                nc.vector.scalar_tensor_tensor(x[:, t, :], x[:, t, :], ms[:, t, 3:4], g[:, 1, :], ALU.mult, ALU.mult)\
                    .then_inc(made, 1)


def modulated_norm(nc, consts, name, sources, norm_g, mods, shift_at, dst, keep=None, tiles=None):
    def params(st, scale, bias):
        g = st.sb("g", [P, KD])
        n = 1 + max(i for _, _, i in sources)

        def make(dve):
            nc.vector.tensor_scalar(scale[:, 0:n, :], scale[:, 0:n, :], 1.0, None, ALU.add)
            dve.drain()
            for i in range(n):
                nc.vector.tensor_tensor(scale[:, i, :], scale[:, i, :], g[:, :], ALU.mult)

        loads = [(g[:, :], column(norm_g))]
        for i in range(n):
            loads += [(bias[:, i, :], column(mods[i, shift_at:shift_at + D])),
                      (scale[:, i, :], column(mods[i, shift_at + D:shift_at + 2 * D]))]
        return loads, make

    norm_columns(nc, consts, name, sources, params, dst, keep, tiles)


def plain_norm(nc, consts, name, src, norm_g, dst):
    def params(st, scale, bias):
        return [(scale[:, 0, :], column(norm_g))], lambda dve: nc.vector.memset(bias[:], 0.0)

    norm_columns(nc, consts, name, [(src, 0, 0)], params, dst)


def first_block(nc, consts, i, s):
    mods, proj, mix, x1 = s["mods"], s["proj"], s["mix"], s["x1"]
    rw, hg = s["rw"], s["hg"]
    modulation(nc, i["c"], i["c_ctx"], i["w_mod"], i["b_mod"], mods)
    with nc.sbuf_tensor("hT", [P, KD, TOK], F32) as hT:
        modulated_norm(nc, consts, "norm1", [(i["ctx"][0], 0, 1), (i["x"][0], CTX, 0)], i["norm1_g"][0], mods, 0, hT)
        linear_columns(nc, "proj", i["w_in"][0], hT, TOK, proj)
    rwkv_prepare(nc, consts, proj, {
        "conv": i["rw_conv"][0].rearrange("y x c -> (y x) c"), "w0": i["rw_w0"][0], "a0": i["rw_a0"][0],
        "k_k": i["rw_k_k"][0], "k_a": i["rw_k_a"][0], "r_k": i["rw_r_k"][0].rearrange("h d -> (h d)"),
        "w2": i["rw_w2"][0].rearrange("d r c -> (d r) c"), "a2": i["rw_a2"][0].rearrange("d r c -> (d r) c"),
        "g2": i["rw_g2"][0]}, rw)
    for d in range(2):
        rwkv_chunks(nc, consts, rw, d)
    rwkv_states(nc, rw)
    rwkv_output(nc, consts, rw, {"lnx_g": i["rw_lnx_g"][0], "lnx_b": i["rw_lnx_b"][0]}, mix)
    hgrn_prepare(nc, proj, {"lb": i["hg_lb_logits"]}, hg)
    hgrn_scan(nc, consts, proj, hg)
    hgrn_output(nc, consts, proj, hg, {"norm_g": i["hg_norm_g"][0]}, mix)
    linear_tokens(nc, "out1", mix, i["w_out"][0], i["x"][0], x1, mods[0:1, 2 * D:3 * D])
    moe_block(nc, consts, i, s)


def moe_block(nc, consts, i, s):
    mods, x1 = s["mods"], s["x1"]
    with ExitStack() as ctx:
        def sb(name, shape, dt=F32):
            return ctx.enter_context(nc.sbuf_tensor("moe_" + name, shape, dt))

        acc = sb("acc", [P, LAT_TILES, D])
        scale, bias = sb("scale", [P, 2, KD]), sb("bias", [P, 2, KD])
        tb = {"place": sb("place", [P, LAT_TILES, N_EXPERTS]), "info": sb("info", [P, LAT_TILES, N_EXPERTS, 4]),
              "slot": sb("slot", [P, P]), "lane": sb("lane", [P, 3]), "owner": sb("owner", [1, MAX_BLOCKS + 4], I32),
              "start": sb("start", [1, N_EXPERTS], I32)}
        with nc.sbuf_tensor("h2", [P, KD, SEQ], F32) as h2, \
                nc.sbuf_tensor("gates", [P, LAT_TILES, N_EXPERTS], F32) as gates, \
                nc.sbuf_tensor("chosen", [P, LAT_TILES, N_EXPERTS], F32) as chosen:
            modulated_norm(nc, consts, "norm2", [(x1, 0, 0)], i["norm2_g"][0], mods, 3 * D, h2, s["yn"], (scale, bias))
            route(nc, h2, i["router_w"][0], i["router_b"][0], gates, chosen)
            dispatch(nc, consts, gates, chosen, tb)
            shared_expert(nc, h2, acc, i["sh_w_gate"][0], i["sh_w_up"][0], i["sh_w_down"][0])
        routed_experts(nc, consts, s["yn"], scale, bias, tb,
                       [i["exp_w_gate"][0], i["exp_w_up"][0], i["exp_w_down"][0]], s["results"])
        gather_results(nc, acc, s["results"])
        finish_block(nc, acc, mods[0:1, 5 * D:6 * D], x1, i["final_norm_g"], s["h"])


def log1p(nc, dve, out, e, z, z2):
    nc.vector.tensor_scalar(z, e, 2.0, None, ALU.add)
    dve.drain()
    nc.vector.reciprocal(z, z)
    dve.drain()
    nc.vector.tensor_tensor(z, z, e, ALU.mult)
    dve.drain()
    nc.vector.tensor_tensor(z2, z, z, ALU.mult)
    dve.drain()
    nc.vector.tensor_scalar(out, z2, 1.0 / 17, None, ALU.mult)
    for k in range(7, 0, -1):
        dve.drain()
        nc.vector.scalar_tensor_tensor(out, out, 1.0 / (2 * k + 1), z2, ALU.add, ALU.mult)
    dve.drain()
    nc.vector.scalar_tensor_tensor(out, out, 1.0, z, ALU.add, ALU.mult)
    dve.drain()
    nc.vector.tensor_scalar(out, out, 2.0, None, ALU.mult)
    dve.drain()


def attention_prepare(nc, consts, proj, par, at):
    with Stage(nc, "atprep") as st:
        x = st.sb("x", [P, 2, 2, SEQ])
        sq = st.sb("sq", [P, 2, SEQ])
        gcol = st.sb("gcol", [P, 2])
        f = st.sb("f", [HEADS, 6, SEQ])
        fb = st.sb("fb", [HEADS, 1])
        ps = st.psum("ps", [P, 2, 2 * BANK])
        once, sq_made, sums, guarded, rooted, made = (st.sem("once"), st.sem("sq_made"), st.sem("sums"), st.sem("guarded"),
                                                      st.sem("rooted"), st.sem("made"))
        f_abs, f_made, f_sent = st.sem("f_abs"), st.sem("f_made"), st.sem("f_sent")
        loaded = [st.sem(f"loaded{u}") for u in range(2)]
        stored = [st.sem(f"stored{u}") for u in range(2)]
        block = st.block()

        @block.sync
        def _(sp):
            for j, name in enumerate(("q_g", "k_g")):
                for h in range(2):
                    sp.dma_start(gcol[h * HEAD:(h + 1) * HEAD, j:j + 1], par[name].rearrange("(p o) -> p o", o=1))\
                        .then_inc(once, 16)
            sp.dma_start(f[:, 0, :], proj[ROW2_F:ROW2_F + HEADS, :]).then_inc(once, 16)
            sp.dma_start(fb[:, :], par["f_b"].rearrange("(p o) -> p o", o=1)).then_inc(once, 16)

            def body(i, u, r):
                sp.wait_ge(stored[u], (r + 1) * 64)
                for j, row in enumerate((ROW2_Q, ROW2_K)):
                    sp.dma_start(x[:, u, j, :], proj[bass.ds(i * P + row, P), :]).then_inc(loaded[u], 16)

            steps(sp, QT, 2, body)

        @block.tensor
        def _(pe):
            def body(i, u, r):
                for j in range(2):
                    pe.wait_ge(sq_made, i * 2 + (j + 1))
                    pe.wait_ge(guarded, i * 2 + (j + 1))
                    for a, n in chunks(SEQ):
                        op = nc.tensor.matmul(ps[:, j, a:a + n], consts["headsum"][:, :], sq[:, j, a:a + n],
                                              start=True, stop=True)
                    op.then_inc(sums, 1)

            steps(pe, QT, 2, body)

        @block.scalar
        def _(act):
            act.wait_ge(once, 96)
            nc.scalar.activation(f[:, 1, :], f[:, 0, :], ACT.Abs, bias=fb[:, 0:1])
            nc.scalar.activation(f[:, 2, :], f[:, 0, :], ACT.Identity, bias=fb[:, 0:1])
            act.drain()
            nc.scalar.activation(f[:, 1, :], f[:, 1, :], ACT.Exp, scale=-1.0).then_inc(f_abs, 1)
            for u in range(2):
                act.sem_inc(stored[u], 64)

            def body(i, u, r):
                act.wait_ge(loaded[u], (r + 1) * 32)
                for j in range(2):
                    act.wait_ge(made, i * 2 + (j + 1))
                    nc.scalar.activation(sq[:, j, :], x[:, u, j, :], ACT.Square).then_inc(sq_made, 1)
                for j in range(2):
                    act.wait_ge(guarded, i * 2 + (j + 3))
                    nc.scalar.activation(sq[:, j, :], sq[:, j, :], ACT.Sqrt).then_inc(rooted, 1)
                for j, name in enumerate(("q", "k")):
                    act.wait_ge(made, i * 2 + (j + 3))
                    for h in range(2):
                        act.dma_start(at[name][bass.ds(i * 2 + h, 1), 0:HEAD, :].rearrange("o k t -> (o k) t"),
                                      x[h * HEAD:(h + 1) * HEAD, u, j, :]).then_inc(stored[u], 16)

            steps(act, QT, 2, body)
            act.wait_ge(f_made, 1)
            for name, row, src in (("q", HEAD, 3), ("q", HEAD + 1, 4), ("k", HEAD, 4), ("k", HEAD + 1, 5)):
                act.dma_start(at[name][:, row, :], f[:, src, :]).then_inc(f_sent, 16)
            act.wait_ge(f_sent, 64)
            for u in range(2):
                act.wait_ge(stored[u], 64 * (QT // 2 + 1))

        @block.vector
        def _(dve):
            dve.sem_inc(guarded, 2)
            dve.sem_inc(made, 2)
            dve.wait_ge(once, 96)

            dve.wait_ge(f_abs, 1)
            log1p(nc, dve, f[:, 3, :], f[:, 1, :], f[:, 4, :], f[:, 5, :])
            nc.vector.scalar_tensor_tensor(f[:, 5, :], f[:, 2, :], 0.0, f[:, 3, :], ALU.min, ALU.subtract)
            nc.vector.memset(f[:, 4, :], 1.0)
            dve.drain()
            nc.vector.tensor_tensor_scan(f[:, 3, :], f[:, 4, :], f[:, 5, :], 0.0, ALU.mult, ALU.add)
            dve.drain()
            nc.vector.tensor_scalar(f[:, 5, :], f[:, 3, :], -1.0, None, ALU.mult).then_inc(f_made, 1)

            def body(i, u, r):
                for j in range(2):
                    dve.wait_ge(sums, i * 2 + (j + 1))
                    nc.vector.tensor_scalar(sq[:, j, :], ps[:, j, :], 1.0 / HEAD, EPS, ALU.mult, ALU.add)\
                        .then_inc(guarded, 1)
                for j in range(2):
                    dve.wait_ge(rooted, i * 2 + (j + 1))
                    nc.vector.reciprocal(sq[:, j, :], sq[:, j, :])
                    dve.drain()
                    nc.vector.scalar_tensor_tensor(x[:, u, j, :], x[:, u, j, :], gcol[:, j:j + 1], sq[:, j, :],
                                                   ALU.mult, ALU.mult)
                    dve.drain()
                    if j == 0:
                        nc.vector.tensor_scalar(x[:, u, j, :], x[:, u, j, :], HEAD ** -0.5, None, ALU.mult)
                        dve.drain()
                    dve.sem_inc(made, 1)

            steps(dve, QT, 2, body)


def attention(nc, consts, proj, at, out):
    KA = HEAD + 2
    NT = LAT_TILES
    with Stage(nc, "attn") as st:
        qk = st.sb("qk", [KA, 2, 2, SEQ])
        vf = st.sb("vf", [HEAD, 2, SEQ])
        v = st.sb("v", [P, NT, HEAD])
        p = st.sb("p", [P, 2, SEQ])
        pT = st.sb("pT", [P, NT, P])
        o = st.sb("o", [P, 2, NT, HEAD])
        after = st.sb("after", [P, P])
        stat = st.sb("stat", [P, 2, 3])
        ps = st.psum("ps", [P, 2, 2 * BANK])
        pt = st.psum("pt", [P, 2 * BANK])
        po = st.psum("po", [P, BANK])
        pv = st.psum("pv", [P, BANK])
        loaded = [st.sem(f"loaded{u}") for u in range(2)]
        stored = [st.sem(f"stored{u}") for u in range(2)]
        v_turned, v_made, logits, peak, p_made, p_turned, pT_made, o_ready, o_made = (
            st.sem(n) for n in ("v_turned", "v_made", "logits", "peak", "p_made", "p_turned", "pT_made", "o_ready", "o_made"))
        block = st.block()

        @block.sync
        def _(sp):
            def body(h, u, r):
                sp.wait_ge(o_made, (h + 1) * NT)
                for j, name in enumerate(("q", "k")):
                    sp.dma_start(qk[:, u, j, :], at[name][bass.ds(h, 1)].rearrange("o k t -> (o k) t")).then_inc(loaded[u], 16)
                sp.dma_start(vf[:, u, :], proj[bass.ds(h * HEAD + ROW2_V, HEAD), :]).then_inc(loaded[u], 16)

            steps(sp, HEADS, 2, body)

        @block.tensor
        def _(pe):
            def score(h, u, t):
                pe.wait_ge(p_made, h * NT + (t + 1))
                for a, n in chunks((t + 1) * P):
                    op = nc.tensor.matmul(ps[:, t % 2, a:a + n], qk[:, u, 0, t * P:(t + 1) * P], qk[:, u, 1, a:a + n],
                                          start=True, stop=True)
                op.then_inc(logits, 1)

            def body(h, u, r):
                pe.wait_ge(loaded[u], (r + 1) * 48)
                pe.wait_ge(v_made, h + 1)
                score(h, u, 0)
                for t in range(NT):
                    op = nc.tensor.transpose(pv[:, t * HEAD:(t + 1) * HEAD], vf[:, u, t * P:(t + 1) * P],
                                             consts["ident"][0:HEAD, 0:HEAD])
                op.then_inc(v_turned, 1)
                for t in range(NT):
                    if t + 1 < NT:
                        score(h, u, t + 1)
                    pe.wait_ge(p_made, h * NT + (t + 3))
                    pe.wait_ge(pT_made, h * NT + (t + 1))
                    for j in range(t + 1):
                        op = nc.tensor.transpose(pt[:, j * P:(j + 1) * P], p[:, t % 2, j * P:(j + 1) * P],
                                                 consts["ident"][:, :])
                    op.then_inc(p_turned, 1)
                    pe.wait_ge(pT_made, h * NT + (t + 2))
                    pe.wait_ge(o_made, h * NT + (t + 2 * NT))
                    if t == 0:
                        pe.wait_ge(v_made, h + 2)
                    for j in range(t + 1):
                        op = nc.tensor.matmul(po[:, 0:HEAD], pT[:, j, :], v[:, j, :], start=(j == 0), stop=(j == t))
                    op.then_inc(o_ready, 1)

            steps(pe, HEADS, 2, body)

        @block.scalar
        def _(act):
            act.sem_inc(p_made, 2)
            act.sem_inc(v_made, 1)
            act.sem_inc(pT_made, 1)
            for u in range(2):
                act.sem_inc(stored[u], 16)

            def body(h, u, r):
                act.wait_ge(v_turned, h + 1)
                nc.scalar.copy(v[:].rearrange("p t k -> p (t k)"), pv[:, :]).then_inc(v_made, 1)
                for t in range(NT):
                    act.wait_ge(peak, h * NT + (t + 1))
                    act.wait_ge(o_made, h * NT + (t + 2 * NT - 1))
                    act.wait_ge(p_turned, h * NT + (t + 1))
                    nc.scalar.activation(p[:, t % 2, 0:(t + 1) * P], ps[:, t % 2, 0:(t + 1) * P], ACT.Exp,
                                         bias=stat[:, t % 2, 0:1], accum_out=stat[:, t % 2, 1:2]).then_inc(p_made, 1)
                    act.wait_ge(p_turned, h * NT + (t + 3))
                    act.wait_ge(o_ready, h * NT + (t + 1))
                    nc.scalar.copy(pT[:, 0:t + 1, :].rearrange("p j t -> p (j t)"), pt[:, 0:(t + 1) * P])\
                        .then_inc(pT_made, 1)
                act.wait_ge(o_made, (h + 3) * NT)
                act.dma_start(out[:, bass.ds(h * HEAD, HEAD)].rearrange("(t p) k -> p t k", p=P), o[:, u])\
                    .then_inc(stored[u], 16)

            steps(act, HEADS, 2, body)
            for u in range(2):
                act.wait_ge(stored[u], 16 * (HEADS // 2 + 1))

        @block.vector
        def _(dve):
            nc.vector.tensor_tensor(after[:, :], consts["upto"][:, :], consts["ident"][:, :], ALU.subtract)
            dve.drain()
            nc.vector.tensor_scalar(after[:, :], after[:, :], -1e30, None, ALU.mult)
            dve.drain()
            dve.sem_inc(o_made, 2 * NT)

            def top(h, u, t):
                dve.wait_ge(logits, h * NT + (t + 1))
                diag = ps[:, t % 2, t * P:(t + 1) * P]
                nc.vector.tensor_tensor(diag, diag, after[:, :], ALU.add)
                dve.drain()
                nc.vector.tensor_reduce(stat[:, t % 2, 0:1], ps[:, t % 2, 0:(t + 1) * P], AX.X, ALU.max)
                dve.drain()
                nc.vector.tensor_scalar(stat[:, t % 2, 0:1], stat[:, t % 2, 0:1], -1.0, None, ALU.mult).then_inc(peak, 1)

            def body(h, u, r):
                dve.wait_ge(stored[u], (r + 1) * 16)
                top(h, u, 0)
                for t in range(NT):
                    if t + 1 < NT:
                        top(h, u, t + 1)
                    dve.wait_ge(o_ready, h * NT + (t + 2))
                    nc.vector.reciprocal(stat[:, t % 2, 2:3], stat[:, t % 2, 1:2])
                    dve.drain()
                    nc.vector.tensor_scalar(o[:, u, t, :], po[:, 0:HEAD], stat[:, t % 2, 2:3], None, ALU.mult)\
                        .then_inc(o_made, 1)

            steps(dve, HEADS, 2, body)

        @block.gpsimd
        def _(pool):
            pool.sem_inc(p_turned, 2)
            pool.sem_inc(o_ready, 1)


def gated_columns(nc, consts, src, gate, out):
    with Stage(nc, "gated") as st:
        o = st.sb("o", [P, 2, WID])
        g = st.sb("g", [P, 2, QT, P])
        res = st.sb("res", [P, 2, QT, P])
        pt = st.psum("pt", [P, 2, BANK])
        loaded = [st.sem(f"loaded{u}") for u in range(2)]
        stored = [st.sem(f"stored{u}") for u in range(2)]
        turned, silu_made, made = st.sem("turned"), st.sem("silu_made"), st.sem("made")
        block = st.block()

        @block.sync
        def _(sp):
            def body(i, u, r):
                sp.wait_ge(made, i + 1)
                sp.dma_start(o[:, u, :], src[bass.ds(i * P, P), :]).then_inc(loaded[u], 16)
                sp.dma_start(g[:, u], gate[:, bass.ds(i * P, P)].rearrange("(j p) t -> p j t", p=P)).then_inc(loaded[u], 16)

            steps(sp, LAT_TILES, 2, body)

        @block.tensor
        def _(pe):
            def body(i, u, r):
                pe.wait_ge(loaded[u], (r + 1) * 32)
                pe.wait_ge(made, i + 1)
                for j in range(QT):
                    op = nc.tensor.transpose(pt[:, u, j * P:(j + 1) * P], o[:, u, j * P:(j + 1) * P], consts["ident"][:, :])
                op.then_inc(turned, 1)

            steps(pe, LAT_TILES, 2, body)

        @block.scalar
        def _(act):
            for u in range(2):
                act.sem_inc(stored[u], 16)

            def body(i, u, r):
                act.wait_ge(loaded[u], (r + 1) * 32)
                nc.scalar.activation(g[:, u], g[:, u], ACT.Silu).then_inc(silu_made, 1)
                act.wait_ge(made, i + 3)
                act.dma_start(out[:, bass.ds(i * P, P)].rearrange("(j p) t -> p j t", p=P), res[:, u]).then_inc(stored[u], 16)

            steps(act, LAT_TILES, 2, body)
            for u in range(2):
                act.wait_ge(stored[u], 16 * (LAT_TILES // 2 + 1))

        @block.vector
        def _(dve):
            dve.sem_inc(made, 2)

            def body(i, u, r):
                dve.wait_ge(turned, i + 1)
                dve.wait_ge(silu_made, i + 1)
                dve.wait_ge(stored[u], (r + 1) * 16)
                nc.vector.tensor_tensor(res[:, u].rearrange("p j t -> p (j t)"), pt[:, u, :],
                                        g[:, u].rearrange("p j t -> p (j t)"), ALU.mult).then_inc(made, 1)

            steps(dve, LAT_TILES, 2, body)


def causal_conv(nc, dve, out, x, taps, bias):
    nc.vector.tensor_scalar(out, x, taps[:, CONV_WIDTH - 1:CONV_WIDTH], bias, ALU.mult, ALU.add)
    for j in range(1, CONV_WIDTH):
        dve.drain()
        nc.vector.scalar_tensor_tensor(out[:, j:], x[:, :SEQ - j], taps[:, CONV_WIDTH - 1 - j:CONV_WIDTH - j],
                                       out[:, j:], ALU.mult, ALU.add)


def ssd_prepare(nc, proj, par, sd):
    with Stage(nc, "ssdprep") as st:
        x = st.sb("x", [P, 2, SEQ])
        y = st.sb("y", [P, 2, SEQ])
        taps = st.sb("taps", [P, 2, CONV_WIDTH])
        bias = st.sb("bias", [P, 2, 1])
        t = st.sb("t", [SSD_HEADS, 6, SEQ])
        hp = st.sb("hp", [SSD_HEADS, 4])
        once, conv_made, silu_made, t_abs, t_made, t_sent = (st.sem(n) for n in (
            "once", "conv_made", "silu_made", "t_abs", "t_made", "t_sent"))
        loaded = [st.sem(f"loaded{u}") for u in range(2)]
        stored = [st.sem(f"stored{u}") for u in range(2)]
        n = SSD_CONV // P
        block = st.block()

        @block.sync
        def _(sp):
            sp.dma_start(t[:, 0, :], proj[ROW2_DT:ROW2_DT + SSD_HEADS, :]).then_inc(once, 16)
            for j, name in enumerate(("dt_bias", "a_log")):
                sp.dma_start(hp[:, j:j + 1], par[name].rearrange("(p o) -> p o", o=1)).then_inc(once, 16)

            def body(i, u, r):
                sp.wait_ge(conv_made, i + 1)
                at = bass.ds(i * P, P)
                sp.dma_start(x[:, u, :], proj[bass.ds(i * P + ROW2_XBC, P), :]).then_inc(loaded[u], 16)
                sp.dma_start(taps[:, u, :], par["conv_w"][:, at].rearrange("t p -> p t")).then_inc(loaded[u], 16)
                sp.dma_start(bias[:, u, :], par["conv_b"][at].rearrange("(p o) -> p o", o=1)).then_inc(loaded[u], 16)

            steps(sp, n, 2, body)

        @block.scalar
        def _(act):
            act.wait_ge(once, 48)
            nc.scalar.activation(t[:, 1, :], t[:, 0, :], ACT.Abs, bias=hp[:, 0:1])
            nc.scalar.activation(t[:, 2, :], t[:, 0, :], ACT.Identity, bias=hp[:, 0:1])
            act.drain()
            nc.scalar.activation(t[:, 1, :], t[:, 1, :], ACT.Exp, scale=-1.0)
            nc.scalar.activation(hp[:, 2:3], hp[:, 1:2], ACT.Exp).then_inc(t_abs, 1)
            for u in range(2):
                act.sem_inc(stored[u], 16)

            def body(i, u, r):
                act.wait_ge(conv_made, i + 3)
                nc.scalar.activation(y[:, u, :], y[:, u, :], ACT.Silu).then_inc(silu_made, 1)
                act.wait_ge(silu_made, i + 1)
                act.dma_start(sd["xbc"][bass.ds(i * P, P), :], y[:, u, :]).then_inc(stored[u], 16)

            steps(act, n, 2, body)
            act.wait_ge(t_made, 1)
            act.dma_start(sd["dt"], t[:, 3, :]).then_inc(t_sent, 16)
            act.dma_start(sd["acs"], t[:, 2, :]).then_inc(t_sent, 16)
            act.wait_ge(t_sent, 32)
            for u in range(2):
                act.wait_ge(stored[u], 16 * (n // 2 + 1))

        @block.vector
        def _(dve):
            dve.sem_inc(conv_made, 2)

            def body(i, u, r):
                dve.wait_ge(loaded[u], (r + 1) * 48)
                dve.wait_ge(stored[u], (r + 1) * 16)
                causal_conv(nc, dve, y[:, u, :], x[:, u, :], taps[:, u, :], bias[:, u, :])
                dve.drain()
                dve.sem_inc(conv_made, 1)

            steps(dve, n, 2, body)
            dve.wait_ge(t_abs, 1)
            log1p(nc, dve, t[:, 3, :], t[:, 1, :], t[:, 4, :], t[:, 5, :])
            nc.vector.scalar_tensor_tensor(t[:, 3, :], t[:, 2, :], 0.0, t[:, 3, :], ALU.max, ALU.add)
            nc.vector.memset(t[:, 5, :], 1.0)
            dve.drain()
            nc.vector.memset(t[:, 5, :].rearrange("p (c t) -> p c t", t=P)[:, :, 0:1], 0.0)
            nc.vector.tensor_scalar(t[:, 4, :], t[:, 3, :], hp[:, 2:3], -1.0, ALU.mult, ALU.mult)
            dve.drain()
            nc.vector.tensor_tensor_scan(t[:, 2, :], t[:, 5, :], t[:, 4, :], 0.0, ALU.mult, ALU.add).then_inc(t_made, 1)


def ssd_scan(nc, consts, proj, par, sd, mix):
    XT, G, HG = SSD_WIDTH // P, SSD_GROUPS, SSD_HEADS // SSD_GROUPS
    with Stage(nc, "ssd") as st:
        xf = st.sb("xf", [P, 2, XT, P])
        zf = st.sb("zf", [P, 2, XT, P])
        bc = st.sb("bc", [P, 2, 2, G, P])
        row = st.sb("row", [P, 2, SSD_HEADS, P])
        da = st.sb("da", [SSD_HEADS, 2, 2, P])
        dskip = st.sb("dskip", [P, SSD_HEADS])
        ng = st.sb("ng", [P, XT])
        x = st.sb("x", [P, SSD_WIDTH])
        z = st.sb("z", [P, SSD_WIDTH])
        bT = st.sb("bT", [P, G, P])
        col = st.sb("col", [P, 6, SSD_HEADS])
        xdt = st.sb("xdt", [P, SSD_WIDTH])
        xdd = st.sb("xdd", [P, SSD_WIDTH])
        cb = st.sb("cb", [P, G, P])
        L = st.sb("L", [P, SSD_HEADS, P])
        s = st.sb("s", [P, SSD_WIDTH])
        y = st.sb("y", [P, SSD_WIDTH])
        t1 = st.sb("t1", [P, SSD_WIDTH])
        stat = st.sb("stat", [P, 4, G])
        res = st.sb("res", [P, 2, XT, P])
        pa = st.psum("pa", [P, 2 * BANK])
        pb = st.psum("pb", [P, 2 * BANK])
        pc = st.psum("pc", [P, BANK])
        pd = st.psum("pd", [P, BANK])
        pe_s = st.psum("pe_s", [P, 2 * BANK])
        names = ("once", "z_silu", "turned", "x_made", "z_made", "small_made", "seg_made", "exp_made", "L_made", "M_made",
                 "xdt_made", "xdd_made", "diag_ready", "off_ready", "s_ready", "s_made", "var_made", "root_made", "y_made",
                 "y_turned", "res_made", "cb_made")
        (once, z_silu, turned, x_made, z_made, small_made, seg_made, exp_made, L_made, M_made, xdt_made, xdd_made,
         diag_ready, off_ready, s_ready, s_made, var_made, root_made, y_made, y_turned, res_made, cb_made) = (
            st.sem(n) for n in names)
        loaded = [st.sem(f"loaded{u}") for u in range(2)]
        stored = [st.sem(f"stored{u}") for u in range(2)]
        LOADS = 2 + 2 + 1 + 2
        block = st.block()

        def heads(ap):
            return ap.rearrange("p (h k) -> p h k", k=HEAD)

        @block.sync
        def _(sp):
            sp.dma_start(dskip[:, :], par["d"].rearrange("(o e) -> o e", o=1).broadcast_to([P, SSD_HEADS])).then_inc(once, 16)
            sp.dma_start(ng[:, :], column(par["norm_g"])).then_inc(once, 16)

            def body(i, u, r):
                tk = bass.ds(i * P, P)
                sp.wait_ge(y_made, i + 1)
                sp.dma_start(xf[:, u], sd["xbc"][0:SSD_WIDTH, tk].rearrange("(j p) t -> p j t", p=P)).then_inc(loaded[u], 16)
                for j in range(2):
                    a = SSD_WIDTH + j * G * SSD_STATE
                    sp.dma_start(bc[:, u, j], sd["xbc"][a:a + G * SSD_STATE, tk].rearrange("(g n) t -> n g t", n=P))\
                        .then_inc(loaded[u], 16)
                sp.dma_start(zf[:, u], proj[ROW2_ZS:ROW2_ZS + SSD_WIDTH, tk].rearrange("(j p) t -> p j t", p=P))\
                    .then_inc(loaded[u], 16)
                sp.dma_start(row[:, u], sd["acs"][:, tk].rearrange("(o h) t -> o h t", o=1).broadcast_to([P, SSD_HEADS, P]))\
                    .then_inc(loaded[u], 16)
                sp.dma_start(da[:, u, 0, :], sd["dt"][:, tk]).then_inc(loaded[u], 16)
                sp.dma_start(da[:, u, 1, :], sd["acs"][:, tk]).then_inc(loaded[u], 16)

            steps(sp, SSD_CHUNKS, 2, body)

        @block.tensor
        def _(pe):
            def body(i, u, r):
                ident = consts["ident"]
                pe.wait_ge(loaded[u], (r + 1) * (16 * LOADS))
                pe.wait_ge(res_made, i + 1)
                for j in range(XT):
                    op = nc.tensor.transpose(pa[:, j * P:(j + 1) * P], xf[:, u, j, :], ident[:, :])
                op.then_inc(turned, 1)
                for j in range(2):
                    nc.tensor.transpose(pc[:, 2 * P + 16 * j:2 * P + 16 * (j + 1)], da[:, u, j, :], ident[0:16, 0:16])
                for g in range(G):
                    op = nc.tensor.transpose(pc[:, g * P:(g + 1) * P], bc[:, u, 0, g, :], ident[:, :])
                op.then_inc(turned, 1)
                for g in range(G):
                    op = nc.tensor.matmul(pd[:, g * P:(g + 1) * P], bc[:, u, 0, g, :], bc[:, u, 1, g, :],
                                          start=True, stop=True)
                op.then_inc(turned, 1)
                pe.wait_ge(z_silu, i + 1)
                pe.wait_ge(y_made, i + 2)
                for j in range(XT):
                    op = nc.tensor.transpose(pb[:, j * P:(j + 1) * P], zf[:, u, j, :], ident[:, :])
                op.then_inc(turned, 1)
                pe.wait_ge(z_made, i + 1)
                pe.wait_ge(s_made, i + 1)
                for g in range(G):
                    op = nc.tensor.matmul(pb[:, g * BANK:(g + 1) * BANK], bc[:, u, 1, g, :], s[:, g * BANK:(g + 1) * BANK],
                                          start=True, stop=True)
                op.then_inc(off_ready, 1)
                pe.wait_ge(xdd_made, i + 1)
                for g in range(G):
                    op = nc.tensor.matmul(pe_s[:, g * BANK:(g + 1) * BANK], bT[:, g, :], xdd[:, g * BANK:(g + 1) * BANK],
                                          start=True, stop=True)
                op.then_inc(s_ready, 1)
                pe.wait_ge(M_made, i + 1)
                pe.wait_ge(xdt_made, i + 1)
                for h in range(SSD_HEADS):
                    op = nc.tensor.matmul(pa[:, h * HEAD:(h + 1) * HEAD], L[:, h, :], xdt[:, h * HEAD:(h + 1) * HEAD],
                                          start=True, stop=True)
                op.then_inc(diag_ready, 1)
                pe.wait_ge(y_made, i + 3)
                for j in range(XT):
                    op = nc.tensor.transpose(pa[:, j * P:(j + 1) * P], y[:, j * P:(j + 1) * P], ident[:, :])
                op.then_inc(y_turned, 1)

            steps(pe, SSD_CHUNKS, 2, body)

        @block.scalar
        def _(act):
            act.wait_ge(once, 32)
            act.sem_inc(res_made, 1)
            for u in range(2):
                act.sem_inc(stored[u], 16)

            def body(i, u, r):
                act.wait_ge(loaded[u], (r + 1) * (16 * LOADS))
                nc.scalar.activation(zf[:, u], zf[:, u], ACT.Silu).then_inc(z_silu, 1)
                act.wait_ge(y_made, i + 2)
                act.wait_ge(turned, i * 4 + 1)
                nc.scalar.copy(x[:, :], pa[:, :]).then_inc(x_made, 1)
                act.wait_ge(turned, i * 4 + 2)
                act.wait_ge(s_made, i + 1)
                nc.scalar.copy(col[:, 0:2, :].rearrange("p j h -> p (j h)"), pc[:, 2 * P:2 * P + 32])
                nc.scalar.copy(bT[:].rearrange("p g t -> p (g t)"), pc[:, 0:2 * P]).then_inc(small_made, 1)
                act.wait_ge(turned, i * 4 + 4)
                nc.scalar.copy(z[:, :], pb[:, :]).then_inc(z_made, 1)
                act.wait_ge(seg_made, i * 2 + 1)
                nc.scalar.activation(col[:, 2, :], col[:, 1, :], ACT.Exp)
                nc.scalar.activation(col[:, 4, :], col[:, 3, :], ACT.Exp)
                nc.scalar.activation(col[:, 5, :], row[:, u, :, P - 1], ACT.Exp).then_inc(exp_made, 1)
                act.wait_ge(seg_made, i * 2 + 2)
                nc.scalar.activation(L[:], L[:], ACT.Exp).then_inc(L_made, 1)
                act.wait_ge(var_made, i + 1)
                nc.scalar.activation(stat[:, 2, :], stat[:, 1, :], ACT.Sqrt).then_inc(root_made, 1)
                act.wait_ge(y_turned, i + 1)
                act.wait_ge(stored[u], (r + 1) * 16)
                for j in range(XT):
                    op = nc.scalar.activation(res[:, u, j, :], pa[:, j * P:(j + 1) * P], ACT.Identity,
                                              scale=ng[:, j:j + 1])
                op.then_inc(res_made, 1)
                act.wait_ge(res_made, i + 2)
                act.dma_start(mix[WID:WID + SSD_WIDTH, bass.ds(i * P, P)].rearrange("(j p) t -> p j t", p=P), res[:, u])\
                    .then_inc(stored[u], 16)

            steps(act, SSD_CHUNKS, 2, body)
            for u in range(2):
                act.wait_ge(stored[u], 16 * (SSD_CHUNKS // 2 + 1))

        @block.gpsimd
        def _(pool):
            def body(i, u, r):
                pool.wait_ge(L_made, i + 1)
                pool.wait_ge(cb_made, i + 1)
                for g in range(G):
                    part = L[:, g * HG:(g + 1) * HG, :]
                    op = nc.gpsimd.tensor_tensor(part, part, over(cb[:, g, :], HG), ALU.mult)
                op.then_inc(M_made, 1)

            steps(pool, SSD_CHUNKS, 2, body)

        @block.vector
        def _(dve):
            dve.wait_ge(once, 32)
            nc.vector.memset(s[:, :], 0.0)
            dve.drain()
            dve.sem_inc(s_made, 1)
            dve.sem_inc(y_made, 2)

            def body(i, u, r):
                dve.wait_ge(small_made, i + 1)
                last = row[:, u, :, P - 1]
                nc.vector.tensor_tensor(col[:, 3, :], last, col[:, 1, :], ALU.subtract).then_inc(seg_made, 1)
                for h in range(SSD_HEADS):
                    op = nc.vector.tensor_scalar(L[:, h, :], row[:, u, h, :], col[:, 1, h:h + 1], 0.0, ALU.subtract, ALU.min)
                op.then_inc(seg_made, 1)
                dve.wait_ge(turned, i * 4 + 3)
                nc.vector.tensor_tensor(cb[:], pd[:, 0:2 * P].rearrange("p (g t) -> p g t", g=G), over(consts["upto"][:, :], G),
                                        ALU.mult).then_inc(cb_made, 1)
                dve.wait_ge(x_made, i + 1)
                nc.vector.tensor_tensor(heads(xdt[:, :]), heads(x[:, :]), last_of(col[:, 0, :], HEAD), ALU.mult)\
                    .then_inc(xdt_made, 1)
                nc.vector.tensor_tensor(heads(y[:, :]), heads(x[:, :]), last_of(dskip[:, :], HEAD), ALU.mult)
                dve.drain()
                dve.wait_ge(exp_made, i + 1)
                nc.vector.tensor_tensor(heads(xdd[:, :]), heads(xdt[:, :]), last_of(col[:, 4, :], HEAD), ALU.mult)\
                    .then_inc(xdd_made, 1)
                dve.wait_ge(off_ready, i + 1)
                nc.vector.tensor_tensor(heads(t1[:, :]), heads(pb[:, :]), last_of(col[:, 2, :], HEAD), ALU.mult)
                nc.vector.tensor_tensor(heads(s[:, :]), heads(s[:, :]), last_of(col[:, 5, :], HEAD), ALU.mult)
                dve.drain()
                nc.vector.tensor_tensor(y[:, :], y[:, :], t1[:, :], ALU.add)
                dve.wait_ge(s_ready, i + 1)
                nc.vector.tensor_tensor(s[:, :], s[:, :], pe_s[:, :], ALU.add).then_inc(s_made, 1)
                dve.drain()
                dve.wait_ge(diag_ready, i + 1)
                nc.vector.tensor_tensor(y[:, :], y[:, :], pa[:, :], ALU.add)
                dve.drain()
                dve.wait_ge(z_made, i + 1)
                nc.vector.tensor_tensor(y[:, :], y[:, :], z[:, :], ALU.mult)
                dve.drain()
                nc.vector.tensor_tensor(t1[:, :], y[:, :], y[:, :], ALU.mult)
                dve.drain()
                nc.vector.tensor_reduce(stat[:, 0, :], t1[:, :].rearrange("p (g n) -> p g n", g=G), AX.X, ALU.add)
                dve.drain()
                nc.vector.tensor_scalar(stat[:, 1, :], stat[:, 0, :], float(G) / SSD_WIDTH, EPS, ALU.mult, ALU.add)\
                    .then_inc(var_made, 1)
                dve.wait_ge(root_made, i + 1)
                nc.vector.reciprocal(stat[:, 3, :], stat[:, 2, :])
                dve.drain()
                v = y[:, :].rearrange("p (g n) -> p g n", g=G)
                nc.vector.tensor_tensor(v, v, last_of(stat[:, 3, :], SSD_WIDTH // G), ALU.mult).then_inc(y_made, 1)

            steps(dve, SSD_CHUNKS, 2, body)


def rglru(nc, proj, par, mix):
    with Stage(nc, "lru") as st:
        x = st.sb("x", [P, SEQ])
        z = st.sb("z", [P, SEQ])
        xc = st.sb("xc", [P, SEQ])
        gi = st.sb("gi", [P, SEQ])
        th = st.sb("th", [P, SEQ])
        inv = st.sb("inv", [P, SEQ])
        root = st.sb("root", [P, SEQ])
        a = st.sb("a", [P, SEQ])
        h = st.sb("h", [P, SEQ])
        taps = st.sb("taps", [P, CONV_WIDTH])
        cols = st.sb("cols", [P, 3])
        w = st.sb("w", [P, 2, P])
        lam = st.sb("lam", [P, 6, QT])
        ps = st.psum("ps", [P, 4, BANK])
        once, loaded, conv_made, lam_abs, gates_ready, i_made, th_made, root_made, z_made, sent, used = (
            st.sem(n) for n in ("once", "loaded", "conv_made", "lam_abs", "gates_ready", "i_made", "th_made", "root_made",
                                "z_made", "sent", "used"))
        w_zero, lam_made = st.sem("w_zero"), st.sem("lam_made")
        block = st.block()
        LOADS = 2 + 1 + 3 + 4

        @block.sync
        def _(sp):
            sp.dma_start(lam[:, 0, :], column(par["lam"])).then_inc(once, 16)
            sp.wait_ge(w_zero, 1)

            for i in range(QT):
                at = slice(i * P, (i + 1) * P)
                if i:
                    sp.wait_ge(used, i)
                sp.dma_start(x[:, :], proj[ROW2_XL + i * P:ROW2_XL + (i + 1) * P, :]).then_inc(loaded, 16)
                sp.dma_start(z[:, :], proj[ROW2_ZL + i * P:ROW2_ZL + (i + 1) * P, :]).then_inc(loaded, 16)
                sp.dma_start(taps[:, :], par["conv_w"][:, at].rearrange("t p -> p t")).then_inc(loaded, 16)
                for j, name in enumerate(("conv_b", "b_a", "b_x")):
                    sp.dma_start(cols[:, j:j + 1], par[name][at].rearrange("(p o) -> p o", o=1)).then_inc(loaded, 16)
                for j, name in enumerate(("w_a", "w_x")):
                    for b in range(2):
                        sp.dma_start(w[b * HEAD:(b + 1) * HEAD, j, b * HEAD:(b + 1) * HEAD], par[name][2 * i + b])\
                            .then_inc(loaded, 16)

        @block.gpsimd
        def _(pool):
            nc.gpsimd.memset(w[:], 0.0).then_inc(w_zero, 1)

        @block.tensor
        def _(pe):
            for i in range(QT):
                pe.wait_ge(conv_made, i + 1)
                if i:
                    pe.wait_ge(i_made, i)
                    pe.wait_ge(th_made, 2 * i)
                for j in range(2):
                    for c, (at, n) in enumerate(chunks(SEQ)):
                        op = nc.tensor.matmul(ps[:, 2 * j + c, :], w[:, j, :], xc[:, at:at + n], start=True, stop=True)
                op.then_inc(gates_ready, 1)

        @block.scalar
        def _(act):
            act.wait_ge(once, 16)
            nc.scalar.activation(lam[:, 1, :], lam[:, 0, :], ACT.Abs)
            act.drain()
            nc.scalar.activation(lam[:, 1, :], lam[:, 1, :], ACT.Exp, scale=-1.0).then_inc(lam_abs, 1)
            act.wait_ge(lam_made, 1)
            for i in range(QT):
                act.wait_ge(gates_ready, i + 1)
                nc.scalar.activation(gi[:, :], ps[:, 2:4, :].rearrange("p b n -> p (b n)"), ACT.Sigmoid, bias=cols[:, 2:3])\
                    .then_inc(i_made, 1)
                nc.scalar.activation(th[:, :], ps[:, 0:2, :].rearrange("p b n -> p (b n)"), ACT.Sigmoid, bias=cols[:, 1:2])\
                    .then_inc(th_made, 1)
                act.drain()
                nc.scalar.activation(th[:, :], th[:, :], ACT.Tanh, scale=lam[:, 5, i:i + 1]).then_inc(th_made, 1)
                act.drain()
                nc.scalar.activation(root[:, :], th[:, :], ACT.Sqrt).then_inc(root_made, 1)
                nc.scalar.activation(z[:, :], z[:, :], ACT.Silu).then_inc(z_made, 1)
                act.wait_ge(used, i + 1)
                act.dma_start(mix[WID + SSD_WIDTH + i * P:WID + SSD_WIDTH + (i + 1) * P, :], h[:, :]).then_inc(sent, 16)
            act.wait_ge(sent, 16 * QT)

        @block.vector
        def _(dve):
            dve.wait_ge(lam_abs, 1)
            log1p(nc, dve, lam[:, 2, :], lam[:, 1, :], lam[:, 3, :], lam[:, 4, :])
            nc.vector.tensor_scalar(lam[:, 3, :], lam[:, 0, :], -1.0, 0.0, ALU.mult, ALU.max)
            dve.drain()
            nc.vector.tensor_tensor(lam[:, 4, :], lam[:, 3, :], lam[:, 2, :], ALU.add)
            dve.drain()
            nc.vector.tensor_scalar(lam[:, 5, :], lam[:, 4, :], 4.0, None, ALU.mult).then_inc(lam_made, 1)
            for i in range(QT):
                dve.wait_ge(loaded, (i + 1) * (16 * LOADS))
                causal_conv(nc, dve, xc[:, :], x[:, :], taps[:, :], cols[:, 0:1])
                dve.drain()
                dve.sem_inc(conv_made, 1)
                dve.wait_ge(th_made, 2 * i + 2)
                nc.vector.tensor_scalar(inv[:, :], th[:, :], 1.0, None, ALU.add)
                dve.drain()
                nc.vector.reciprocal(inv[:, :], inv[:, :])
                nc.vector.tensor_scalar(a[:, :], th[:, :], -1.0, 1.0, ALU.mult, ALU.add)
                dve.drain()
                nc.vector.tensor_tensor(a[:, :], a[:, :], inv[:, :], ALU.mult)
                dve.wait_ge(root_made, i + 1)
                nc.vector.scalar_tensor_tensor(root[:, :], root[:, :], 2.0, inv[:, :], ALU.mult, ALU.mult)
                dve.drain()
                nc.vector.memset(root[:, 0:1], 1.0)
                dve.wait_ge(i_made, i + 1)
                nc.vector.tensor_tensor(gi[:, :], gi[:, :], xc[:, :], ALU.mult)
                dve.drain()
                nc.vector.tensor_tensor(gi[:, :], gi[:, :], root[:, :], ALU.mult)
                dve.drain()
                if i:
                    dve.wait_ge(sent, 16 * i)
                nc.vector.tensor_tensor_scan(h[:, :], a[:, :], gi[:, :], 0.0, ALU.mult, ALU.add)
                dve.drain()
                dve.wait_ge(z_made, i + 1)
                nc.vector.tensor_tensor(h[:, :], h[:, :], z[:, :], ALU.mult).then_inc(used, 1)


def second_block(nc, consts, i, s, out):
    h, proj, mix = s["h"], s["proj2"], s["mix2"]
    with nc.sbuf_tensor("uT", [P, KD, SEQ], F32) as uT:
        plain_norm(nc, consts, "norm3", h, i["norm_g_2"][0], uT)
        linear_columns(nc, "proj2", i["w_in_2"][0], uT, SEQ, proj)
    second_mix(nc, consts, i, s)
    linear_tokens(nc, "out2", mix, i["w_out_2"][0], h, out[0])


def second_mix(nc, consts, i, s):
    proj, mix = s["proj2"], s["mix2"]
    attention_prepare(nc, consts, proj, {"q_g": i["q_norm_g_2"][0], "k_g": i["k_norm_g_2"][0], "f_b": i["forget_b_2"][0]},
                      s["at"])
    attention(nc, consts, proj, s["at"], s["att"])
    gated_columns(nc, consts, s["att"], proj[ROW2_ZA:ROW2_ZA + WID, :], mix[0:WID, :])
    ssd_prepare(nc, proj, {"conv_w": i["ssd_conv_w_2"][0], "conv_b": i["ssd_conv_b_2"][0],
                           "dt_bias": i["ssd_dt_bias_2"][0], "a_log": i["ssd_a_log_2"][0]}, s["sd"])
    ssd_scan(nc, consts, proj, {"d": i["ssd_d_2"][0], "norm_g": i["ssd_norm_g_2"][0]}, s["sd"], mix)
    rglru(nc, proj, {"conv_w": i["lru_conv_w_2"][0], "conv_b": i["lru_conv_b_2"][0], "w_a": i["lru_w_a_2"][0],
                     "b_a": i["lru_b_a_2"][0], "w_x": i["lru_w_x_2"][0], "b_x": i["lru_b_x_2"][0],
                     "lam": i["lru_lambda_2"][0]}, mix)


def two_blocks(nc, i, out):
    def dram(name, shape):
        return nc.dram_tensor(name, shape, F32, kind="Internal").ap()

    rw = {n: dram("rw_" + n, (2, WID, TOK)) for n in ("a", "r", "b", "k", "bh", "kh")}
    rw["tot"] = dram("rw_tot", (2, WID, RW_CHUNKS))
    rw["v"] = dram("rw_v", (WID, TOK))
    rw["bonus"] = dram("rw_bonus", (WID, SEQ))
    rw["gate"] = dram("rw_gate", (WID, SEQ))
    rw["q_out"] = dram("rw_q_out", (2, TILES, 2, HEAD, 4, P))
    rw["y_out"] = dram("rw_y_out", (2, TILES, 2, P, 4, HEAD))
    rw["m_out"] = dram("rw_m_out", (2, TILES, 2, HEAD, 8, HEAD))
    rw["n_out"] = dram("rw_n_out", (2, TILES, 2, HEAD, 8, HEAD))
    rw["s"] = dram("rw_s", (2, TILES, HEAD, 2, HEADS, HEAD))
    hg = {n: dram("hg_" + n, (2, WID, TOK)) for n in ("qs", "ks", "qc", "kh")}
    hg["tot"] = dram("hg_tot", (2, WID, HG_CHUNKS))
    hg["o"] = dram("hg_o", (2, SEQ, WID))
    s = {
        "mods": dram("mods", (2, N_MOD * D)), "yn": dram("yn", (SEQ, D)),
        "results": dram("results", (TOP_K * SEQ + P, D)), "proj": dram("proj", (P_IN, TOK)), "mix": dram("mix", (D, SEQ)),
        "x1": dram("x1", (SEQ, D)), "h": dram("h", (SEQ, D)), "rw": rw, "hg": hg,
        "proj2": dram("proj2", (D_IN, SEQ)), "mix2": dram("mix2", (MIX2, SEQ)), "att": dram("att", (SEQ, WID)),
        "at": {n: dram("at_" + n, (HEADS, HEAD + 2, SEQ)) for n in ("q", "k")},
        "sd": {"xbc": dram("sd_xbc", (SSD_CONV, SEQ)), "dt": dram("sd_dt", (SSD_HEADS, SEQ)),
               "acs": dram("sd_acs", (SSD_HEADS, SEQ))},
    }
    with ExitStack() as ctx:
        consts = build_constants(nc, ctx)
        first_block(nc, consts, i, s)
        second_block(nc, consts, i, s, out)


_INS = ["x", "c", "ctx", "c_ctx", "w_mod", "b_mod", "norm1_g", "norm2_g", "w_in", "rw_conv", "rw_w0", "rw_w2", "rw_a0",
        "rw_a2", "rw_g2", "rw_k_k", "rw_k_a", "rw_r_k", "rw_lnx_g", "rw_lnx_b", "hg_lb_logits", "hg_norm_g", "w_out",
        "router_w", "router_b", "exp_w_gate", "exp_w_up", "exp_w_down", "sh_w_gate", "sh_w_up", "sh_w_down",
        "final_norm_g", "norm_g_2", "w_in_2", "q_norm_g_2", "k_norm_g_2", "forget_b_2", "ssd_conv_w_2", "ssd_conv_b_2",
        "ssd_dt_bias_2", "ssd_a_log_2", "ssd_d_2", "ssd_norm_g_2", "lru_conv_w_2", "lru_conv_b_2", "lru_w_a_2",
        "lru_b_a_2", "lru_w_x_2", "lru_b_x_2", "lru_lambda_2", "w_out_2"]
_OUTS = [((1, SEQ, D), "float32")]


def kernel(**inputs):
    import numpy as _np
    import concourse.bacc as _bacc
    from concourse import mybir as _mybir
    from concourse.bass_utils import run_bass_kernel_spmd as _run

    nc = _bacc.Bacc("TRN2", target_bir_lowering=False, num_devices=1)
    arrays, args = {}, {}
    for name in _INS:
        a = _np.ascontiguousarray(inputs[name])
        arrays[f"in_{name}_dram"] = a
        args[name] = nc.dram_tensor(f"in_{name}_dram", a.shape, _mybir.dt.from_np(a.dtype), kind="ExternalInput").ap()
    shape, dtype = _OUTS[0]
    out = nc.dram_tensor("out_0_dram", shape, _mybir.dt.from_np(_np.dtype(dtype)), kind="ExternalOutput").ap()
    two_blocks(nc, args, out)
    r = _run(nc, [arrays], core_ids=[0])
    return r.results[0]["out_0_dram"]
```
